# Optimizing a Trainium2 kernel written in Bass

```python
import math
import jax, jax.numpy as jnp
from jax import lax
import numpy as np

D_MODEL = 1024
BATCH = 1
SEQ = 512
DEPTH = 1
DEC_BATCH = 8
DEC_SEQ = 8
PAST_LEN = 4096
PAGE_SIZE = 128

N_META = 16
MLA_HEADS = 8
MLA_NOPE = 64
MLA_ROPE = 32
MLA_V = 64
MLA_KV_LORA = 256
MLA_Q_LORA = 768
MLA_SCALE = (MLA_NOPE + MLA_ROPE) ** -0.5
DSA_HEADS = 8
DSA_HEAD_DIM = 64
DSA_SCALE = DSA_HEAD_DIM ** -0.5
IDX_HEADS = 8
IDX_DIM = 64
TOPK_MAX = 256
D_FF = 2816
CONV_W = 3
ROPE_THETA = 10000.0
EPS = 1e-6
Q_BLOCK = 128
NEG_INF = -1e30
MIX_SIZES = (MLA_Q_LORA, MLA_KV_LORA, MLA_ROPE,
             DSA_HEADS * DSA_HEAD_DIM, DSA_HEADS * DSA_HEAD_DIM, DSA_HEADS * DSA_HEAD_DIM,
             IDX_HEADS * IDX_DIM, IDX_DIM, IDX_HEADS, D_MODEL, D_MODEL)
D_IN = (MLA_Q_LORA + MLA_KV_LORA + MLA_ROPE + 3 * DSA_HEADS * DSA_HEAD_DIM
        + IDX_HEADS * IDX_DIM + IDX_DIM + IDX_HEADS + 2 * D_MODEL)

kernel_name = 'mla_dsa_gated_hybrid_step'

def rms_norm(x, g):
    xf = x.astype(jnp.float32)
    y = xf * lax.rsqrt(jnp.mean(xf * xf, axis=-1, keepdims=True) + EPS)
    return (y * g.astype(jnp.float32)).astype(x.dtype)

def rope(x, pos):
    half = x.shape[-1] // 2
    inv_freq = 1.0 / (ROPE_THETA ** (jnp.arange(half, dtype=jnp.float32) / half))
    ang = pos.astype(jnp.float32)[:, None] * inv_freq[None, :]
    cos = jnp.cos(ang)[:, None, :]
    sin = jnp.sin(ang)[:, None, :]
    xf = x.astype(jnp.float32)
    x1, x2 = xf[..., :half], xf[..., half:]
    return jnp.concatenate([x1 * cos - x2 * sin, x2 * cos + x1 * sin], axis=-1).astype(x.dtype)

def project_mixers(h, pos, lw):
    B, L, _ = h.shape
    z = jnp.einsum('bld,de->ble', h, lw['w_in'])
    cuts = [int(c) for c in np.cumsum(MIX_SIZES)[:-1]]
    c_q, c_kv, k_pe, q_b, k_b, v_b, q_i, k_i, w_i, gate_a, gate_b = jnp.split(z, cuts, axis=-1)
    q = jnp.einsum('blc,chd->blhd', rms_norm(c_q, lw['g_q']), lw['w_uq'])
    q_lat = jnp.einsum('blhn,chn->blhc', q[..., :MLA_NOPE], lw['w_uk'])
    q_pe = rope(q[..., MLA_NOPE:], pos)
    c_kv = rms_norm(c_kv, lw['g_kv'])
    k_pe = rope(k_pe[:, :, None, :], pos)[:, :, 0]
    q_b = rope(q_b.reshape(B, L, DSA_HEADS, DSA_HEAD_DIM), pos)
    k_b = rope(k_b.reshape(B, L, DSA_HEADS, DSA_HEAD_DIM), pos)
    v_b = v_b.reshape(B, L, DSA_HEADS, DSA_HEAD_DIM)
    q_i = rope(q_i.reshape(B, L, IDX_HEADS, IDX_DIM), pos)
    k_i = rope(k_i[:, :, None, :], pos)[:, :, 0]
    w_i = w_i * (IDX_HEADS ** -0.5)
    return (q_lat, q_pe, q_b, q_i, w_i), (c_kv, k_pe, k_b, v_b, k_i), (gate_a, gate_b)

def mla_attend(q_lat, q_pe, q_pos, c_kv, k_pe, w_uv):
    s = jnp.einsum('bqhc,bkc->bhqk', q_lat, c_kv) + jnp.einsum('bqhr,bkr->bhqk', q_pe, k_pe)
    s = s.astype(jnp.float32) * MLA_SCALE
    k_pos = jnp.arange(c_kv.shape[1])
    s = jnp.where(k_pos[None, None, None, :] <= q_pos[None, None, :, None], s, NEG_INF)
    p = jax.nn.softmax(s, axis=-1).astype(c_kv.dtype)
    o_lat = jnp.einsum('bhqk,bkc->bqhc', p, c_kv)
    o = jnp.einsum('bqhc,chv->bqhv', o_lat, w_uv)
    return o.reshape(o.shape[0], o.shape[1], MLA_HEADS * MLA_V)

def indexer_topk(q_i, w_i, q_pos, k_i, topk):
    s = jnp.einsum('bqhd,bkd->bqhk', q_i, k_i).astype(jnp.float32) * (IDX_DIM ** -0.5)
    score = jnp.einsum('bqhk,bqh->bqk', jax.nn.relu(s), w_i.astype(jnp.float32))
    k_pos = jnp.arange(k_i.shape[1])
    score = jnp.where(k_pos[None, None, :] <= q_pos[None, :, None], score, NEG_INF)
    _, idx = lax.top_k(score, topk)
    return idx

def dsa_attend(q, q_pos, k_sel, v_sel, idx):
    s = jnp.einsum('bqhd,bqshd->bhqs', q, k_sel).astype(jnp.float32) * DSA_SCALE
    valid = idx <= q_pos[None, :, None]
    s = jnp.where(valid[:, None], s, NEG_INF)
    p = jax.nn.softmax(s, axis=-1).astype(v_sel.dtype)
    o = jnp.einsum('bhqs,bqshd->bqhd', p, v_sel)
    return o.reshape(o.shape[0], o.shape[1], DSA_HEADS * DSA_HEAD_DIM)

def gather_rows(rows, idx):
    return jax.vmap(lambda rb, ib: rb[ib])(rows, idx)

def gather_selected(pool, page_table, new_rows, idx, past_len):
    B = idx.shape[0]
    in_past = idx < past_len
    ip = jnp.minimum(idx, past_len - 1)
    phys = jnp.take_along_axis(page_table, (ip // PAGE_SIZE).reshape(B, -1), axis=1).reshape(idx.shape)
    from_pool = pool[phys, ip % PAGE_SIZE]
    inew = jnp.clip(idx - past_len, 0, new_rows.shape[1] - 1)
    from_new = gather_rows(new_rows, inew)
    return jnp.where(in_past[..., None, None], from_pool, from_new)

def merge_branches(x, mla_o, dsa_o, gate_a, gate_b, lw):
    o = (jax.nn.sigmoid(gate_a) * jnp.einsum('blv,vd->bld', mla_o, lw['w_br_a'])
         + jax.nn.sigmoid(gate_b) * jnp.einsum('blv,vd->bld', dsa_o, lw['w_br_b']))
    return x + jnp.einsum('bld,de->ble', o, lw['w_o'])

def conv_ffn(h, conv_state, lw):
    L = h.shape[1]
    g = jnp.einsum('bld,df->blf', h, lw['w_ffn_g'])
    u = jnp.einsum('bld,df->blf', h, lw['w_ffn_u'])
    gp = jnp.concatenate([conv_state.astype(g.dtype), g], axis=1)
    gc = lw['ffn_conv_b'] + lw['ffn_conv_w'][0] * gp[:, 0:L]
    for j in range(1, CONV_W):
        gc = gc + lw['ffn_conv_w'][j] * gp[:, j:j + L]
    out = jnp.einsum('blf,fd->bld', jax.nn.silu(gc) * u, lw['w_ffn_d'])
    return out, gp[:, L:]

def prompt_layer(x, lw):
    B, L, _ = x.shape
    pos = jnp.arange(L)
    h = rms_norm(x, lw['norm1_g'])
    (q_lat, q_pe, q_b, q_i, w_i), (c_kv, k_pe, k_b, v_b, k_i), (gate_a, gate_b) = project_mixers(h, pos, lw)
    topk = min(TOPK_MAX, L // 4)
    nb = -(-L // Q_BLOCK)
    lpad = nb * Q_BLOCK

    def to_blocks(a):
        a = jnp.pad(a, [(0, 0), (0, lpad - L)] + [(0, 0)] * (a.ndim - 2))
        return jnp.moveaxis(a.reshape((B, nb, Q_BLOCK) + a.shape[2:]), 1, 0)

    def from_blocks(a):
        return jnp.moveaxis(a, 0, 1).reshape(B, lpad, a.shape[-1])[:, :L]

    def block(args):
        ql, qp, qb, qi, wi, qpos = args
        mla_o = mla_attend(ql, qp, qpos, c_kv, k_pe, lw['w_uv'])
        idx = indexer_topk(qi, wi, qpos, k_i, topk)
        dsa_o = dsa_attend(qb, qpos, gather_rows(k_b, idx), gather_rows(v_b, idx), idx)
        return mla_o, dsa_o

    q_pos_blocks = jnp.arange(lpad).reshape(nb, Q_BLOCK)
    mla_o, dsa_o = lax.map(block, (to_blocks(q_lat), to_blocks(q_pe), to_blocks(q_b),
                                   to_blocks(q_i), to_blocks(w_i), q_pos_blocks))
    x = merge_branches(x, from_blocks(mla_o), from_blocks(dsa_o), gate_a, gate_b, lw)
    zero_state = jnp.zeros((B, CONV_W - 1, D_FF), x.dtype)
    f, conv_new = conv_ffn(rms_norm(x, lw['norm2_g']), zero_state, lw)
    x = x + f
    return x, (c_kv, k_pe, k_b, v_b, k_i, conv_new)

def sample_layer(x, pool_ckv, pool_kpe, pool_k, pool_v, pool_ik, conv_state, page_table, lw):
    B, T, _ = x.shape
    past_len = page_table.shape[1] * PAGE_SIZE
    pos = past_len + jnp.arange(T)
    h = rms_norm(x, lw['norm1_g'])
    (q_lat, q_pe, q_b, q_i, w_i), (c_kv, k_pe, k_b, v_b, k_i), (gate_a, gate_b) = project_mixers(h, pos, lw)

    def paged_rows(pool):
        g = pool[page_table]
        return g.reshape((B, past_len) + pool.shape[2:])

    ckv_all = jnp.concatenate([paged_rows(pool_ckv).astype(c_kv.dtype), c_kv], axis=1)
    kpe_all = jnp.concatenate([paged_rows(pool_kpe).astype(k_pe.dtype), k_pe], axis=1)
    ik_all = jnp.concatenate([paged_rows(pool_ik).astype(k_i.dtype), k_i], axis=1)
    mla_o = mla_attend(q_lat, q_pe, pos, ckv_all, kpe_all, lw['w_uv'])
    topk = min(TOPK_MAX, (past_len + T) // 4)
    idx = indexer_topk(q_i, w_i, pos, ik_all, topk)
    k_sel = gather_selected(pool_k.astype(k_b.dtype), page_table, k_b, idx, past_len)
    v_sel = gather_selected(pool_v.astype(v_b.dtype), page_table, v_b, idx, past_len)
    dsa_o = dsa_attend(q_b, pos, k_sel, v_sel, idx)
    x = merge_branches(x, mla_o, dsa_o, gate_a, gate_b, lw)
    f, conv_new = conv_ffn(rms_norm(x, lw['norm2_g']), conv_state, lw)
    x = x + f
    return x, (c_kv, k_pe, k_b, v_b, k_i, conv_new)

def setup_inputs(seed: int = 0) -> dict:
    key = jax.random.key(seed)
    ks = jax.random.split(key, 32)
    n_pages = PAST_LEN // PAGE_SIZE
    n_used = DEC_BATCH * n_pages
    n_pool = n_used + n_used // 4
    nrm = jax.random.normal
    f32 = jnp.float32
    page_table = jax.random.permutation(ks[0], n_pool)[:n_used].reshape(DEC_BATCH, n_pages).astype(jnp.int32)
    return {
        'x_prompt': nrm(ks[1], (BATCH, SEQ, D_MODEL), f32),
        'x_sample': nrm(ks[2], (DEC_BATCH, DEC_SEQ, D_MODEL), f32),
        'cache_mla_ckv': nrm(ks[3], (DEPTH, n_pool, PAGE_SIZE, MLA_KV_LORA), f32),
        'cache_mla_kpe': nrm(ks[4], (DEPTH, n_pool, PAGE_SIZE, MLA_ROPE), f32),
        'cache_dsa_k': nrm(ks[5], (DEPTH, n_pool, PAGE_SIZE, DSA_HEADS, DSA_HEAD_DIM), f32),
        'cache_dsa_v': nrm(ks[6], (DEPTH, n_pool, PAGE_SIZE, DSA_HEADS, DSA_HEAD_DIM), f32),
        'cache_idx_k': nrm(ks[7], (DEPTH, n_pool, PAGE_SIZE, IDX_DIM), f32),
        'state_ffn_conv': nrm(ks[8], (DEPTH, DEC_BATCH, CONV_W - 1, D_FF), f32),
        'page_table': page_table,
        'meta_tokens': nrm(ks[9], (N_META, D_MODEL), f32),
        'norm1_g': 1.0 + 0.02 * nrm(ks[10], (DEPTH, D_MODEL), f32),
        'w_in': nrm(ks[11], (DEPTH, D_MODEL, D_IN), f32) * D_MODEL ** -0.5,
        'g_q': 1.0 + 0.02 * nrm(ks[12], (DEPTH, MLA_Q_LORA), f32),
        'g_kv': 1.0 + 0.02 * nrm(ks[13], (DEPTH, MLA_KV_LORA), f32),
        'w_uq': nrm(ks[14], (DEPTH, MLA_Q_LORA, MLA_HEADS, MLA_NOPE + MLA_ROPE), f32) * MLA_Q_LORA ** -0.5,
        'w_uk': nrm(ks[15], (DEPTH, MLA_KV_LORA, MLA_HEADS, MLA_NOPE), f32) * MLA_KV_LORA ** -0.5,
        'w_uv': nrm(ks[16], (DEPTH, MLA_KV_LORA, MLA_HEADS, MLA_V), f32) * MLA_KV_LORA ** -0.5,
        'w_br_a': nrm(ks[17], (DEPTH, MLA_HEADS * MLA_V, D_MODEL), f32) * (MLA_HEADS * MLA_V) ** -0.5,
        'w_br_b': nrm(ks[18], (DEPTH, DSA_HEADS * DSA_HEAD_DIM, D_MODEL), f32) * (DSA_HEADS * DSA_HEAD_DIM) ** -0.5,
        'w_o': nrm(ks[19], (DEPTH, D_MODEL, D_MODEL), f32) * D_MODEL ** -0.5,
        'norm2_g': 1.0 + 0.02 * nrm(ks[20], (DEPTH, D_MODEL), f32),
        'w_ffn_g': nrm(ks[21], (DEPTH, D_MODEL, D_FF), f32) * D_MODEL ** -0.5,
        'w_ffn_u': nrm(ks[22], (DEPTH, D_MODEL, D_FF), f32) * D_MODEL ** -0.5,
        'ffn_conv_w': nrm(ks[23], (DEPTH, CONV_W, D_FF), f32) * CONV_W ** -0.5,
        'ffn_conv_b': 0.02 * nrm(ks[24], (DEPTH, D_FF), f32),
        'w_ffn_d': nrm(ks[25], (DEPTH, D_FF, D_MODEL), f32) * D_FF ** -0.5,
        'final_g': 1.0 + 0.02 * nrm(ks[26], (D_MODEL,), f32),
    }

def reference(x_prompt, x_sample, cache_mla_ckv, cache_mla_kpe, cache_dsa_k, cache_dsa_v, cache_idx_k,
              state_ffn_conv, page_table, meta_tokens, norm1_g, w_in, g_q, g_kv, w_uq, w_uk, w_uv,
              w_br_a, w_br_b, w_o, norm2_g, w_ffn_g, w_ffn_u, ffn_conv_w, ffn_conv_b, w_ffn_d, final_g):
    B = x_prompt.shape[0]
    meta = jnp.broadcast_to(meta_tokens[None].astype(x_prompt.dtype), (B, N_META, x_prompt.shape[-1]))
    xp = jnp.concatenate([meta, x_prompt], axis=1)
    xs = x_sample
    new_p = []
    new_s = []
    for l in range(DEPTH):
        lw = {'norm1_g': norm1_g[l], 'w_in': w_in[l], 'g_q': g_q[l], 'g_kv': g_kv[l], 'w_uq': w_uq[l],
              'w_uk': w_uk[l], 'w_uv': w_uv[l], 'w_br_a': w_br_a[l], 'w_br_b': w_br_b[l], 'w_o': w_o[l],
              'norm2_g': norm2_g[l], 'w_ffn_g': w_ffn_g[l], 'w_ffn_u': w_ffn_u[l],
              'ffn_conv_w': ffn_conv_w[l], 'ffn_conv_b': ffn_conv_b[l], 'w_ffn_d': w_ffn_d[l]}
        xp, rows_p = prompt_layer(xp, lw)
        xs, rows_s = sample_layer(xs, cache_mla_ckv[l], cache_mla_kpe[l], cache_dsa_k[l], cache_dsa_v[l],
                                  cache_idx_k[l], state_ffn_conv[l], page_table, lw)
        new_p.append(rows_p)
        new_s.append(rows_s)
    y_prompt = rms_norm(xp, final_g)[:, N_META:]
    y_sample = rms_norm(xs, final_g)
    new_ckv_p = jnp.stack([r[0] for r in new_p], axis=0)
    new_kpe_p = jnp.stack([r[1] for r in new_p], axis=0)
    new_k_p = jnp.stack([r[2] for r in new_p], axis=0)
    new_v_p = jnp.stack([r[3] for r in new_p], axis=0)
    new_ik_p = jnp.stack([r[4] for r in new_p], axis=0)
    new_conv_p = jnp.stack([r[5] for r in new_p], axis=0)
    new_ckv_s = jnp.stack([r[0] for r in new_s], axis=0)
    new_kpe_s = jnp.stack([r[1] for r in new_s], axis=0)
    new_k_s = jnp.stack([r[2] for r in new_s], axis=0)
    new_v_s = jnp.stack([r[3] for r in new_s], axis=0)
    new_ik_s = jnp.stack([r[4] for r in new_s], axis=0)
    new_conv_s = jnp.stack([r[5] for r in new_s], axis=0)
    return (y_prompt, y_sample, new_ckv_p, new_kpe_p, new_k_p, new_v_p, new_ik_p, new_conv_p,
            new_ckv_s, new_kpe_s, new_k_s, new_v_s, new_ik_s, new_conv_s)


_drawn_inputs = setup_inputs


def setup_inputs(seed=0):
    import zlib

    import numpy as np

    out = dict(_drawn_inputs(seed))
    spreads = {}
    factors = {'cache_mla_ckv': 3.596,
     'cache_mla_kpe': 6.594,
     'norm1_g': 2.888,
     'g_q': 8.0,
     'g_kv': 2.684,
     'norm2_g': 2.9,
     'ffn_conv_b': 5.522,
     'final_g': 2.787}
    for name, (base, spread) in spreads.items():
        noise = np.random.default_rng([zlib.crc32(name.encode()), seed]).standard_normal(out[name].shape)
        drawn = base * np.exp(spread * noise) if base else spread * noise
        out[name] = __import__('jax').numpy.asarray(drawn.astype(out[name].dtype))
    for name, factor in factors.items():
        out[name] = (out[name] * factor).astype(out[name].dtype)
    return out
```

```python
from contextlib import ExitStack

import numpy as np
import concourse.bass as bass
import concourse.mybir as mybir

F32 = mybir.dt.float32
I32 = mybir.dt.int32
U32 = mybir.dt.uint32
ACT = mybir.ActivationFunctionType
ALU = mybir.AluOpType
AX = mybir.AxisListType

D = 1024
KD = D // 128
NP = 528
NM = 16
NB = 8
NT = 8
NS = NB * NT
H = 8
PAST = 4096
PAGE = 128
NPG = PAST // PAGE
QL, KVL, PE_, HD = 768, 256, 32, 64
FF = 2816
NF = FF // 128
EPS = 1e-6
NEG = -1e30
TAKEN = -3e38
DUMMY = 3e38
MLA_SCALE = 96.0 ** -0.5
DSA_SCALE = 64.0 ** -0.5
TOPK_P = 132
TOPK_S = 256
NTILE = 5
TW = [128, 128, 128, 128, 80]
NCOL = 592
LAST = 576
C_CQ, C_CKV, C_KPE, C_QB, C_KB, C_VB, C_QI, C_KI, C_WI, C_GA, C_GB = (
    0, 768, 1024, 1056, 1568, 2080, 2592, 3104, 3168, 3176, 4200)


SHARED = {name: sem for sem, names in {
    "turned": "h_turned sturned pturned mix_turned h2_turned conv_w_turned state_turned conv_turned dots_turned "
              "sel_turned rows_turned",
    "product": "keysT_used piece_used index_dots latent_dots scored_p mixed_dots out_dots up_done y_dots new_dots",
    "turn_out": "turned_act sturn_out pturn_out mix_turn_out sel_out state_out conv_turned_out conv_w_out "
                "row_no_ready o_s_out",
    "squared": "x_squared c_squared x2_squared y_squared",
    "root": "x_root c_root x2_root y_root",
    "exped": "exped_p sel_exped",
    "mean": "x_mean c_mean x2_mean y_mean",
    "h_ready": "h2_ready",
    "neg_max": "neg_max_p",
    "chain_dve": "picks_done",
    "x_scaled": "x_normed",
}.items() for name in names.split()}


class Signals:

    def __init__(self, nc, ctx, values):
        self.nc, self.ctx, self.values = nc, ctx, values
        self.sems, self.count, self.now = {}, {}, {}
        self.last = Last()

    def sem(self, signal):
        name = SHARED.get(signal, signal)
        if name not in self.sems:
            self.sems[name] = self.ctx.enter_context(self.nc.semaphore(name))
        return self.sems[name]

    def tick(self, signal, *key, by=1):
        name = SHARED.get(signal, signal)
        self.count[name] = self.count.get(name, 0) + by
        assert (signal, *key) not in self.now or not key, (signal, key)
        self.now[(signal, *key)] = self.count[name]
        self.last.sem, self.last.value = self.sem(signal), self.count[name]
        return by

    def upto(self, signal, *key):
        return 1 if self.values is None else self.values[(signal, *key)]

    def same(self, key, event):
        assert SHARED.get(key[0], key[0]) == SHARED.get(event[0], event[0])
        self.now[key] = self.now[event]


class Last:
    pass


class Region:

    def __init__(self, mem, start, end):
        self.mem, self.at, self.end = mem, start, end

    def take(self, *shape, dtype=F32):
        n = int(np.prod(shape))
        assert self.at + n <= self.end, ("SBUF", shape, self.at + n - self.end)
        v = self.mem[:, self.at:self.at + n]
        self.at += n
        if dtype is not F32:
            v = v.bitcast(dtype)
        if len(shape) == 2:
            v = v.rearrange("p (a b) -> p a b", a=shape[0])
        elif len(shape) == 3:
            v = v.rearrange("p (a b c) -> p a b c", a=shape[0], b=shape[1])
        elif len(shape) == 4:
            v = v.rearrange("p (a b c d) -> p a b c d", a=shape[0], b=shape[1], c=shape[2])
        return v


def token_cols(m):
    return slice(128 * m, 128 * m + TW[m])


def trunk(nc, I, O, scratch, events):
    ctx = ExitStack()
    with ctx:
        S = Signals(nc, ctx, events)
        sem, tick, upto, same, last = S.sem, S.tick, S.upto, S.same, S.last
        mem = ctx.enter_context(nc.sbuf_tensor("mem", [128, 53200], F32))
        PS = ctx.enter_context(nc.psum_tensor("PS", [128, 8, 512], F32))

        K = Region(mem, 0, 30500)
        ident = K.take(128)
        cc64, ss64 = K.take(5, 64), K.take(5, 64)
        cc32, ss32 = K.take(5, 32), K.take(5, 32)
        same_t = K.take(8)
        quarter = K.take(1)
        g1c = K.take(KD)
        gqc = K.take(6)
        g2c = K.take(KD)
        w_i = K.take(5, 8)
        wcol = K.take(NB)
        ptx = K.take(NB, dtype=I32)
        idx_row = K.take(NB, dtype=U32)
        idx_ckv = K.take(NB, 4, dtype=U32)
        small = K.take(64)
        wuv = K.take(2, 512)
        heads_at = K.at
        qT, kT, vm = K.take(H, NCOL), K.take(H, NP), K.take(5, 512)
        qb_at = K.at
        qbT, kbT, vb, qiT, kiT = K.take(4, NCOL), K.take(4, NCOL), K.take(5, 512), K.take(4, NCOL), K.take(NCOL)
        ql_s, qpe_s, qi_s = K.take(2, 512), K.take(512), K.take(512)
        ckv_new = K.take(2, NS)
        kpe_new = K.take(NS)
        oT_s = K.take(4, NS)
        picked = K.take(TOPK_S, dtype=U32)
        causal8 = K.take(8)
        A = Region(mem, K.at, 53200)
        hT = A.take(KD, NCOL)
        ckvT = A.take(2, NCOL)
        w_ring = A.take(2, 4608)
        cq = A.take(2, QL)
        lat = A.take(5, 288)
        q_tok = A.take(2, QL)
        kid = A.take(5, 128)
        tok = A.take(3, 512)
        ta, tb = A.take(512), A.take(512)
        gkv = A.take(KVL)
        wuk = A.take(2, 512)
        C = Region(mem, K.at, 53200)
        raw = C.take(5, 2048)
        kpe_raw = C.take(1024)
        row_scores = C.take(PAST + NT)
        pick_scores = C.take(PAST + NT)
        keysT = C.take(4, 512)
        kpeT = C.take(8, 128)
        probsT = C.take(33, 64)
        lat_new = C.take(KVL)
        qpe_z = C.take(4, 64)
        o_lat = C.take(2, 512)
        wb = C.take(NB, 8)
        top8 = C.take(8)
        chunk_max = C.take(16)
        col = C.take(4)
        diag = C.take(64)
        relu_i = probsT.rearrange("p a b -> p (a b)")[:, 0:2048].rearrange("p (a b) -> p a b", a=4)

        P = Region(mem, K.at, 53200)
        oT_a, oT_b = P.take(4, NCOL), P.take(4, NCOL)
        wide_tri = P.take(640)
        score_acc = P.take(4 + NP)
        mask_s = P.take(NP)
        probs = P.take(3, NP)
        probs_T = P.take(2, 640)
        relu_p = P.take(2, NP)
        o_tok = P.take(2, 512)
        vb_last = P.take(512)
        wi_last = P.take(8)
        stat = P.take(3, 4)
        top8_p = P.take(8)
        rows = P.take(5, 1024)
        q_wide = P.take(2, 512)
        prod = P.take(1024)
        dots_k = P.take(16, 64)
        s_sel = P.take(H, TOPK_S + NS)
        p_sel = P.take(2, 64, 8)
        p_new = P.take(8, 64)
        page = P.take(TOPK_S, dtype=U32)
        offset = P.take(TOPK_S, dtype=U32)
        phys = P.take(TOPK_S)
        hit = P.take(TOPK_S)
        slot_bias = P.take(TOPK_S)
        row_no = P.take(2, 64, dtype=U32)
        pages_q = P.take(NPG, dtype=I32)
        pages_f = P.take(NPG)
        new_hit = P.take(8)
        new_bias = P.take(8, 8)
        same_b = P.take(8)
        head_max, head_sum = P.take(8), P.take(8)

        F1 = Region(mem, heads_at, K.at)
        F2 = Region(mem, K.at + 2 * 4 * NCOL, 53200)
        w_slots = F1.take(6, 2048)
        o_mix = F1.take(5, D)
        h2T = flat(o_mix)[:, 0:KD * NCOL].rearrange("p (a b) -> p a b", a=KD)
        hT_f = F1.take(KD, NCOL)
        x2 = F2.take(5, D)
        up_at = F2.at
        upT = F2.take(NF, NCOL)
        conv_state = F2.take(FF)
        F3 = Region(mem, up_at, up_at + NF * NCOL)
        w_b1 = F3.take(2, 4096)
        o_mixT = F3.take(KD, NCOL)
        gates = mem[:, F2.at - FF:F2.at - FF + 2048].rearrange("p (a b c) -> p a b c", a=2, b=2)
        F4 = Region(mem, heads_at + 6 * 2048 + 5 * D, heads_at + 6 * 2048 + 5 * D + KD * NCOL)
        conv_in, conv_sum, conv_sig = F4.take(2, 610), F4.take(2, NCOL), F4.take(2, NCOL)
        g_row = F4.take(D)
        x_norm = mem[:, F4.at - D - 2 * 1184 - 1220:F4.at - D - 2 * 1184 - 1220 + 2048].rearrange("p (a b) -> p a b", a=2)
        conv_out = mem[:, K.at:K.at + FF]
        conv_w = mem[:, K.at + FF:K.at + FF + 88]
        conv_rows = mem[:, K.at + FF + 96:K.at + FF + 96 + 128]
        last_two = mem[:, K.at + FF + 256:K.at + FF + 256 + 36].rearrange("p (a b) -> p a b", a=2)

        x_ring = flat(qT)[:, 0:2048].rearrange("p (a b) -> p a b", a=2)
        cqT = mem[:, qb_at:qb_at + 6 * NCOL].rearrange("p (a b) -> p a b", a=6)
        junk = flat(vm)[:, 0:1024]
        dup = flat(vm)[:, 1024:2048].rearrange("p (a b) -> p a b", a=8)
        wukT = flat(vb)[:, 0:2048].rearrange("p (a b) -> p a b", a=8)

        units = [(k, m) for k in ("qi", "sm", "cq", "uq") for m in range(NTILE)]
        units += [("wt", 0)] + [("kn", h) for h in range(H)] + [("kl", 0), ("ql", 0), ("ql", 1)]
        units += [(k, m) for k in ("vm", "qb", "kb", "vb") for m in range(NTILE)]
        chunk_at = {"qi": (C_QI, 512), "qb": (C_QB, 512), "kb": (C_KB, 512), "vb": (C_VB, 512)}
        slot_of = {"qi": 0, "sm": 1, "c0": 0, "c1": 1, "uq": 0, "qb": 1, "kb": 0, "vb": 1}
        banks, before = {}, {}
        user, n = [None] * 4, 0
        for u in units:
            banks[u], before[u] = [], []
            for _ in range({"cq": 2, "uq": 2, "wt": 0}.get(u[0], 1)):
                banks[u].append(n % 4)
                before[u].append(user[n % 4])
                user[n % 4] = u
                n += 1

        def turns_of(u):
            kind, m = u
            if kind not in ("qi", "cq", "uq", "wt", "qb", "kb"):
                return []
            r = slice(0, TW[m])
            if kind in ("qi", "qb", "kb"):
                t = tok[:, units_tok[u]]
                out = [((kind, m, 0), [(t[r, 128 * i:128 * i + 128]) for i in range(4)])]
                if u == ("qi", 4):
                    out += [((kind, m, 1 + j), [dup[0:NS, 4 * j + i, :] for i in range(4)]) for j in range(2)]
                return out
            if kind == "cq":
                c = cq[:, m % 2]
                l4 = [lat[r, m, 0:128], lat[r, m, 128:256], lat[r, m, 192:288], kid[r, m, :]]
                out = [((kind, m, 0), [c[r, 128 * i:128 * i + 128] for i in range(4)]),
                       ((kind, m, 1), [c[r, 128 * i:128 * i + 128] for i in range(4, 6)]),
                       ((kind, m, 2), l4)]
                if m == 4:
                    out.append(((kind, m, 3), [lat[0:NS, m, 256:288]]))
                return out
            if kind == "uq":
                q = q_tok[:, m % 2].rearrange("p (h n) -> p h n", h=H)
                out = [((kind, m, j), [q[r, 4 * j + i, :] for i in range(4)]) for j in range(2)]
                if m == 4:
                    out += [((kind, m, 2 + j), [dup[0:NS, 4 * j + i, :] for i in range(4)]) for j in range(2)]
                return out
            return [((kind, m, j), [wuk[:, c, 64 * h:64 * h + 64] for h in (2 * j, 2 * j + 1) for c in range(2)])
                    for j in range(4)]

        units_tok = {u: i % 3 for i, u in enumerate([u for u in units if u[0] in ("qi", "qb", "kb")])}
        tok_before = {}
        for i, u in enumerate([u for u in units if u[0] in ("qi", "qb", "kb")]):
            tok_before[u] = [v for v in units_tok if units_tok[v] == i % 3][i // 3 - 1] if i >= 3 else None
        turns = [(("h", m, j), None) for m in range(NTILE) for j in range(2)]
        for u in units:
            turns += turns_of(u)
        turn_bank = {key: 4 + i % 4 for i, (key, _) in enumerate(turns)}
        turn_before = {key: turns[i - 4][0] if i >= 4 else None for i, (key, _) in enumerate(turns)}

        def load_x(sp, m):
            dst = x_ring[:, m % 2, :]
            if m == 0:
                sp.dma_start(dst[0:NM], I["meta_tokens"]).then_inc(sem(f"x_in{m}"), tick(f"x_in{m}", by=16))
                sp.dma_start(dst[NM:128], I["x_prompt"][0, 0:128 - NM, :]).then_inc(
                    sem(f"x_in{m}"), tick(f"x_in{m}", m, by=16))
            elif m < 4:
                sp.dma_start(dst, I["x_prompt"][0, 128 * m - NM:128 * m + 128 - NM, :]).then_inc(
                    sem(f"x_in{m}"), tick(f"x_in{m}", m, by=16))
            else:
                sp.dma_start(dst[0:NS], I["x_sample"].rearrange("b t d -> (b t) d")).then_inc(
                    sem(f"x_in{m}"), tick(f"x_in{m}", by=16))
                sp.dma_start(dst[NS:NS + 16], I["x_prompt"][0, 512 - NM:528 - NM, :]).then_inc(
                    sem(f"x_in{m}"), tick(f"x_in{m}", m, by=16))

        def w_view(name):
            flat_slot = w_ring[:, slot_of[name], :]
            if name == "uq":
                return flat_slot.rearrange("p (k n) -> p k n", k=6)
            if name == "sm":
                return flat_slot[:, 0:KD * 104].rearrange("p (k n) -> p k n", k=KD)
            return flat_slot[:, 0:KD * 512].rearrange("p (k n) -> p k n", k=KD)

        def load_w(sp, name):
            w = I["w_in"][0].rearrange("(k p) n -> p k n", p=128)
            dst = w_view(name)
            if name == "uq":
                sp.dma_start(dst, I["w_uq"][0].rearrange("(k p) h n -> p k (h n)", p=128)).then_inc(
                    sem("w_uq_in"), tick("w_uq_in", name, by=16))
            elif name == "sm":
                sp.dma_start(dst[:, :, 0:32], w[:, :, C_KPE:C_KPE + 32]).then_inc(
                    sem("w_sm_in"), tick("w_sm_in", by=16))
                sp.dma_start(dst[:, :, 32:104], w[:, :, C_KI:C_KI + 72]).then_inc(
                    sem("w_sm_in"), tick("w_sm_in", name, by=16))
            else:
                at = {"c0": 0, "c1": 512}.get(name)
                at = chunk_at[name][0] if at is None else at
                sp.dma_start(dst, w[:, :, at:at + 512]).then_inc(sem(f"w_{name}_in"), tick(f"w_{name}_in", name, by=16))

        def store_rows(gp, src, to_p, to_s, m, name):
            tp = rows2(to_p[0, 0])
            if m < 4:
                gp.dma_start(tp[128 * m:128 * m + 128, :], src).then_inc(
                    sem(f"stored_{name}_p" + (str(m) if name == "kb" else "")),
                    tick(f"stored_{name}_p" + (str(m) if name == "kb" else ""), m, by=16))
            else:
                gp.dma_start(tp[512:528, :], src[NS:NS + 16]).then_inc(
                    sem(f"stored_{name}_p" + (str(m) if name == "kb" else "")),
                    tick(f"stored_{name}_p" + (str(m) if name == "kb" else ""), m, by=16))
                gp.dma_start(rows3(to_s[0]), src[0:NS]).then_inc(sem(f"stored_{name}_s"), tick(f"stored_{name}_s", m, by=16))

        def act_unit(act, u):
            kind, m = u
            if kind in ("qi", "uq", "qb", "kb", "wt"):
                return
            b = banks[u]
            act.wait_ge(sem("product"), upto("product", *u))
            if kind == "sm":
                r = slice(0, TW[m])
                ins = act.activation(w_i[r, m, :], PS[r, b[0], 96:104], ACT.Copy, scale=8.0 ** -0.5)
                ins.then_inc(sem("wi_scaled"), tick("wi_scaled", m))
            elif kind == "cq":
                r = slice(0, TW[m])
                act.activation(junk[r, 0:512], PS[r, b[0], :], ACT.Square, accum_out=small[r, 16 + m:17 + m])
                act.activation(junk[r, 512:768], PS[r, b[1], 0:256], ACT.Square, accum_out=small[r, 24 + m:25 + m])
                act.activation(junk[r, 768:1024], PS[r, b[1], 256:512], ACT.Square,
                                      accum_out=small[r, 32 + 2 * m:33 + 2 * m]).then_inc(
                    sem("c_squared"), tick("c_squared", m))
                act.wait_ge(sem("c_mean"), upto("c_mean", m))
                act.activation(small[r, 32 + 2 * m:34 + 2 * m], small[r, 32 + 2 * m:34 + 2 * m], ACT.Sqrt).then_inc(
                    sem("c_root"), tick("c_root", m))
            elif kind == "kn":
                act.copy(kT[0:64, m, 0:512], PS[0:64, b[0], :]).then_inc(sem("unit_act"), tick("unit_act", *u))
            elif kind == "kl":
                act.copy(kT[0:64, :, 512:528], PS[0:64, b[0], 0:128].rearrange("p (h n) -> p h n", h=H)).then_inc(
                    sem("unit_act"), tick("unit_act", *u))
            elif kind == "ql":
                act.copy(ql_s[:, m, :].rearrange("p (b h t) -> p h b t", b=NB, h=H),
                                PS[:, b[0], :].rearrange("p (h b t) -> p h b t", h=H, b=NB)).then_inc(
                    sem("unit_act"), tick("unit_act", *u))
            elif kind == "vm":
                r = slice(0, 128 if m < 4 else 16)
                act.copy(vm[r, m, :], PS[r, b[0], :]).then_inc(sem("unit_act"), tick("unit_act", *u))
            elif kind == "vb":
                r = slice(0, TW[m])
                act.copy(vb[r, m, :], PS[r, b[0], :]).then_inc(sem("unit_act"), tick("unit_act", *u))

        def act_turn(act, key):
            kind, m, j = key
            n = TW[m]
            src = PS[:, turn_bank[key], :].rearrange("p (a n) -> p a n", a=4)
            cols = token_cols(m)
            bht = lambda v: v.rearrange("p (b h t) -> p h b t", b=NB, h=H)[:, 4 * jj:4 * jj + 4]
            from_hbt = lambda v: v.rearrange("p a (b t) -> p a b t", b=NB)
            act.wait_ge(sem("turned"), upto("turned", *key))
            if kind in ("qi", "qb", "kb") and j == 0:
                dst = {"qi": qiT, "qb": qbT, "kb": kbT}[kind]
                ins = act.copy(dst[:, :, cols], src[:, :, 0:n])
            elif kind == "qi":
                jj = j - 1
                ins = act.copy(bht(qi_s), from_hbt(src[:, :, 0:NS]))
            elif kind == "cq" and j < 2:
                for i in range(4 if j == 0 else 2):
                    k = 4 * j + i
                    ins = act.activation(cqT[:, k, cols], src[:, i, 0:n], ACT.Copy, scale=gqc[:, k:k + 1])
            elif kind == "cq" and j == 2:
                act.copy(ckvT[:, :, cols], src[:, 0:2, 0:n])
                act.copy(kiT[:, cols], src[:, 3, 0:n])
                if m == 4:
                    act.copy(ckv_new, src[:, 0:2, 0:NS])
                a, b, c = (0, 128, 128 * m) if m < 4 else (NS, NS + 16, 512)
                ins = act.copy(kT[64:96, :, c:c + b - a], src[64:96, 2, a:b].unsqueeze(1).to_broadcast([32, H, b - a]))
            elif kind == "cq":
                ins = act.copy(kpe_new[0:32, :], src[0:32, 0, 0:NS])
            elif kind == "uq" and j < 2:
                ins = act.copy(qT[0:96, 4 * j:4 * j + 4, cols], src[0:96, :, 0:n])
            elif kind == "uq":
                jj = j - 2
                ins = act.copy(bht(qpe_s), from_hbt(src[:, :, 0:NS]))
            elif kind == "wt":
                ins = act.copy(wukT[0:64, 2 * j:2 * j + 2, :].rearrange("p h (c n) -> p (h c) n", c=2), src[0:64, :, :])
            ins.then_inc(sem("turned_act"), tick("turned_act", *key))

        def rope(dve, link, dst, src, cos, sin, half):
            n, h, w = src.shape
            a = ta[0:n, 0:h * w].rearrange("p (h w) -> p h w", h=h)
            b = tb[0:n, 0:h * w].rearrange("p (h w) -> p h w", h=h)
            wide = lambda t: t.unsqueeze(1).to_broadcast([n, h, t.shape[1]])
            dve.wait_ge(last.sem, last.value)
            dve.tensor_tensor(a, src, wide(cos[0:n]), ALU.mult)
            dve.tensor_tensor(b[:, :, 0:half], src[:, :, half:w], wide(sin[0:n, 0:half]), ALU.mult)
            link(dve.tensor_tensor(b[:, :, half:w], src[:, :, 0:half], wide(sin[0:n, half:w]), ALU.mult))
            return dve.tensor_tensor(dst, a, b, ALU.add)

        def dve_unit(dve, link, u):
            kind, m = u
            if kind in ("kn", "kl", "ql", "vm", "vb", "wt"):
                return
            r, n = slice(0, TW[m]), TW[m]
            b = banks[u]
            heads = lambda v: v.rearrange("p (h n) -> p h n", h=H)
            dve.wait_ge(sem("product"), upto("product", *u))
            if kind in ("qi", "qb", "kb"):
                t = tok[:, units_tok[u]]
                if tok_before[u]:
                    dve.wait_ge(sem("turned"), upto("turned", *tok_before[u], 0))
                    if tok_before[u] == ("qb", 4):
                        dve.wait_ge(sem("q_b_stored"), upto("q_b_stored", 0))
                    if tok_before[u][0] == "kb":
                        dve.wait_ge(sem(f"stored_kb_p{tok_before[u][1]}"), upto(f"stored_kb_p{tok_before[u][1]}", tok_before[u][1]))
                rope(dve, link, heads(t[r]), heads(PS[r, b[0], :]), cc64[:, m], ss64[:, m], 32).then_inc(
                    sem("b_roped"), tick("b_roped", *u))
                if u == ("qi", 4):
                    dve.wait_ge(sem("b_roped"), upto("b_roped", *u))
                    q = heads(t[0:NS]).unsqueeze(2).to_broadcast([NS, H, 2, 64])
                    dve.tensor_copy(dup[0:NS].rearrange("p h (a n) -> p h a n", a=2), q).then_inc(
                        sem("dup_ready"), tick("dup_ready", "qi"))
            elif kind == "sm":
                one = lambda v: v.unsqueeze(1)
                dve.wait_ge(sem("wi_scaled"), upto("wi_scaled", m))
                link(rope(dve, link, one(kid[r, m, 0:64]), one(PS[r, b[0], 32:96]), cc64[:, m], ss64[:, m], 32))
                dve.tensor_copy(kid[r, m, 64:128], kid[r, m, 0:64]).then_inc(
                    sem("ki_roped"), tick("ki_roped", m))
                rope(dve, link, one(lat[r, m, 256:288]), one(PS[r, b[0], 0:32]), cc32[:, m], ss32[:, m], 16).then_inc(
                    sem("unit_dve"), tick("unit_dve", *u))
            elif kind == "cq":
                dve.wait_ge(sem("c_squared"), upto("c_squared", m))
                link(dve.tensor_tensor(small[r, 16 + m:17 + m], small[r, 16 + m:17 + m], small[r, 24 + m:25 + m],
                                       ALU.add))
                dve.tensor_scalar(small[r, 33 + 2 * m:34 + 2 * m], small[r, 16 + m:17 + m], 1.0 / QL, EPS,
                                  ALU.mult, ALU.add)
                dve.tensor_scalar(small[r, 32 + 2 * m:33 + 2 * m], small[r, 32 + 2 * m:33 + 2 * m], 1.0 / KVL,
                                         EPS, ALU.mult, ALU.add).then_inc(
                    sem("c_mean"), tick("c_mean", m))
                dve.wait_ge(sem("c_root"), upto("c_root", m))
                link(dve.reciprocal(small[r, 32 + 2 * m:34 + 2 * m], small[r, 32 + 2 * m:34 + 2 * m]))
                if m >= 2:
                    dve.wait_ge(sem("turned"), upto("turned", "cq", m - 2, 1))
                rq, rk = small[r, 33 + 2 * m:34 + 2 * m], small[r, 32 + 2 * m:33 + 2 * m]
                dve.tensor_scalar(cq[r, m % 2, 0:512], PS[r, b[0], :], rq, None, ALU.mult)
                dve.tensor_scalar(cq[r, m % 2, 512:768], PS[r, b[1], 0:256], rq, None, ALU.mult)
                dve.scalar_tensor_tensor(out=lat[r, m, 0:256], in0=PS[r, b[1], 256:512], scalar=rk,
                                                in1=gkv[r, :], op0=ALU.mult, op1=ALU.mult).then_inc(
                    sem("latent_normed"), tick("latent_normed", m))
            elif kind == "uq":
                if m >= 2:
                    dve.wait_ge(sem("turned"), upto("turned", "uq", m - 2, 1))
                q = heads(q_tok[:, m % 2])
                for j in range(2):
                    src = PS[r, b[j], 0:384].rearrange("p (h n) -> p h n", h=4)
                    dve.tensor_copy(q[r, 4 * j:4 * j + 4, 0:64], src[:, :, 0:64])
                    ins = rope(dve, link, q[r, 4 * j:4 * j + 4, 64:96], src[:, :, 64:96], cc32[:, m], ss32[:, m], 16)
                    ins.then_inc(sem("q_roped"), tick("q_roped", m, j))
                if m == 4:
                    dve.wait_ge(sem("q_roped"), upto("q_roped", m, 1))
                    dve.wait_ge(sem("turned"), upto("turned", "qi", 4, 2))
                    dve.tensor_copy(dup[0:NS].rearrange("p h (a n) -> p h a n", a=4),
                                           q[0:NS, :, 64:96].unsqueeze(2).to_broadcast([NS, H, 4, 32])).then_inc(
                        sem("dup_ready"), tick("dup_ready", "uq"))

        def wait_unit_read(pe, u):
            kind, m = u
            if kind in ("qi", "qb", "kb"):
                pe.wait_ge(sem("b_roped"), upto("b_roped", *u))
            elif kind == "sm":
                pe.wait_ge(sem("unit_dve"), upto("unit_dve", *u))
                pe.wait_ge(sem("wi_scaled"), upto("wi_scaled", m))
            elif kind == "cq":
                pe.wait_ge(sem("latent_normed"), upto("latent_normed", m))
            elif kind == "uq":
                pe.wait_ge(sem("q_roped"), upto("q_roped", m, 1))
            else:
                pe.wait_ge(sem("unit_act"), upto("unit_act", *u))

        def pe_unit(pe, u):
            kind, m = u
            for v in before[u]:
                if v:
                    wait_unit_read(pe, v)
            b = banks[u]
            cols = token_cols(m) if kind not in ("kn", "kl", "ql", "wt") else None
            n = TW[m] if cols else 0

            def groups(bank, w, k_range, left, width, at=0, out_at=0):
                for k in range(k_range):
                    ins = pe.matmul(PS[0:n, b[bank], out_at:out_at + width], left[:, k, cols], w[:, k, at:at + width],
                                    start=k == 0, stop=k == k_range - 1)
                return ins

            if kind in ("qi", "qb", "kb", "vb"):
                pe.wait_ge(sem(f"w_{kind}_in"), upto(f"w_{kind}_in", kind))
                pe.wait_ge(sem("h_ready"), upto("h_ready", ("h", m, 1)))
                ins = groups(0, w_view(kind), KD, hT, 512)
            elif kind == "sm":
                pe.wait_ge(sem("w_sm_in"), upto("w_sm_in", "sm"))
                ins = groups(0, w_view(kind), KD, hT, 104)
            elif kind == "cq":
                pe.wait_ge(sem("w_c0_in"), upto("w_c0_in", "c0"))
                groups(0, w_view("c0"), KD, hT, 512)
                pe.wait_ge(sem("w_c1_in"), upto("w_c1_in", "c1"))
                ins = groups(1, w_view("c1"), KD, hT, 512)
            elif kind == "uq":
                pe.wait_ge(sem("w_uq_in"), upto("w_uq_in", "uq"))
                pe.wait_ge(sem("turned_act"), upto("turned_act", "cq", m, 1))
                groups(0, w_view("uq"), 6, cqT, 384)
                ins = groups(1, w_view("uq"), 6, cqT, 384, at=384)
            elif kind == "wt":
                return
            elif kind == "kn":
                pe.wait_ge(sem("turned_act"), upto("turned_act", "cq", 4, 2))
                for c in range(2):
                    ins = pe.matmul(PS[0:64, b[0], :], wuk[:, c, 64 * m:64 * m + 64], ckvT[:, c, 0:512],
                                    start=c == 0, stop=c == 1)
            elif kind == "kl":
                for h in range(H):
                    for c in range(2):
                        ins = pe.matmul(PS[0:64, b[0], 16 * h:16 * h + 16], wuk[:, c, 64 * h:64 * h + 64],
                                        ckvT[:, c, LAST:LAST + 16], start=c == 0, stop=c == 1)
            elif kind == "ql":
                pe.wait_ge(sem("turned_act"), upto("turned_act", "wt", 0, 3))
                pe.wait_ge(sem("turned_act"), upto("turned_act", "uq", 4, 1))
                for h in range(H):
                    ins = pe.matmul(PS[:, b[0], 64 * h:64 * h + 64], wukT[0:64, h, 128 * m:128 * m + 128],
                                    qT[0:64, h, 512:512 + NS], start=True, stop=True)
            elif kind == "vm":
                pe.wait_ge(sem("wuv_in"), upto("wuv_in", 0))
                cols = token_cols(m) if m < 4 else slice(LAST, LAST + 16)
                n = 128 if m < 4 else 16
                ins = groups(0, wuv, 2, ckvT, 512)
            ins.then_inc(sem("product"), tick("product", *u))

        sturns = [("i", b, i) for b in range(NB) for i in range(4)]
        for b in range(NB):
            sturns += [("p", b, 0), ("p", b, 1)] + [("c", b, c, f) for c in range(8) for f in range(2)]
            sturns += [("t", b, i) for i in range(5)]
        sturn_no = {key: i for i, key in enumerate(sturns)}
        keysT_users = [k for k in sturns if k[0] in "ic"]
        keysT_no = {key: i for i, key in enumerate(keysT_users)}

        def sturn_bank(key):
            return 4 + sturn_no[key] % 4

        def wait_stored(eng, name):
            if name == "kb":
                for m in range(NTILE):
                    eng.wait_ge(sem(f"stored_kb_p{m}"), upto(f"stored_kb_p{m}", m))
            else:
                eng.wait_ge(sem(f"stored_{name}_p"), upto(f"stored_{name}_p", 4))

        def phase_a_done(eng):
            eng.wait_ge(sem("product"), upto("product", "vb", 4))
            eng.wait_ge(sem("unit_act"), upto("unit_act", "vb", 4))
            eng.wait_ge(sem("b_roped"), upto("b_roped", "kb", 4))
            eng.wait_ge(sem("turned_act"), upto("turned_act", "kb", 4, 0))
            eng.wait_ge(sem("h_stored"), upto("h_stored", 0))
            for name in ("ki", "ckv", "kpe", "kb"):
                wait_stored(eng, name)
                eng.wait_ge(sem(f"stored_{name}_s"), upto(f"stored_{name}_s", 4))

        def pe_sturn(pe, key, srcs, width, right=None):
            i = sturn_no[key]
            if i >= 4:
                pe.wait_ge(sem("sturn_out"), upto("sturn_out", sturns[i - 4]))
            bank = PS[:, sturn_bank(key), :].rearrange("p (a n) -> p a n", n=width)
            for n, src in enumerate(srcs):
                k, w = src.shape
                if right is None:
                    ins = pe.transpose(bank[0:w, n, 0:k], src, ident[0:k, 0:k])
                else:
                    ins = pe.matmul(bank[0:w, n, :], src, right, start=True, stop=True)
            ins.then_inc(sem("sturned"), tick("sturned", key))

        def act_sturn(act, key, dst, src):
            act.wait_ge(sem("sturned"), upto("sturned", key))
            if key in keysT_no and keysT_no[key] >= 4:
                act.wait_ge(sem("keysT_used"), upto("keysT_used", keysT_users[keysT_no[key] - 4]))
            act.copy(dst, src).then_inc(sem("sturn_out"), tick("sturn_out", key))

        def pe_index(pe):
            phase_a_done(pe)
            def turn(b, i):
                if i == 0:
                    pe.wait_ge(sem(f"ik_in{b % 3}"), upto(f"ik_in{b % 3}", b))
                ik = raw[:, b % 3, :]
                pe_sturn(pe, ("i", b, i), [ik[:, 128 * (4 * i + q):128 * (4 * i + q) + 128] for q in range(4)], 128)

            def weigh(n):
                b, i, par = n
                g = index_groups.index(n)
                pe.wait_ge(sem("relued"), upto("relued", n))
                if g >= 2:
                    pe.wait_ge(sem("weighed_out"), upto("weighed_out", index_groups[g - 2]))
                w = 512 if i < 4 else NT
                pe.matmul(PS[0:8, 2 + g % 2, 0:w], wb[0:64, b, :], relu_i[0:64, g % 4, 0:w], start=True,
                                 stop=True).then_inc(
                    sem("weighed"), tick("weighed", n))

            turn(0, 0)
            pe.wait_ge(sem("wb_ready"), upto("wb_ready", NB - 1))
            nxt = [(b, i) for b in range(NB) for i in range(4)][1:] + [None]
            for n, (b, i, par) in enumerate(index_groups):
                if par == 0 and i < 4:
                    t = nxt[4 * b + i]
                    if t:
                        turn(*t)
                    pe.wait_ge(sem("sturn_out"), upto("sturn_out", ("i", b, i)))
                if n >= 2:
                    pe.wait_ge(sem("relued"), upto("relued", index_groups[n - 2]))
                q = qi_s[64 * par:64 * par + 64, 64 * b:64 * b + 64]
                if i < 4:
                    k = keysT[64 * par:64 * par + 64, keysT_no[("i", b, i)] % 4, :]
                    w = 512
                else:
                    k = kiT[0:64, 512 + NT * b:512 + NT * b + NT]
                    w = NT
                pe.matmul(PS[0:64, n % 2, 0:w], q, k, start=True, stop=True).then_inc(
                    sem("index_dots"), tick("index_dots", (b, i, par)))
                if i < 4 and par == 1:
                    same(("keysT_used", ("i", b, i)), ("index_dots", (b, i, par)))
                if n >= 1:
                    weigh(index_groups[n - 1])
            weigh(index_groups[-1])

        index_groups = [(b, i, par) for b in range(NB) for i in range(5) for par in range(2) if i < 4 or par == 0]

        def act_index(act):
            phase_a_done(act)
            order = []
            for b in range(NB):
                for i in range(4):
                    order.append(("turn", (b, i)))
                for i in range(5):
                    for par in range(2 if i < 4 else 1):
                        order.append(("relu", (b, i, par)))
            turn_list = [("i", b, i) for b in range(NB) for i in range(4)]

            def turn(n):
                if n < len(turn_list):
                    key = turn_list[n]
                    act_sturn(act, key, keysT[:, keysT_no[key] % 4, :], PS[:, sturn_bank(key), :])

            turn(0)
            for g, (b, i, par) in enumerate(index_groups):
                if par == 0 and i < 4:
                    turn(4 * b + i + 1)
                act.wait_ge(sem("index_dots"), upto("index_dots", (b, i, par)))
                if g >= 4:
                    act.wait_ge(sem("weighed"), upto("weighed", index_groups[g - 4]))
                w = 512 if i < 4 else NT
                act.activation(relu_i[0:64, g % 4, 0:w], PS[0:64, g % 2, 0:w], ACT.Relu, scale=0.125).then_inc(
                    sem("relued"), tick("relued", (b, i, par)))

        def dve_index(dve):
            phase_a_done(dve)
            dve.memset(qpe_z, 0.0).then_inc(sem("zeroed"), tick("zeroed"))
            dve.wait_ge(sem("wcol_in"), upto("wcol_in", H - 1))
            for b in range(NB):
                dve.tensor_scalar(wb[0:64, b, :], same_t[0:64], wcol[0:64, b:b + 1], None, ALU.mult).then_inc(
                    sem("wb_ready"), tick("wb_ready", b))
            by_key = row_scores[0:8, 0:PAST].rearrange("t (p j) -> t j p", j=32)
            for g, (b, i, par) in enumerate(index_groups):
                dve.wait_ge(sem("weighed"), upto("weighed", (b, i, par)))
                if b and i == 0 and par == 0:
                    dve.wait_ge(sem(f"rows_moved{(b - 1) % 2}"), upto(f"rows_moved{(b - 1) % 2}", b - 1))
                if i < 4:
                    ins = dve.tensor_copy(by_key[:, 8 * i + par:8 * i + par + 7:2, :],
                                          PS[0:8, 2 + g % 2, :].rearrange("t (q p) -> t q p", q=4))
                else:
                    ins = dve.tensor_tensor(row_scores[0:8, PAST:PAST + NT], PS[0:8, 2 + g % 2, 0:NT],
                                            causal8[0:8], ALU.add)
                ins.then_inc(sem("weighed_out"), tick("weighed_out", (b, i, par)))

        def gp_sample_loads(gp):
            phase_a_done(gp)
            gp.wait_ge(sem("index_ready"), upto("index_ready"))
            ik_rows = I["cache_idx_k"].rearrange("l n (q r) d -> (l n q) (r d)", q=4)
            for b in range(NB):
                if b >= 3:
                    gp.wait_ge(sem("sturned"), upto("sturned", ("i", b - 3, 3)))
                gp.indirect_dma_start(raw[:, b % 3, :], None, ik_rows,
                                             bass.IndirectOffsetOnAxis(ap=idx_row[:, b:b + 1], axis=0)).then_inc(
                    sem(f"ik_in{b % 3}"), tick(f"ik_in{b % 3}", b, by=16))
            kpe_rows = I["cache_mla_kpe"].rearrange("l n (q r) d -> (l n q) (r d)", q=4)
            ckv_rows = I["cache_mla_ckv"].rearrange("l n (q r) c -> (l n q) (r c)", q=16)
            for b in range(NB):
                if b:
                    gp.wait_ge(sem("sturned"), upto("sturned", ("p", b - 1, 1)))
                gp.indirect_dma_start(kpe_raw, None, kpe_rows,
                                             bass.IndirectOffsetOnAxis(ap=idx_row[:, b:b + 1], axis=0)).then_inc(
                    sem("kpe_in"), tick("kpe_in", b, by=16))
                for j in range(4):
                    n = 4 * b + j
                    if n < 3:
                        gp.wait_ge(sem("sturned"), upto("sturned", ("i", 5 + (n - 5) % 3, 3)))
                    if n < 5:
                        gp.wait_ge(sem("sturned"), upto("sturned", ("i", NB - 1, 3)))
                    else:
                        gp.wait_ge(sem("latents_used"), upto("latents_used", n - 5))
                    gp.indirect_dma_start(raw[:, n % 5, :], None, ckv_rows,
                                                 bass.IndirectOffsetOnAxis(ap=idx_ckv[:, b, j:j + 1], axis=0)).then_inc(
                        sem(f"ckv_in{n % 5}"), tick(f"ckv_in{n % 5}", n, by=16))

        def sp_sample(sp):
            for b in range(NB):
                sp.wait_ge(sem("weighed_out"), upto("weighed_out", (b, 4, 0)))
                sp.dma_start(pick_scores[8 * b:8 * b + 8, :], row_scores[0:8, :]).then_inc(
                    sem(f"rows_moved{b % 2}"), tick(f"rows_moved{b % 2}", b, by=16))
            sp.wait_ge(sem("stored_ckv_s"), upto("stored_ckv_s", 4))
            for b in range(NB):
                if b:
                    sp.wait_ge(sem("o_lat_done"), upto("o_lat_done", b - 1))
                sp.dma_start(lat_new[0:NT, :], O["new_ckv_s"][0, b]).then_inc(
                    sem("lat_new_in"), tick("lat_new_in", b, by=16))

        def pe_latent(pe):
            def turn(b, c, f):
                if c % 2 == 0 and f == 0:
                    n = 4 * b + c // 2
                    pe.wait_ge(sem(f"ckv_in{n % 5}"), upto(f"ckv_in{n % 5}", n))
                slot = raw[:, (4 * b + c // 2) % 5, :].rearrange("p (j c) -> p j c", j=8)
                pe_sturn(pe, ("c", b, c, f), [slot[:, 4 * (c % 2) + q, 128 * f:128 * f + 128] for q in range(4)], 128)

            for b in range(NB):
                pe.wait_ge(sem("kpe_in"), upto("kpe_in", b))
                for i in range(2):
                    pe_sturn(pe, ("p", b, i), [kpe_raw[:, 128 * (4 * i + q):128 * (4 * i + q) + 128]
                                               for q in range(4)], 128)
                turn(b, 0, 0)
                turn(b, 0, 1)
                pe.wait_ge(sem("sturn_out"), upto("sturn_out", ("p", b, 1)))
                pe.wait_ge(sem("qpe_spread"), upto("qpe_spread", b))
                if b:
                    pe.wait_ge(sem("new_scored"), upto("new_scored", b - 1))
                else:
                    pe.wait_ge(sem("relued"), upto("relued", index_groups[-1]))
                q2 = [ql_s[:, f, 64 * b:64 * b + 64] for f in range(2)]
                for c in range(8):
                    if c < 7:
                        turn(b, c + 1, 0)
                        turn(b, c + 1, 1)
                    out = PS[0:64, c % 2, :]
                    if c >= 2:
                        pe.wait_ge(sem("scored"), upto("scored", b, c - 2))
                    for f in range(2):
                        key = ("c", b, c, f)
                        pe.wait_ge(sem("sturn_out"), upto("sturn_out", key))
                        ins = pe.matmul(out, q2[f], keysT[:, keysT_no[key] % 4, :], start=f == 0, stop=False,
                                        skip_group_check=True)
                        ins.then_inc(sem("keysT_used"), tick("keysT_used", key))
                    for q in range(4):
                        ins = pe.matmul(out[:, 128 * q:128 * q + 128], qpe_z[:, q, :], kpeT[:, c, :], start=False,
                                        stop=q == 3, skip_group_check=True)
                    ins.then_inc(sem("latent_dots"), tick("latent_dots", b, c))
                pe.wait_ge(sem("scored"), upto("scored", b, 6))
                new = slice(NT * b, NT * b + NT)
                for f in range(2):
                    pe.matmul(PS[0:64, 0, 0:NT], q2[f], ckv_new[:, f, new], start=f == 0, stop=False)
                pe.matmul(PS[0:64, 0, 0:NT], qpe_s[0:32, 64 * b:64 * b + 64],
                                 kpe_new[0:32, NT * b:NT * b + NT], start=False, stop=True).then_inc(
                    sem("latent_dots"), tick("latent_dots", b, 8))
                pe.wait_ge(sem("diag_ready"), upto("diag_ready", b))
                for i in range(4):
                    pe_sturn(pe, ("t", b, i), [row_scores[0:64, 128 * j:128 * j + 128] for j in range(8 * i, 8 * i + 8)],
                             64, diag[0:64, :])
                pe_sturn(pe, ("t", b, 4), [row_scores[0:64, PAST:PAST + NT]], 64, diag[0:64, :])
                if b:
                    pe.wait_ge(sem("o_lat_out"), upto("o_lat_out", b - 1))
                else:
                    pe.wait_ge(sem("weighed_out"), upto("weighed_out", index_groups[-1]))
                for j in range(32):
                    if j % 8 == 0:
                        pe.wait_ge(sem("sturn_out"), upto("sturn_out", ("t", b, j // 8)))
                    slot = raw[:, (4 * b + j // 8) % 5, :].rearrange("p (j c) -> p j c", j=8)
                    for f in range(2):
                        ins = pe.matmul(PS[:, 2 + f, 0:64], slot[:, j % 8, 128 * f:128 * f + 128], probsT[:, j, :],
                                        start=j == 0, stop=False)
                    if j % 8 == 7:
                        ins.then_inc(sem("latents_used"), tick("latents_used", 4 * b + j // 8))
                pe.wait_ge(sem("sturn_out"), upto("sturn_out", ("t", b, 4)))
                pe.wait_ge(sem("lat_new_in"), upto("lat_new_in", b))
                for f in range(2):
                    ins = pe.matmul(PS[:, 2 + f, 0:64], lat_new[0:NT, 128 * f:128 * f + 128],
                                    probsT[0:NT, 32, :], start=False, stop=True)
                ins.then_inc(sem("o_lat_done"), tick("o_lat_done", b))
            pe.wait_ge(sem("o_lat_out"), upto("o_lat_out", NB - 1))
            for h in range(H):
                for f in range(2):
                    ins = pe.matmul(PS[64 * (h % 2):64 * (h % 2) + 64, 0, 64 * (h // 2):64 * (h // 2) + 64],
                                    wuv[:, f, 64 * h:64 * h + 64],
                                    o_lat[:, f, :].rearrange("p (b h t) -> p b h t", b=NB, h=H)[:, :, h, :],
                                    start=f == 0, stop=f == 1)
            ins.then_inc(sem("o_s_done"), tick("o_s_done", 0))

        def act_latent(act):
            for b in range(NB):
                for i in range(2):
                    act_sturn(act, ("p", b, i), kpeT[:, 4 * i:4 * i + 4, :],
                              PS[:, sturn_bank(("p", b, i)), :].rearrange("p (a n) -> p a n", a=4))
                for f in range(2):
                    turn_out(act, b, 0, f)
                if b:
                    act.wait_ge(sem("latent_dots"), upto("latent_dots", b - 1, 7))
                else:
                    act.wait_ge(sem("zeroed"), upto("zeroed"))
                for q in range(4):
                    ins = act.copy(qpe_z[32 * q:32 * q + 32, q, :], qpe_s[32 * q:32 * q + 32, 64 * b:64 * b + 64])
                ins.then_inc(sem("qpe_spread"), tick("qpe_spread", b))
                if b:
                    act.wait_ge(sem("sturned"), upto("sturned", ("t", b - 1, 4)))
                else:
                    act.wait_ge(sem("rows_moved1"), upto("rows_moved1", NB - 1))
                    act.wait_ge(sem("rows_moved0"), upto("rows_moved0", NB - 2))
                for c in range(8):
                    if c < 7:
                        for f in range(2):
                            turn_out(act, b, c + 1, f)
                    act.wait_ge(sem("latent_dots"), upto("latent_dots", b, c))
                    act.mul(row_scores[0:64, 512 * c:512 * c + 512], PS[0:64, c % 2, :], MLA_SCALE).then_inc(
                        sem("scored"), tick("scored", b, c))
                act.wait_ge(sem("neg_max"), upto("neg_max", b))
                act.activation(row_scores[0:64, :], row_scores[0:64, :], ACT.Exp, bias=col[0:64, 0:1],
                                      accum_out=col[0:64, 1:2]).then_inc(
                    sem("exped"), tick("exped", b))
                for i in range(4):
                    key = ("t", b, i)
                    act_sturn(act, key, probsT[:, 8 * i:8 * i + 8, :],
                              PS[:, sturn_bank(key), :].rearrange("p (a n) -> p a n", a=8))
                act_sturn(act, ("t", b, 4), probsT[0:NT, 32, :], PS[0:NT, sturn_bank(("t", b, 4)), 0:64])
                act.wait_ge(sem("o_lat_done"), upto("o_lat_done", b))
                act.copy(o_lat[:, :, 64 * b:64 * b + 64], PS[:, 2:4, 0:64]).then_inc(
                    sem("o_lat_out"), tick("o_lat_out", b))
            act.wait_ge(sem("o_s_done"), upto("o_s_done", 0))
            act.copy(oT_s, PS[:, 0, 0:256].rearrange("p (a n) -> p a n", a=4)).then_inc(
                sem("o_s_out"), tick("o_s_out", 0))

        def turn_out(act, b, c, f):
            key = ("c", b, c, f)
            act_sturn(act, key, keysT[:, keysT_no[key] % 4, :], PS[:, sturn_bank(key), :])

        def dve_latent(dve, link):
            for b in range(NB):
                dve.wait_ge(sem(f"rows_moved{b % 2}"), upto(f"rows_moved{b % 2}", b))
            steps = [(r, k) for r in range(TOPK_S // 8) for k in range(3)]
            for b in range(NB):
                mine = steps[12 * b:12 * b + 12]
                for n, (r, k) in enumerate(mine):
                    if k == 0:
                        link(dve.max(top8[0:64], pick_scores[0:64]))
                    elif k == 1:
                        dve.max_index(picked[0:64, 8 * r:8 * r + 8], top8[0:64], pick_scores[0:64])
                    else:
                        link(dve.match_replace(pick_scores[0:64], top8[0:64], pick_scores[0:64], TAKEN))
                        same(("picks_done",), ("chain_dve",))
                    if n < 8:
                        dve.wait_ge(sem("scored"), upto("scored", b, n))
                        if n == 0 and b:
                            dve.wait_ge(last.sem, last.value)
                        dve.tensor_reduce(chunk_max[0:64, n:n + 1], row_scores[0:64, 512 * n:512 * n + 512],
                                                 AX.X, ALU.max).then_inc(
                            sem("chunk_maxed"), tick("chunk_maxed", b, n))
                    if n == 8:
                        dve.wait_ge(sem("latent_dots"), upto("latent_dots", b, 8))
                        dve.scalar_tensor_tensor(out=row_scores[0:64, PAST:PAST + NT], in0=PS[0:64, 0, 0:NT],
                                                        scalar=MLA_SCALE, in1=causal8[0:64], op0=ALU.mult,
                                                        op1=ALU.add).then_inc(
                            sem("new_scored"), tick("new_scored", b))
                        dve.wait_ge(last.sem, last.value)
                        link(dve.tensor_reduce(chunk_max[0:64, 8:9], row_scores[0:64, PAST:PAST + NT], AX.X, ALU.max))
                        link(dve.tensor_reduce(col[0:64, 2:3], chunk_max[0:64, 0:9], AX.X, ALU.max))
                        dve.tensor_scalar(col[0:64, 0:1], col[0:64, 2:3], -1.0, None, ALU.mult).then_inc(
                            sem("neg_max"), tick("neg_max", b))
                    if n == 9:
                        dve.wait_ge(sem("exped"), upto("exped", b))
                        link(dve.reciprocal(col[0:64, 3:4], col[0:64, 1:2]))
                        dve.tensor_scalar(diag[0:64], ident[0:64, 0:64], col[0:64, 3:4], None, ALU.mult).then_inc(
                            sem("diag_ready"), tick("diag_ready", b))

        KEYS = [128, 256, 384, 512, NP]
        QW = [128, 128, 128, 128, 16]
        groups_p = []
        for m in range(NTILE):
            groups_p += [("i", m, h) for h in range(H)] if m else []
            groups_p += [("a", m, h) for h in range(H)] + [("b", m, h) for h in range(H)]
        group_no = {g: i for i, g in enumerate(groups_p)}
        steps_p = [g for g in groups_p if g[0] != "i"]
        step_no = {g: i for i, g in enumerate(steps_p)}
        pturns = []
        for g in steps_p:
            pturns.append(("P", g))
            if g[2] == H - 1:
                pturns.append(("O", g))
        pturn_no = {t: i + 1 for i, t in enumerate(pturns)}

        def q_cols(m):
            return slice(128 * m, 128 * m + 128) if m < 4 else slice(LAST, LAST + 16)

        def scores_at(g):
            n = 2 * (group_no[g] % 2)
            return PS[:, n:n + 2, :].rearrange("p a b -> p (a b)")

        def group_read(eng, g):
            eng.wait_ge(sem("relu_p_done" if g[0] == "i" else "masked"), upto("relu_p_done" if g[0] == "i" else "masked", g))

        def phase_c_done(eng):
            eng.wait_ge(sem("o_s_done"), upto("o_s_done", 0))
            eng.wait_ge(sem("o_s_out"), upto("o_s_out", 0))
            eng.wait_ge(sem("picks_done"), upto("picks_done"))

        def pe_prompt(pe):
            phase_c_done(pe)
            pe.wait_ge(sem("row_found"), upto("row_found"))
            for f in range(2):
                ins = pe.transpose(PS[:, 4, 64 * f:64 * f + 64], phys[0:64, 128 * f:128 * f + 128], ident[0:64, 0:64])
            ins.then_inc(sem("rows_turned"), tick("rows_turned"))
            pe.wait_ge(sem("o_s_out"), upto("o_s_out", 0))

            def score(g):
                kind, m, h = g
                n = group_no[g]
                if n >= 2:
                    group_read(pe, groups_p[n - 2])
                out = scores_at(g)[0:QW[m]]
                par = slice(64 * (h % 2), 64 * (h % 2) + 64)
                if kind == "i":
                    q, keys, last = qiT[par, h // 2, q_cols(m)], kiT[par], LAST
                elif kind == "b":
                    q, keys, last = qbT[par, h // 2, q_cols(m)], kbT[par, h // 2], LAST
                else:
                    q, keys, last = qT[0:96, h, q_cols(m)], kT[0:96, h], 512
                ins = pe.matmul(out[:, 0:min(KEYS[m], 512)], q, keys[:, 0:min(KEYS[m], 512)], start=True, stop=True)
                if m == 4:
                    ins = pe.matmul(out[:, 512:NP], q, keys[:, last:last + 16], start=True, stop=True)
                ins.then_inc(sem("scored_p"), tick("scored_p", g))

            def turn(t, srcs):
                n = pturn_no[t]
                if n >= 2:
                    pe.wait_ge(sem("pturn_out"), upto("pturn_out", pturns[n - 3] if n >= 3 else ("N",)))
                bank = PS[:, 4 + n % 2, :]
                at = 0
                for src in srcs:
                    k, w = src.shape
                    ins = pe.transpose(bank[0:w, at:at + k], src, ident[0:k, 0:k])
                    at += k
                ins.then_inc(sem("pturned"), tick("pturned", t))

            def weigh(g):
                kind, m, h = g
                w, n = QW[m], step_no[g]
                pe.wait_ge(sem("exped_p"), upto("exped_p", g))
                p = probs[0:w, n % 3, :]
                tiles = [(128 * k, 128) for k in range(min(m + 1, 4))] + ([(512, 16)] if m == 4 else [])
                turn(("P", g), [p[:, a:a + k] for a, k in tiles])
                pe.wait_ge(sem("pturn_out"), upto("pturn_out", ("P", g)))
                if n >= 2:
                    pe.wait_ge(sem("o_out"), upto("o_out", steps_p[n - 2]))
                v = vm if kind == "a" else vb
                for k, (a, rows_k) in enumerate(tiles):
                    vk = v[0:rows_k, k, :] if kind == "a" or k < 4 else vb_last[0:16]
                    ins = pe.matmul(PS[0:w, 6 + n % 2, 0:64], probs_T[0:rows_k, n % 2, k * w:k * w + w],
                                    vk[:, 64 * h:64 * h + 64], start=k == 0, stop=k == len(tiles) - 1)
                ins.then_inc(sem("o_done"), tick("o_done", g))

            def close(g):
                pe.wait_ge(sem("o_out"), upto("o_out", g))
                w = QW[g[1]]
                o = o_tok[0:w, 0 if g[0] == "a" else 1, :]
                turn(("O", g), [o[:, 128 * i:128 * i + 128] for i in range(4)])

            pe.wait_ge(sem("vb_last_in"), upto("vb_last_in"))
            open_step = None
            for g in groups_p:
                score(g)
                if g[0] == "i":
                    continue
                if open_step:
                    weigh(open_step)
                    if open_step[2] == H - 1:
                        close(open_step)
                open_step = g
            weigh(open_step)
            close(open_step)

        def act_prompt(act):
            phase_c_done(act)
            act.wait_ge(sem("rows_turned"), upto("rows_turned"))
            act.copy(row_no, PS[:, 4, 0:128].rearrange("p (a n) -> p a n", a=2)).then_inc(
                sem("row_no_ready"), tick("row_no_ready"))
            same(("pturn_out", ("N",)), ("row_no_ready",))
            act.copy(oT_a[:, :, 512:512 + NS], oT_s)

            def out(g):
                kind, m, h = g
                w, n = QW[m], step_no[g]
                t = ("P", g)
                act.wait_ge(sem("pturned"), upto("pturned", t))
                if n >= 2:
                    act.wait_ge(sem("o_done"), upto("o_done", steps_p[n - 2]))
                bank = PS[:, 4 + pturn_no[t] % 2, :]
                full = min(m + 1, 4) * w
                ins = act.copy(probs_T[:, n % 2, 0:full], bank[:, 0:full])
                if m == 4:
                    ins = act.copy(probs_T[0:16, n % 2, full:full + w], bank[0:16, full:full + w])
                ins.then_inc(sem("pturn_out"), tick("pturn_out", t))
                if h == H - 1:
                    t = ("O", g)
                    act.wait_ge(sem("pturned"), upto("pturned", t))
                    dst = oT_a if kind == "a" else oT_b
                    act.copy(dst[:, :, q_cols(m)], PS[:, 4 + pturn_no[t] % 2, 0:4 * w]
                                    .rearrange("p (a n) -> p a n", a=4)).then_inc(
                        sem("pturn_out"), tick("pturn_out", t))

            open_step = None
            for g in groups_p:
                kind, m, h = g
                w = QW[m]
                if kind == "i":
                    act.wait_ge(sem("scored_p"), upto("scored_p", g))
                    if group_no[g] >= 2 and (h >= 2 or m > 1):
                        act.wait_ge(sem("acc_done"), upto("acc_done", ("i", m, h - 2) if h >= 2 else ("i", m - 1, 6 + h)))
                    act.activation(relu_p[0:w, h % 2, 0:KEYS[m]], scores_at(g)[0:w, 0:KEYS[m]], ACT.Relu,
                                          scale=0.125).then_inc(
                        sem("relu_p_done"), tick("relu_p_done", g))
                    continue
                n = step_no[g]
                act.wait_ge(sem("neg_max_p"), upto("neg_max_p", g))
                st = stat[0:w, n % 3, :]
                act.activation(probs[0:w, n % 3, 0:KEYS[m]], probs[0:w, n % 3, 0:KEYS[m]], ACT.Exp,
                                      bias=st[:, 1:2], accum_out=st[:, 2:3]).then_inc(
                    sem("exped_p"), tick("exped_p", g))
                if open_step:
                    out(open_step)
                open_step = g
            out(open_step)

        def dve_prompt(dve, link):
            phase_c_done(dve)
            q = slice(0, NS)
            dve.wait_ge(sem("tables_in"), upto("tables_in"))
            link(dve.tensor_copy(pages_f[q], pages_q[q]))
            link(dve.tensor_scalar(page[q], picked[q], 7, None, ALU.logical_shift_right))
            link(dve.tensor_scalar(offset[q], picked[q], 127, None, ALU.bitwise_and))
            page_f, off_f = prod[q, 0:256], prod[q, 256:512]
            link(dve.tensor_copy(page_f, page[q]))
            link(dve.tensor_copy(off_f, offset[q]))
            link(dve.tensor_scalar(phys[q], page_f, 0.0, pages_f[q, 0:1], ALU.is_equal, ALU.mult))
            for p in range(1, NPG):
                link(dve.tensor_scalar(hit[q], page_f, float(p), pages_f[q, p:p + 1], ALU.is_equal, ALU.mult))
                link(dve.tensor_tensor(phys[q], phys[q], hit[q], ALU.add))
            dve.scalar_tensor_tensor(out=phys[q], in0=phys[q], scalar=float(PAGE), in1=off_f, op0=ALU.mult,
                                            op1=ALU.add).then_inc(
                sem("row_found"), tick("row_found"))
            link(dve.tensor_scalar(slot_bias[q], page_f, float(NPG), NEG, ALU.is_ge, ALU.mult))
            for j in range(NT):
                link(dve.tensor_scalar(hit[q], page_f, float(NPG), None, ALU.is_equal))
                link(dve.scalar_tensor_tensor(out=hit[q], in0=off_f, scalar=float(j), in1=hit[q],
                                              op0=ALU.is_equal, op1=ALU.mult))
                link(dve.tensor_reduce(new_hit[q, j:j + 1], hit[q], AX.X, ALU.max))
            link(dve.tensor_tensor(new_bias[q], same_b[q].unsqueeze(2).to_broadcast([NS, 8, 8]),
                                   new_hit[q].unsqueeze(1).to_broadcast([NS, 8, 8]), ALU.mult))
            link(dve.tensor_scalar(new_bias[q], new_bias[q], 1.0, -NEG, ALU.subtract, ALU.mult))

            def tail(g):
                w, n = QW[g[1]], step_no[g]
                st = stat[0:w, n % 3, :]
                dve.wait_ge(sem("exped_p"), upto("exped_p", g))
                link(dve.reciprocal(st[:, 3:4], st[:, 2:3]))
                dve.wait_ge(sem("o_done"), upto("o_done", g))
                if g[2] == 0 and g[1]:
                    dve.wait_ge(sem("pturned"), upto("pturned", ("O", (g[0], g[1] - 1, H - 1))))
                dve.tensor_scalar(o_tok[0:w, 0 if g[0] == "a" else 1, 64 * g[2]:64 * g[2] + 64],
                                         PS[0:w, 6 + n % 2, 0:64], st[:, 3:4], None, ALU.mult).then_inc(
                    sem("o_out"), tick("o_out", g))

            dve.wait_ge(sem("wi_last_in"), upto("wi_last_in"))
            open_step = None
            dve.memset(score_acc[:, 0:4], DUMMY)
            for g in groups_p:
                kind, m, h = g
                w, keys = QW[m], KEYS[m]
                if kind == "i":
                    weight = w_i[0:w, m, h:h + 1] if m < 4 else wi_last[0:16, h:h + 1]
                    acc = score_acc[0:w, 4:4 + keys]
                    dve.wait_ge(sem("relu_p_done"), upto("relu_p_done", g))
                    dve.wait_ge(last.sem, last.value)
                    r = relu_p[0:w, h % 2, 0:keys]
                    if h == 0:
                        ins = dve.tensor_scalar(acc, r, weight, None, ALU.mult)
                    else:
                        ins = dve.scalar_tensor_tensor(out=acc, in0=r, scalar=weight, in1=acc, op0=ALU.mult,
                                                       op1=ALU.add)
                    ins.then_inc(sem("acc_done"), tick("acc_done", g))
                    if h == H - 1:
                        dve.wait_ge(last.sem, last.value)
                        d = min(128 * m, 512)
                        link(dve.memset(score_acc[0:w, 0:4], DUMMY))
                        link(dve.tensor_tensor(acc[:, d:keys], acc[:, d:keys], wide_tri[0:w, 512:512 + keys - d],
                                               ALU.add))
                    continue
                n = step_no[g]
                p = probs[0:w, n % 3, 0:keys]
                st = stat[0:w, n % 3, :]
                if kind == "a" or m == 0:
                    d = 512 - min(128 * m, 512)
                    mask = wide_tri[0:w, d:d + keys]
                else:
                    mask = mask_s[0:w, 0:keys]
                scale = MLA_SCALE if kind == "a" else DSA_SCALE
                dve.wait_ge(sem("scored_p"), upto("scored_p", g))
                if n >= 3:
                    dve.wait_ge(sem("pturned"), upto("pturned", ("P", steps_p[n - 3])))
                dve.tensor_tensor_reduce(p, scores_at(g)[0:w, 0:keys], mask, scale, NEG, ALU.add, ALU.max,
                                                st[:, 0:1]).then_inc(
                    sem("masked"), tick("masked", g))
                dve.wait_ge(last.sem, last.value)
                dve.tensor_scalar(st[:, 1:2], st[:, 0:1], -1.0, None, ALU.mult).then_inc(
                    sem("neg_max_p"), tick("neg_max_p", g))
                if open_step:
                    tail(open_step)
                open_step = g
                if kind == "a" and m:
                    rounds = TOPK_P // 8 + 1
                    all_s = score_acc[0:w, 0:4 + keys]
                    for _ in range(rounds * h // H, rounds * (h + 1) // H):
                        link(dve.max(top8_p[0:w], all_s))
                        link(dve.match_replace(all_s, top8_p[0:w], all_s, TAKEN))
                    if h == H - 1:
                        link(dve.tensor_scalar(mask_s[0:w, 0:keys], score_acc[0:w, 4:4 + keys], -2e38, NEG,
                                               ALU.is_gt, ALU.mult))
                        d = min(128 * m, 512)
                        link(dve.tensor_tensor(mask_s[0:w, d:keys], mask_s[0:w, d:keys],
                                               wide_tri[0:w, 512:512 + keys - d], ALU.add))
                if n < NS:
                    score_rows(dve, n)
            tail(open_step)

        def score_rows(dve, q):
            dve.wait_ge(sem(f"rows_in{q % 5}"), upto(f"rows_in{q % 5}", "k", q))
            dve.wait_ge(sem(f"q_wide_in{q % 2}"), upto(f"q_wide_in{q % 2}", q))
            dve.wait_ge(last.sem, last.value)
            k = rows[:, q % 5, :].rearrange("p (f n) -> p f n", f=2)
            dve.tensor_tensor(prod.rearrange("p (f n) -> p f n", f=2), k,
                                     q_wide[:, q % 2, :].unsqueeze(1).to_broadcast([128, 2, 512]), ALU.mult).then_inc(
                sem("k_used"), tick("k_used", q))
            dve.wait_ge(last.sem, last.value)
            dve.tensor_reduce(dots_k[:, :, q], prod.rearrange("p (a d) -> p a d", d=64), AX.X, ALU.add).then_inc(
                sem("k_scored"), tick("k_scored", q))

        def sp_prompt(sp):
            phase_c_done(sp)
            sp.dma_start(wide_tri, I["c_wide_tri"]).then_inc(sem("tables_in"), tick("tables_in", by=16))
            sp.dma_start(same_b[0:NS], I["c_same_b"]).then_inc(sem("tables_in"), tick("tables_in", by=16))
            for b in range(NB):
                sp.dma_start(pages_q[8 * b:8 * b + 8, :], I["page_table"][b].partition_broadcast(8)).then_inc(
                    sem("tables_in"), tick("tables_in", by=16))
            wait_stored(sp, "vb")
            sp.dma_start(vb_last[0:16], O["new_v_p"][0, 0, 512:528].rearrange("l h d -> l (h d)")).then_inc(
                sem("vb_last_in"), tick("vb_last_in", by=16))
            sp.dma_start(wi_last[0:16], w_i[NS:NS + 16, 4, :]).then_inc(
                sem("wi_last_in"), tick("wi_last_in", by=16))
            sp.wait_ge(sem("q_b_stored"), upto("q_b_stored", 0))
            for q in range(NS):
                if q >= 2:
                    sp.wait_ge(sem("k_used"), upto("k_used", q - 2))
                sp.dma_start(q_wide[:, q % 2, :], scratch["q_b"][q].partition_broadcast(128)).then_inc(
                    sem(f"q_wide_in{q % 2}"), tick(f"q_wide_in{q % 2}", q, by=16))

        def gp_gather(gp):
            phase_c_done(gp)
            gp.wait_ge(sem("row_no_ready"), upto("row_no_ready"))
            for name, pool in (("k", I["cache_dsa_k"]), ("v", I["cache_dsa_v"])):
                pool_rows = pool.rearrange("l n p h d -> (l n p) (h d)")
                for q in range(NS):
                    if q >= 5 or name == "v":
                        if q >= 5:
                            gp.wait_ge(sem(f"{name}_used"), upto(f"{name}_used", q - 5))
                        else:
                            gp.wait_ge(sem("k_used"), upto("k_used", max(x for x in range(NS) if x % 5 == q)))
                    for f in range(2):
                        gp.indirect_dma_start(rows[:, q % 5, 512 * f:512 * f + 512], None, pool_rows,
                                                     bass.IndirectOffsetOnAxis(ap=row_no[:, f, q:q + 1], axis=0)).then_inc(
                            sem(f"rows_in{q % 5}"), tick(f"rows_in{q % 5}", *((name, q) if f else ()), by=16))

        def pe_sparse(pe):
            for g in groups_p[-2:]:
                group_read(pe, g)
            for g in steps_p[-2:]:
                pe.wait_ge(sem("o_out"), upto("o_out", g))
            for t in pturns[-2:]:
                pe.wait_ge(sem("pturn_out"), upto("pturn_out", t))
            for h in range(H):
                par = slice(64 * (h % 2), 64 * (h % 2) + 64)
                ins = pe.matmul(PS[0:NS, 4 + h % 2, 64 * (h // 2):64 * (h // 2) + 64], qbT[par, h // 2, 512:512 + NS],
                                kbT[par, h // 2, 512:512 + NS], start=True, stop=True)
            ins.then_inc(sem("new_dots"), tick("new_dots"))
            pe.wait_ge(sem("k_scored"), upto("k_scored", NS - 1))
            for i in range(4):
                for n in range(4):
                    ins = pe.transpose(PS[0:NS, i, 128 * n:128 * n + 128], dots_k[:, 4 * i + n, :], ident)
                ins.then_inc(sem("dots_turned"), tick("dots_turned", i))
            pe.wait_ge(sem("sel_probs"), upto("sel_probs"))
            for f in range(2):
                for h in range(H):
                    ins = pe.transpose(PS[:, f, 64 * h:64 * h + 64], s_sel[0:NS, h, 128 * f:128 * f + 128],
                                       ident[0:NS, 0:NS])
                ins.then_inc(sem("sel_turned"), tick("sel_turned", f))
            for h in range(H):
                ins = pe.transpose(PS[0:NS, 2, 64 * h:64 * h + 64], s_sel[0:NS, h, TOPK_S:TOPK_S + NS],
                                   ident[0:NS, 0:NS])
            ins.then_inc(sem("sel_turned"), tick("sel_turned", 2))
            for f in range(3):
                pe.wait_ge(sem("sel_out"), upto("sel_out", f))
            for h in range(H):
                p = h // 2
                ins = pe.matmul(PS[:, 7, 64 * h:64 * h + 64], vb[0:NS, 4, 128 * p:128 * p + 128], p_new[0:NS, h, :],
                                start=True, stop=True)
            ins.then_inc(sem("o_new_done"), tick("o_new_done"))
            for q in range(NS):
                pe.wait_ge(sem(f"rows_in{q % 5}"), upto(f"rows_in{q % 5}", "v", q))
                v = rows[:, q % 5, :].rearrange("p (f n) -> p f n", f=2)
                for p in range(4):
                    for f in range(2):
                        ins = pe.matmul(PS[:, 6, 8 * q + 2 * p:8 * q + 2 * p + 2], v[:, f, 128 * p:128 * p + 128],
                                        p_sel[:, f, q, 2 * p:2 * p + 2], start=f == 0, stop=f == 1)
                ins.then_inc(sem("v_used"), tick("v_used", q))

        def act_sparse(act):
            act.wait_ge(sem("sel_shifted"), upto("sel_shifted"))
            act.activation(s_sel[0:NS], s_sel[0:NS], ACT.Exp).then_inc(sem("sel_exped"), tick("sel_exped"))
            for f in range(2):
                act.wait_ge(sem("sel_turned"), upto("sel_turned", f))
                act.copy(p_sel[:, f].rearrange("p q h -> p h q"),
                                PS[:, f, :].rearrange("p (h q) -> p h q", h=H)).then_inc(
                    sem("sel_out"), tick("sel_out", f))
            act.wait_ge(sem("sel_turned"), upto("sel_turned", 2))
            act.copy(p_new[0:NS], PS[0:NS, 2, :].rearrange("p (h q) -> p h q", h=H)).then_inc(
                sem("sel_out"), tick("sel_out", 2))
            act.wait_ge(sem("o_new_done"), upto("o_new_done"))
            act.wait_ge(sem("k_scored"), upto("k_scored", NS - 1))
            act.copy(prod[:, 0:512], PS[:, 7, :]).then_inc(sem("o_new_out"), tick("o_new_out"))

        def dve_sparse(dve, link):
            q = slice(0, NS)
            dve.wait_ge(sem("new_dots"), upto("new_dots"))
            bias = new_bias[q].rearrange("p a b -> p (a b)").unsqueeze(1).to_broadcast([NS, 4, NS])
            for par in range(2):
                dve.scalar_tensor_tensor(out=s_sel[q, par:H:2, TOPK_S:TOPK_S + NS],
                                         in0=PS[q, 4 + par, 0:256].rearrange("p (h k) -> p h k", h=4),
                                         scalar=DSA_SCALE, in1=bias, op0=ALU.mult, op1=ALU.add)
            for i in range(4):
                f, h0 = i // 2, 4 * (i % 2)
                dve.wait_ge(sem("dots_turned"), upto("dots_turned", i))
                link(dve.scalar_tensor_tensor(out=s_sel[q, h0:h0 + 4, 128 * f:128 * f + 128],
                                              in0=PS[q, i, :].rearrange("p (h k) -> p h k", h=4), scalar=DSA_SCALE,
                                              in1=slot_bias[q, 128 * f:128 * f + 128].unsqueeze(1)
                                              .to_broadcast([NS, 4, 128]), op0=ALU.mult, op1=ALU.add))
            wide = lambda v: v[q].unsqueeze(2).to_broadcast([NS, H, TOPK_S + NS])
            link(dve.tensor_reduce(head_max[q], s_sel[q], AX.X, ALU.max))
            dve.tensor_tensor(s_sel[q], s_sel[q], wide(head_max), ALU.subtract).then_inc(
                sem("sel_shifted"), tick("sel_shifted"))
            dve.wait_ge(sem("sel_exped"), upto("sel_exped"))
            link(dve.tensor_reduce(head_sum[q], s_sel[q], AX.X, ALU.add))
            link(dve.reciprocal(head_sum[q], head_sum[q]))
            dve.tensor_tensor(s_sel[q], s_sel[q], wide(head_sum), ALU.mult).then_inc(
                sem("sel_probs"), tick("sel_probs"))
            dve.wait_ge(sem("v_used"), upto("v_used", NS - 1))
            dve.wait_ge(sem("o_new_out"), upto("o_new_out"))
            for par in range(2):
                r = slice(64 * par, 64 * par + 64)
                ins = dve.tensor_tensor(oT_b[r, :, 512:512 + NS],
                                        PS[r, 6, :].rearrange("p (q a b) -> p b a q", q=NS, a=4)[:, par],
                                        prod[r, 0:512].rearrange("p (a b q) -> p b a q", a=4, b=2)[:, par], ALU.add)
            ins.then_inc(sem("o_b_ready"), tick("o_b_ready"))

        mix_units = [(n, m) for n in range(2) for m in range(NTILE)]

        def mix_weights(n):
            if n == 0:
                w = flat(w_slots)
                gate = [w[:, 4096 * i:4096 * i + 4096] for i in range(2)]
                branch = [w[:, 8192 + 2048 * i:8192 + 2048 * i + 2048] for i in range(2)]
            else:
                gate = [w_b1[:, i, :] for i in range(2)]
                t = flat(o_mixT)
                branch = [t[:, 2048 * i:2048 * i + 2048] for i in range(2)]
            return ([g.rearrange("p (k n) -> p k n", k=KD) for g in gate],
                    [b.rearrange("p (k n) -> p k n", k=4) for b in branch])

        w_out = flat(w_slots)[:, 0:8192].rearrange("p (n k c) -> p n k c", n=2, k=KD)
        up_pieces = [(kind, p) for p in range(NF // 2) for kind in ("g", "u")]
        down_pieces = [(n, p) for n in range(2) for p in range(6)]
        pieces = [("up", x) for x in up_pieces] + [("down", x) for x in down_pieces]
        piece_no = {x: i for i, x in enumerate(pieces)}

        def piece_slot(x):
            return w_slots[:, piece_no[x] % 6, :]

        def heads_done(eng):
            eng.wait_ge(sem("o_b_ready"), upto("o_b_ready"))
            eng.wait_ge(sem("v_used"), upto("v_used", NS - 1))
            for t in pturns[-2:]:
                eng.wait_ge(sem("pturn_out"), upto("pturn_out", t))
            eng.wait_ge(sem("pturn_out"), upto("pturn_out", ("O", ("a", 4, H - 1))))
            eng.wait_ge(sem("o_new_out"), upto("o_new_out"))

        def x_rows(m):
            if m == 0:
                return [(slice(0, NM), None), (slice(NM, 128), slice(0, 128 - NM))]
            if m < 4:
                return [(slice(0, 128), slice(128 * m - NM, 128 * m + 128 - NM))]
            return [(slice(NS, NS + 16), slice(512 - NM, 512))]

        def sp_merge(sp):
            heads_done(sp)
            sp.dma_start(flat(hT_f), scratch["hT"]).then_inc(sem("h_back"), tick("h_back", 0, by=16))
            w_in = I["w_in"][0].rearrange("(k p) n -> p k n", p=128)
            br = [I[x][0].rearrange("(k p) n -> p k n", p=128) for x in ("w_br_a", "w_br_b")]
            for n in range(2):
                gate, branch = mix_weights(n)
                for i, at in enumerate((C_GA, C_GB)):
                    sp.dma_start(gate[i], w_in[:, :, at + 512 * n:at + 512 * n + 512]).then_inc(
                        sem(f"mix_w_in{n}"), tick(f"mix_w_in{n}", by=16))
                    sp.dma_start(branch[i], br[i][:, :, 512 * n:512 * n + 512]).then_inc(
                        sem(f"mix_w_in{n}"), tick(f"mix_w_in{n}", by=16))
            for m in range(NTILE):
                for part, src in x_rows(m):
                    rows_in = I["meta_tokens"] if src is None else I["x_prompt"][0, src, :]
                    sp.dma_start(x2[part, m, :], rows_in).then_inc(sem("x_back"), tick("x_back", by=16))
            sp.dma_start(x2[0:NS, 4, :], I["x_sample"].rearrange("b t d -> (b t) d")).then_inc(
                sem("x_back"), tick("x_back", by=16))
            sp.wait_ge(sem("mixed_dots"), upto("mixed_dots", (0, 4)))
            for n in range(2):
                sp.dma_start(w_out[:, n], I["w_o"][0].rearrange("(k p) n -> p k n", p=128)
                                    [:, :, 512 * n:512 * n + 512]).then_inc(
                    sem("w_out_in"), tick("w_out_in", by=16))
            sp.wait_ge(sem("mixed_dots"), upto("mixed_dots", (1, 4)))
            sp.dma_start(conv_rows[0:66], I["ffn_conv_w"][0].rearrange("j (f p) -> (j f) p", p=128)).then_inc(
                sem("conv_in"), tick("conv_in", by=16))
            sp.dma_start(conv_rows[66:88], I["ffn_conv_b"].rearrange("a (f p) -> (a f) p", p=128)).then_inc(
                sem("conv_in"), tick("conv_in", by=16))
            sp.wait_ge(sem("mixed"), upto("mixed", (1, 4)))
            sp.dma_start(conv_state[0:16], I["state_ffn_conv"][0].rearrange("b j f -> (b j) f")).then_inc(
                sem("conv_in"), tick("conv_in", by=16))
            for i, x in enumerate(pieces):
                if i < 4:
                    sp.wait_ge(sem("out_dots"), upto("out_dots", (1, 4)))
                elif i >= 6:
                    sp.wait_ge(sem("piece_used"), upto("piece_used", pieces[i - 6]))
                if x[0] == "up":
                    kind, p = x[1]
                    src = I["w_ffn_" + kind][0].rearrange("(k p) n -> p k n", p=128)[:, :, 256 * p:256 * p + 256]
                    dst = piece_slot(x).rearrange("p (k n) -> p k n", k=KD)
                else:
                    n, p = x[1]
                    k = min(4, NF - 4 * p)
                    src = I["w_ffn_d"][0].rearrange("(f p) n -> p f n", p=128)[:, 4 * p:4 * p + k,
                                                                                 512 * n:512 * n + 512]
                    dst = piece_slot(x)[:, 0:512 * k].rearrange("p (k n) -> p k n", k=k)
                sp.dma_start(dst, src).then_inc(sem(f"piece_in{i % 6}"), tick(f"piece_in{i % 6}", x, by=16))
                if i == 6:
                    sp.wait_ge(sem("h2_ready"), upto("h2_ready", ("h2", 4, 1)))
                    sp.dma_start(g_row, I["final_g"].partition_broadcast(128)).then_inc(
                        sem("g_row_in"), tick("g_row_in", by=16))
            sp.wait_ge(sem("conv_turned_out"), upto("conv_turned_out", NF - 1))
            sp.dma_start(O["new_conv_s"][0].rearrange("b j f -> (b j) f"), conv_out[0:16]).then_inc(
                sem("final_store"), tick("final_store", by=16))
            sp.dma_start(O["new_conv_p"][0, 0], conv_out[16:18]).then_inc(
                sem("final_store"), tick("final_store", by=16))
            for m in range(NTILE):
                sp.wait_ge(sem("y_ready"), upto("y_ready", m))
                for part, dst in x_rows(m):
                    if dst is not None:
                        sp.dma_start(O["y_prompt"][0, dst, :], x2[part, m, :]).then_inc(
                            sem("final_store"), tick("final_store", by=16))
                if m == 4:
                    sp.dma_start(O["y_sample"].rearrange("b t d -> (b t) d"), x2[0:NS, m, :]).then_inc(
                        sem("final_store"), tick("final_store", by=16))
            sp.wait_ge(sem("final_store"), upto("final_store"))

        def pe_merge(pe):
            heads_done(pe)
            pe.wait_ge(sem("h_back"), upto("h_back", 0))
            for i, (n, m) in enumerate(mix_units):
                pe.wait_ge(sem(f"mix_w_in{n}"), upto(f"mix_w_in{n}"))
                if i >= 2:
                    pe.wait_ge(sem("mixed"), upto("mixed", mix_units[i - 2]))
                gate, branch = mix_weights(n)
                b, c, w = 4 * (i % 2), token_cols(m), TW[m]
                for j in range(2):
                    for k in range(KD):
                        pe.matmul(PS[0:w, b + j, :], hT_f[:, k, c], gate[j][:, k, :], start=k == 0, stop=k == KD - 1)
                for j, o in enumerate((oT_a, oT_b)):
                    for k in range(4):
                        ins = pe.matmul(PS[0:w, b + 2 + j, :], o[:, k, c], branch[j][:, k, :], start=k == 0,
                                        stop=k == 3)
                ins.then_inc(sem("mixed_dots"), tick("mixed_dots", (n, m)))
            for m in range(NTILE):
                pe.wait_ge(sem("mixed"), upto("mixed", (1, m)))
                if m == 0:
                    pe.wait_ge(sem("mixed"), upto("mixed", (1, 3)))
                for j in range(2):
                    i = 2 * m + j
                    if i >= 4:
                        pe.wait_ge(sem("mix_turn_out"), upto("mix_turn_out", (i - 4) // 2, i % 2))
                    for k in range(4):
                        ins = pe.transpose(PS[:, i % 4, 128 * k:128 * k + TW[m]],
                                           o_mix[0:TW[m], m, 512 * j + 128 * k:512 * j + 128 * k + 128],
                                           ident[0:TW[m], 0:TW[m]])
                    ins.then_inc(sem("mix_turned"), tick("mix_turned", m, j))
            pe.wait_ge(sem("mixed"), upto("mixed", (1, 4)))
            pe.wait_ge(sem("w_out_in"), upto("w_out_in"))

            def h2_turn(m):
                pe.wait_ge(sem("x_normed"), upto("x_normed", m))
                for j in range(2):
                    if m >= 2:
                        pe.wait_ge(sem("h2_ready"), upto("h2_ready", ("h2", m - 2, j)))
                    else:
                        pe.wait_ge(sem("mix_turn_out"), upto("mix_turn_out", 4 - m, j))
                    for k in range(4):
                        ins = pe.transpose(PS[:, 2 * (m % 2) + j, 128 * k:128 * k + TW[m]],
                                           x_norm[0:TW[m], m % 2, 512 * j + 128 * k:512 * j + 128 * k + 128],
                                           ident[0:TW[m], 0:TW[m]])
                    ins.then_inc(sem("h2_turned"), tick("h2_turned", m, j))

            for m in range(NTILE):
                pe.wait_ge(sem("mix_turn_out"), upto("mix_turn_out", m, 1))
                for n in range(2):
                    if m >= 2:
                        pe.wait_ge(sem("x2_ready"), upto("x2_ready", m - 2, n))
                    for k in range(KD):
                        ins = pe.matmul(PS[0:TW[m], 4 + 2 * (m % 2) + n, :], o_mixT[:, k, token_cols(m)],
                                        w_out[:, n, k, :], start=k == 0, stop=k == KD - 1)
                    ins.then_inc(sem("out_dots"), tick("out_dots", (n, m)))
                if m:
                    h2_turn(m - 1)
            h2_turn(4)
            pe.wait_ge(sem("conv_in"), upto("conv_in"))
            pe.wait_ge(sem("x2_ready"), upto("x2_ready", 3, 1))
            pe.wait_ge(sem("x2_ready"), upto("x2_ready", 4, 1))
            pe_ffn(pe)

        def pe_ffn(pe):
            pe.transpose(PS[:, 6, 0:88], conv_rows[0:88], ident[0:88, 0:88]).then_inc(
                sem("conv_w_turned"), tick("conv_w_turned"))
            pe.wait_ge(sem("h2_ready"), upto("h2_ready", ("h2", 4, 1)))
            pe.wait_ge(sem("conv_w_out"), upto("conv_w_out"))

            def last_rows(f):
                pe.wait_ge(sem("last_two_ready"), upto("last_two_ready", f))
                if f:
                    pe.wait_ge(sem("conv_turned_out"), upto("conv_turned_out", f - 1))
                pe.transpose(PS[0:18, 7, 0:128], last_two[:, f % 2, :], ident).then_inc(
                    sem("conv_turned"), tick("conv_turned", f))

            for f in range(NF):
                b = 3 * (f % 2)
                if f >= 2:
                    pe.wait_ge(sem("gated"), upto("gated", f - 2))
                if f:
                    pe.wait_ge(sem("state_out"), upto("state_out", f - 1))
                pe.transpose(PS[:, 6, 0:16], conv_state[0:16, 128 * f:128 * f + 128], ident[0:16, 0:16]).then_inc(
                    sem("state_turned"), tick("state_turned", f))
                for j, kind in enumerate("gu"):
                    x = ("up", (kind, f // 2))
                    pe.wait_ge(sem(f"piece_in{piece_no[x] % 6}"), upto(f"piece_in{piece_no[x] % 6}", x))
                    w = piece_slot(x).rearrange("p (k n) -> p k n", k=KD)[:, :, 128 * (f % 2):128 * (f % 2) + 128]
                    for k in range(KD):
                        pe.matmul(PS[:, b + j, :], w[:, k, :], h2T[:, k, 0:512], start=k == 0, stop=k == KD - 1)
                    for k in range(KD):
                        ins = pe.matmul(PS[:, b + 2, 128 * j:128 * j + 80], w[:, k, :], h2T[:, k, 512:NCOL],
                                        start=k == 0, stop=k == KD - 1)
                    if f % 2:
                        ins.then_inc(sem("piece_used"), tick("piece_used", x))
                        same(("up_done", f, j), ("piece_used", x))
                    else:
                        ins.then_inc(sem("up_done"), tick("up_done", f, j))
                if f:
                    last_rows(f - 1)
            last_rows(NF - 1)
            for g in (NF - 2, NF - 1):
                pe.wait_ge(sem("gated"), upto("gated", g))
            pe.wait_ge(sem("state_out"), upto("state_out", NF - 1))
            for n in range(2):
                for p in range(6):
                    x = ("down", (n, p))
                    pe.wait_ge(sem(f"piece_in{piece_no[x] % 6}"), upto(f"piece_in{piece_no[x] % 6}", x))
                    k = min(4, NF - 4 * p)
                    w = piece_slot(x)[:, 0:512 * k].rearrange("p (k n) -> p k n", k=k)
                    for i in range(k):
                        f = 4 * p + i
                        for m in range(NTILE):
                            if f == 0 and n == 0 and m == 0:
                                pe.wait_ge(sem("conv_turned_out"), upto("conv_turned_out", NF - 1))
                            if f == 0 and n == 1 and m >= 3:
                                pe.wait_ge(sem("y_summed"), upto("y_summed", 0, m - 3))
                            ins = pe.matmul(PS[0:TW[m], (5 * n + m) % 8, :], upT[:, f, token_cols(m)], w[:, i, :],
                                            start=f == 0, stop=f == NF - 1)
                            if f == NF - 1:
                                ins.then_inc(sem("y_dots"), tick("y_dots", n, m))
                    if p < 5:
                        ins.then_inc(sem("piece_used"), tick("piece_used", x))
                    else:
                        same(("piece_used", x), ("y_dots", n, 4))

        def root(act, m, name):
            act.wait_ge(sem(name + "_mean"), upto(name + "_mean", m))
            act.activation(small[0:TW[m], 8 + m:9 + m], small[0:TW[m], m:m + 1], ACT.Sqrt).then_inc(
                sem(name + "_root"), tick(name + "_root", m))

        def act_merge(act):
            heads_done(act)
            for i, (n, m) in enumerate(mix_units):
                act.wait_ge(sem("mixed_dots"), upto("mixed_dots", (n, m)))
                if i >= 2:
                    act.wait_ge(sem("mixed"), upto("mixed", mix_units[i - 2]))
                w = TW[m]
                ins = act.activation(gates[0:w, i % 2], PS[0:w, 4 * (i % 2):4 * (i % 2) + 2, :], ACT.Sigmoid)
                ins.then_inc(sem("gates_ready"), tick("gates_ready", (n, m)))
            for m in range(NTILE):
                for j in range(2):
                    act.wait_ge(sem("mix_turned"), upto("mix_turned", m, j))
                    act.copy(o_mixT[:, 4 * j:4 * j + 4, token_cols(m)], PS[:, (2 * m + j) % 4, :]
                                    .rearrange("p (a n) -> p a n", a=4)[:, :, 0:TW[m]]).then_inc(
                        sem("mix_turn_out"), tick("mix_turn_out", m, j))
            for m in range(NTILE):
                act.wait_ge(sem("x2_ready"), upto("x2_ready", m, 1))
                if m >= 2:
                    act.wait_ge(sem("h2_turned"), upto("h2_turned", m - 2, 1))
                act.activation(x_norm[0:TW[m], m % 2, :], x2[0:TW[m], m, :], ACT.Square,
                                      accum_out=small[0:TW[m], m:m + 1]).then_inc(
                    sem("x2_squared"), tick("x2_squared", m))
                root(act, m, "x2")
            act.wait_ge(sem("conv_w_turned"), upto("conv_w_turned"))
            act.copy(conv_w, PS[:, 6, 0:88]).then_inc(sem("conv_w_out"), tick("conv_w_out"))
            for f in range(NF + 1):
                if f < NF:
                    b, s2 = 3 * (f % 2), f % 2
                    cp, cs = conv_prompt(s2), conv_sample(s2)
                    if f >= 2:
                        act.wait_ge(sem("conv_summed"), upto("conv_summed", f - 2))
                        act.wait_ge(sem("last_two_ready"), upto("last_two_ready", f - 2))
                    else:
                        act.wait_ge(sem("h2_turned"), upto("h2_turned", 4, 1))
                        act.wait_ge(sem("h2_ready"), upto("h2_ready", ("h2", 4, 1)))
                        act.wait_ge(sem("pads_zeroed"), upto("pads_zeroed"))
                    act.wait_ge(sem("state_turned"), upto("state_turned", f))
                    act.copy(cs[:, :, 0:2], PS[:, 6, 0:16].rearrange("p (b j) -> p b j", b=NB)).then_inc(
                        sem("state_out"), tick("state_out", f))
                    act.wait_ge(sem("up_done"), upto("up_done", f, 0))
                    act.copy(cp[:, 2:514], PS[:, b, :])
                    act.wait_ge(sem("up_done"), upto("up_done", f, 1))
                    act.copy(cs[:, :, 2:10], PS[:, b + 2, 0:NS].rearrange("p (b t) -> p b t", b=NB))
                    act.copy(cp[:, 514:530], PS[:, b + 2, NS:NS + 16]).then_inc(
                        sem("conv_in_ready"), tick("conv_in_ready", f))
                    act.wait_ge(last.sem, last.value)
                    if f >= 2:
                        act.wait_ge(sem("conv_turned"), upto("conv_turned", f - 2))
                    act.copy(last_two[:, s2, 0:16].rearrange("p (b j) -> p b j", b=NB), cs[:, :, 8:10])
                    act.copy(last_two[:, s2, 16:18], cp[:, 528:530]).then_inc(sem("last_two_ready"), tick("last_two_ready", f))
                if f:
                    act.wait_ge(sem("conv_summed"), upto("conv_summed", f - 1))
                    if f >= 3:
                        act.wait_ge(sem("gated"), upto("gated", f - 3))
                    act.activation(conv_sig[:, (f - 1) % 2, :], conv_sum[:, (f - 1) % 2, :], ACT.Sigmoid).then_inc(
                        sem("sig_ready"), tick("sig_ready", f - 1))
                    act.wait_ge(sem("conv_turned"), upto("conv_turned", f - 1))
                    act.copy(conv_out[0:18, 128 * (f - 1):128 * f], PS[0:18, 7, 0:128]).then_inc(
                        sem("conv_turned_out"), tick("conv_turned_out", f - 1))
            for m in range(NTILE):
                act.wait_ge(sem("y_summed"), upto("y_summed", 1, m))
                act.activation(flat(conv_sig)[0:TW[m], 0:D], x2[0:TW[m], m, :], ACT.Square,
                                      accum_out=small[0:TW[m], m:m + 1]).then_inc(
                    sem("y_squared"), tick("y_squared", m))
                root(act, m, "y")

        def conv_prompt(s2):
            return conv_in[:, s2, 0:530]

        def conv_sample(s2):
            return conv_in[:, s2, 530:610].rearrange("p (b t) -> p b t", b=NB)

        def mean(dve, m, name):
            dve.wait_ge(sem(name + "_squared"), upto(name + "_squared", m))
            dve.tensor_scalar(small[0:TW[m], m:m + 1], small[0:TW[m], m:m + 1], 1.0 / D, EPS, ALU.mult,
                                     ALU.add).then_inc(
                sem(name + "_mean"), tick(name + "_mean", m))

        def dve_merge(dve, link):
            heads_done(dve)
            for i, (n, m) in enumerate(mix_units):
                w, b = TW[m], 4 * (i % 2)
                dve.wait_ge(sem("gates_ready"), upto("gates_ready", (n, m)))
                g = gates[0:w, i % 2]
                link(dve.tensor_tensor(g, g, PS[0:w, b + 2:b + 4, :], ALU.mult))
                dve.tensor_tensor(o_mix[0:w, m, 512 * n:512 * n + 512], g[:, 0], g[:, 1], ALU.add).then_inc(
                    sem("mixed"), tick("mixed", (n, m)))

            def add_x(m):
                for n in range(2):
                    dve.wait_ge(sem("out_dots"), upto("out_dots", (n, m)))
                    x = x2[0:TW[m], m, 512 * n:512 * n + 512]
                    dve.tensor_tensor(x, x, PS[0:TW[m], 4 + 2 * (m % 2) + n, :], ALU.add).then_inc(
                        sem("x2_ready"), tick("x2_ready", m, n))

            def h2_out(m):
                for j in range(2):
                    dve.wait_ge(sem("h2_turned"), upto("h2_turned", m, j))
                    src = PS[:, 2 * (m % 2) + j, :].rearrange("p (a n) -> p a n", a=4)[:, :, 0:TW[m]]
                    g = g2c[:, 4 * j:4 * j + 4].unsqueeze(2).to_broadcast([128, 4, TW[m]])
                    dve.wait_ge(sem("mix_turned"), upto("mix_turned", 4, 1))
                    dve.tensor_tensor(h2T[:, 4 * j:4 * j + 4, token_cols(m)], src, g, ALU.mult).then_inc(
                        sem("h2_ready"), tick("h2_ready", ("h2", m, j)))

            dve.wait_ge(sem("x_back"), upto("x_back"))
            add_x(0)
            for m in range(NTILE):
                mean(dve, m, "x2")
                if m < 4:
                    add_x(m + 1)
                dve.wait_ge(sem("x2_root"), upto("x2_root", m))
                link(dve.reciprocal(small[0:TW[m], 8 + m:9 + m], small[0:TW[m], 8 + m:9 + m]))
                dve.tensor_scalar(x_norm[0:TW[m], m % 2, :], x2[0:TW[m], m, :], small[0:TW[m], 8 + m:9 + m],
                                         None, ALU.mult).then_inc(
                    sem("x_normed"), tick("x_normed", m))
                h2_out(m)
            for s2 in range(2):
                ins = dve.memset(conv_prompt(s2)[:, 0:2], 0.0)
            ins.then_inc(sem("pads_zeroed"), tick("pads_zeroed"))
            dve.wait_ge(sem("conv_w_out"), upto("conv_w_out"))
            for f in range(NF):
                s2, b = f % 2, 3 * (f % 2)
                dve.wait_ge(sem("conv_in_ready"), upto("conv_in_ready", f))
                if f >= 2:
                    dve.wait_ge(sem("sig_ready"), upto("sig_ready", f - 2))
                    dve.wait_ge(last.sem, last.value)
                cp, cs = conv_prompt(s2), conv_sample(s2)
                out_p = conv_sum[:, s2, 0:NP]
                out_s = conv_sum[:, s2, NP:NCOL].rearrange("p (b t) -> p b t", b=NB)
                w = lambda j: conv_w[:, 22 * j + f:22 * j + f + 1]
                dve.tensor_scalar(out_p, cp[:, 0:NP], w(0), w(3), ALU.mult, ALU.add)
                link(dve.tensor_scalar(out_s, cs[:, :, 0:8], w(0), w(3), ALU.mult, ALU.add))
                for j in (1, 2):
                    dve.scalar_tensor_tensor(out=out_p, in0=cp[:, j:j + NP], scalar=w(j), in1=out_p, op0=ALU.mult,
                                             op1=ALU.add)
                    ins = dve.scalar_tensor_tensor(out=out_s, in0=cs[:, :, j:j + 8], scalar=w(j), in1=out_s,
                                                   op0=ALU.mult, op1=ALU.add)
                    ins.then_inc(
                        sem("conv_summed" if j == 2 else "conv_step"),
                        tick("conv_summed" if j == 2 else "conv_step", f))
                    dve.wait_ge(last.sem, last.value)
                dve.wait_ge(sem("sig_ready"), upto("sig_ready", f))
                sg = conv_sig[:, s2, :]
                link(dve.tensor_tensor(sg, sg, conv_sum[:, s2, :], ALU.mult))
                dve.wait_ge(sem("up_done"), upto("up_done", f, 1))
                dve.tensor_tensor(upT[:, f, 0:512], sg[:, 0:512], PS[:, b + 1, :], ALU.mult)
                dve.tensor_tensor(upT[:, f, 512:576], sg[:, NP:NCOL], PS[:, b + 2, 128:192], ALU.mult)
                dve.tensor_tensor(upT[:, f, 576:592], sg[:, 512:NP], PS[:, b + 2, 192:208], ALU.mult).then_inc(
                    sem("gated"), tick("gated", f))
            for n in range(2):
                for m in range(NTILE):
                    dve.wait_ge(sem("y_dots"), upto("y_dots", n, m))
                    x = x2[0:TW[m], m, 512 * n:512 * n + 512]
                    dve.tensor_tensor(x, x, PS[0:TW[m], (5 * n + m) % 8, :], ALU.add).then_inc(
                        sem("y_summed"), tick("y_summed", n, m))
            dve.wait_ge(sem("g_row_in"), upto("g_row_in"))
            for m in range(NTILE):
                mean(dve, m, "y")
                dve.wait_ge(sem("y_root"), upto("y_root", m))
                link(dve.reciprocal(small[0:TW[m], 8 + m:9 + m], small[0:TW[m], 8 + m:9 + m]))
                x = x2[0:TW[m], m, :]
                dve.scalar_tensor_tensor(out=x, in0=x, scalar=small[0:TW[m], 8 + m:9 + m], in1=g_row[0:TW[m]],
                                                op0=ALU.mult, op1=ALU.mult).then_inc(
                    sem("y_ready"), tick("y_ready", m))

        block = ctx.enter_context(nc.Block())

        @block.sync
        def _(sp):
            for n, (dst, src) in enumerate([
                    (ident, I["c_ident"]), (cc64, I["c_cos64"]), (ss64, I["c_sin64"]), (cc32, I["c_cos32"]),
                    (ss32, I["c_sin32"]), (same_t[0:64], I["c_same_t"]), (causal8[0:64], I["c_causal8"]), (quarter, I["c_quarter"]),
                    (g1c, I["norm1_g"].rearrange("a (k p) -> p (a k)", p=128)),
                    (gqc, I["g_q"].rearrange("a (k p) -> p (a k)", p=128)),
                    (g2c, I["norm2_g"].rearrange("a (k p) -> p (a k)", p=128)),
                    (gkv, I["g_kv"][0].partition_broadcast(128))] + [(ptx[:, b:b + 1], bass.AP(I["page_table"].tensor, NPG * b, [[1, NPG], [0, 4]]))
                         for b in range(NB)]):
                sp.dma_start(dst, src, allow_slow_non_contiguous=True).then_inc(
                    sem("consts_in"), tick("consts_in", by=16))
                if n == 0:
                    load_x(sp, 0)
                    load_x(sp, 1)
            sp.dma_start(wuk, I["w_uk"][0].rearrange("(c p) h n -> p c (h n)", p=128)).then_inc(
                sem("wuk_in"), tick("wuk_in", 0, by=16))
            sp.dma_start(wuv, I["w_uv"][0].rearrange("(c p) h n -> p c (h n)", p=128)).then_inc(
                sem("wuv_in"), tick("wuv_in", 0, by=16))
            load_w(sp, "qi")
            load_w(sp, "sm")
            for m in range(2, NTILE):
                sp.wait_ge(sem("h_turned"), upto("h_turned", ("h", m - 2, 1)))
                load_x(sp, m)
            for name, last in (("c0", "qi"), ("c1", "sm"), ("uq", "cq"), ("qb", "cq"), ("kb", "uq"), ("vb", "qb")):
                sp.wait_ge(sem("product"), upto("product", last, 4))
                load_w(sp, name)
            sp_sample(sp)
            sp_prompt(sp)
            sp_merge(sp)

        @block.gpsimd
        def _(gp):
            p, s = slice(0, 128), slice(0, NS)
            for m in range(NTILE):
                gp.wait_ge(sem("ki_roped"), upto("ki_roped", m))
                store_rows(gp, kid[:, m, 0:64], O["new_ik_p"], O["new_ik_s"], m, "ki")
            gp.wait_ge(sem("wi_scaled"), upto("wi_scaled", 4))
            gp.dma_start(scratch["w_i"], w_i[0:NS, 4, :]).then_inc(sem("wi_stored"), tick("wi_stored", 0, by=16))
            gp.wait_ge(sem("wi_stored"), upto("wi_stored", 0))
            for h in range(H):
                gp.dma_start(wcol[8 * h:8 * h + 8, :], bass.AP(scratch["w_i"].tensor, h, [[8, 8], [64, 8]]),
                                    allow_slow_non_contiguous=True).then_inc(
                    sem("wcol_in"), tick("wcol_in", h, by=16))
            gp.wait_ge(sem("h_ready"), upto("h_ready", ("h", NTILE - 1, 1)))
            gp.dma_start(scratch["hT"], flat(hT)).then_inc(sem("h_stored"), tick("h_stored", 0, by=16))
            for m in range(NTILE):
                gp.wait_ge(sem("latent_normed"), upto("latent_normed", m))
                store_rows(gp, lat[:, m, 0:256], O["new_ckv_p"], O["new_ckv_s"], m, "ckv")
                store_rows(gp, lat[:, m, 256:288], O["new_kpe_p"], O["new_kpe_s"], m, "kpe")
            gp.wait_ge(sem("b_roped"), upto("b_roped", "qb", 4))
            gp.dma_start(scratch["q_b"], tok[0:NS, units_tok[("qb", 4)]]).then_inc(
                sem("q_b_stored"), tick("q_b_stored", 0, by=16))
            for kind in ("kb", "vb"):
                for m in range(NTILE):
                    if kind == "kb":
                        gp.wait_ge(sem("b_roped"), upto("b_roped", kind, m))
                        src, names = tok[:, units_tok[(kind, m)]], ("new_k_p", "new_k_s")
                    else:
                        gp.wait_ge(sem("unit_act"), upto("unit_act", kind, m))
                        src, names = vb[:, m, :], ("new_v_p", "new_v_s")
                    store_rows(gp, src, O[names[0]], O[names[1]], m, kind)
            for name in ("ki", "ckv", "kpe", "kb", "vb"):
                wait_stored(gp, name)
                gp.wait_ge(sem(f"stored_{name}_s"), upto(f"stored_{name}_s", 4))
            gp_sample_loads(gp)
            gp_gather(gp)

        @block.scalar
        def _(act):
            for m in range(NTILE):
                r = slice(0, TW[m])
                act.wait_ge(sem(f"x_in{m}"), upto(f"x_in{m}", m))
                act.activation(junk[r, 0:D], x_ring[r, m % 2, :], ACT.Square, accum_out=small[r, m:m + 1]).then_inc(
                    sem("x_squared"), tick("x_squared", m))
                act.wait_ge(sem("x_mean"), upto("x_mean", m))
                act.activation(small[r, 8 + m:9 + m], small[r, m:m + 1], ACT.Sqrt).then_inc(
                    sem("x_root"), tick("x_root", m))
            for i, u in enumerate(units + [None]):
                if u:
                    act_unit(act, u)
                if i:
                    for key, _ in turns_of(units[i - 1]):
                        act_turn(act, key)
            act_index(act)
            act_latent(act)
            act_prompt(act)
            act_sparse(act)
            act_merge(act)

        @block.vector
        def _(dve):
            dve.wait_ge(sem("consts_in"), upto("consts_in"))
            link = linker(S, dve)
            link(dve.tensor_copy(ta[:, 0:NB], ptx))
            link(dve.tensor_scalar(tb[:, 0:NB], ta[:, 0:NB], 4.0, quarter[:, 0:1], ALU.mult, ALU.add))
            dve.tensor_copy(idx_row, tb[:, 0:NB])
            for j in range(4):
                ins = dve.tensor_scalar(idx_ckv[:, :, j], tb[:, 0:NB], 4.0, float(j), ALU.mult, ALU.add)
            ins.then_inc(sem("index_ready"), tick("index_ready"))
            def h_out(m):
                for j in range(2):
                    n = TW[m]
                    dve.wait_ge(sem("h_turned"), upto("h_turned", ("h", m, j)))
                    src = PS[:, turn_bank[("h", m, j)], :].rearrange("p (a n) -> p a n", a=4)[:, :, 0:n]
                    g = g1c[:, 4 * j:4 * j + 4].unsqueeze(2).to_broadcast([128, 4, n])
                    dve.tensor_tensor(hT[:, 4 * j:4 * j + 4, token_cols(m)], src, g, ALU.mult).then_inc(
                        sem("h_ready"), tick("h_ready", ("h", m, j)))
            for m in range(NTILE):
                r = slice(0, TW[m])
                dve.wait_ge(sem("x_squared"), upto("x_squared", m))
                dve.tensor_scalar(small[r, m:m + 1], small[r, m:m + 1], 1.0 / D, EPS, ALU.mult, ALU.add).then_inc(
                    sem("x_mean"), tick("x_mean", m))
                if m:
                    h_out(m - 1)
                dve.wait_ge(sem("x_root"), upto("x_root", m))
                link(dve.reciprocal(small[r, 8 + m:9 + m], small[r, 8 + m:9 + m]))
                dve.tensor_scalar(x_ring[r, m % 2, :], x_ring[r, m % 2, :], small[r, 8 + m:9 + m], None,
                                         ALU.mult).then_inc(
                    sem("x_scaled"), tick("x_scaled", m))
            h_out(NTILE - 1)
            for u in units:
                dve_unit(dve, link, u)
            dve_index(dve)
            dve_latent(dve, link)
            dve_prompt(dve, link)
            dve_sparse(dve, link)
            dve_merge(dve, link)

        @block.tensor
        def _(pe):
            pe.wait_ge(sem("consts_in"), upto("consts_in"))

            def turn(key, srcs, name="turned"):
                if turn_before[key]:
                    p = turn_before[key]
                    pe.wait_ge(sem("h_ready"), upto("h_ready", p)) if p[0] == "h" else pe.wait_ge(sem("turned_act"), upto("turned_act", *p))
                bank = PS[:, turn_bank[key], :].rearrange("p (a n) -> p a n", a=4)
                for i, s in enumerate(srcs):
                    n, w = s.shape
                    ins = pe.transpose(bank[0:w, i, 0:n], s, ident[0:n, 0:n])
                ins.then_inc(sem(name), tick(name, *(key if name == "turned" else (key,))))

            for m in range(NTILE):
                pe.wait_ge(sem("x_scaled"), upto("x_scaled", m))
                for j in range(2):
                    x = x_ring[0:TW[m], m % 2, :]
                    turn(("h", m, j), [x[:, 128 * k:128 * k + 128] for k in range(4 * j, 4 * j + 4)], "h_turned")
            for i, u in enumerate(units + [None]):
                if u:
                    pe_unit(pe, u)
                if i:
                    v = units[i - 1]
                    if turns_of(v):
                        if v[0] in ("qi", "qb", "kb"):
                            pe.wait_ge(sem("b_roped"), upto("b_roped", *v))
                        elif v[0] == "cq":
                            pe.wait_ge(sem("latent_normed"), upto("latent_normed", v[1]))
                            pe.wait_ge(sem("unit_dve"), upto("unit_dve", "sm", v[1]))
                        elif v[0] == "uq":
                            pe.wait_ge(sem("q_roped"), upto("q_roped", v[1], 1))
                        else:
                            pe.wait_ge(sem("wuk_in"), upto("wuk_in", 0))
                    for key, srcs in turns_of(v):
                        if key in (("qi", 4, 1), ("uq", 4, 2)):
                            pe.wait_ge(sem("dup_ready"), upto("dup_ready", v[0]))
                        turn(key, srcs)
            pe_index(pe)
            pe_latent(pe)
            pe_prompt(pe)
            pe_sparse(pe)
            pe_merge(pe)

    return S.now


def linker(S, eng):
    def link(ins):
        ins.then_inc(S.sem("chain_dve"), S.tick("chain_dve"))
        eng.wait_ge(S.last.sem, S.last.value)
    return link


def flat(v):
    return v.rearrange("p a b -> p (a b)")


def rows2(v):
    return v if len(v.shape) == 2 else v.rearrange("l h d -> l (h d)")


def rows3(v):
    return v.rearrange("b t c -> (b t) c") if len(v.shape) == 3 else v.rearrange("b t h d -> (b t) (h d)")


_OUTS = {
    "y_prompt": (1, 512, D), "y_sample": (NB, NT, D),
    "new_ckv_p": (1, 1, NP, KVL), "new_kpe_p": (1, 1, NP, PE_), "new_k_p": (1, 1, NP, H, HD),
    "new_v_p": (1, 1, NP, H, HD), "new_ik_p": (1, 1, NP, HD), "new_conv_p": (1, 1, 2, FF),
    "new_ckv_s": (1, NB, NT, KVL), "new_kpe_s": (1, NB, NT, PE_), "new_k_s": (1, NB, NT, H, HD),
    "new_v_s": (1, NB, NT, H, HD), "new_ik_s": (1, NB, NT, HD), "new_conv_s": (1, NB, 2, FF)}
_SCRATCH = {"w_i": (NS, 8), "q_b": (NS, 512), "hT": (128, KD * NCOL)}


def constants():
    pos = np.zeros((5, 128))
    for m in range(4):
        pos[m] = np.arange(128) + 128 * m
    pos[4, 0:NS] = PAST + np.arange(NS) % NT
    pos[4, NS:NS + 16] = 512 + np.arange(16)
    out = {"c_ident": np.eye(128, dtype=np.float32),
           "c_same_t": np.tile(np.eye(8), (8, 1)).astype(np.float32),
           "c_causal8": np.tile(np.where(np.tri(8) > 0, 0.0, NEG), (8, 1)).astype(np.float32),
           "c_wide_tri": np.concatenate([np.zeros((128, 512)), np.where(np.tri(128) > 0, 0.0, NEG)],
                                        1).astype(np.float32),
           "c_same_b": np.repeat(np.eye(8), 8, 0).astype(np.float32),
           "c_quarter": (np.arange(128) % 4).astype(np.float32)[:, None]}
    for w in (64, 32):
        half = w // 2
        freq = np.float32(1.0) / np.power(10000.0, np.arange(half) / half).astype(np.float32)
        ang = (pos.astype(np.float32)[:, :, None] * freq).astype(np.float32)
        cos, sin = np.cos(ang), np.sin(ang)
        out[f"c_cos{w}"] = np.concatenate([cos, cos], -1).transpose(1, 0, 2).astype(np.float32).copy()
        out[f"c_sin{w}"] = np.concatenate([-sin, sin], -1).transpose(1, 0, 2).astype(np.float32).copy()
    return out


_INS = ["x_prompt", "x_sample", "cache_mla_ckv", "cache_mla_kpe", "cache_dsa_k", "cache_dsa_v", "cache_idx_k",
        "state_ffn_conv", "page_table", "meta_tokens", "norm1_g", "w_in", "g_q", "g_kv", "w_uq", "w_uk", "w_uv",
        "w_br_a", "w_br_b", "w_o", "norm2_g", "w_ffn_g", "w_ffn_u", "ffn_conv_w", "ffn_conv_b", "w_ffn_d", "final_g"]


def build(nc, arrays, events):
    I = {n: nc.dram_tensor("in_" + n, a.shape, mybir.dt.from_np(a.dtype), kind="ExternalInput").ap()
         for n, a in arrays.items()}
    O = {n: nc.dram_tensor("out_" + n, s, F32, kind="ExternalOutput").ap() for n, s in _OUTS.items()}
    scratch = {n: nc.dram_tensor("tmp_" + n, s, F32).ap() for n, s in _SCRATCH.items()}
    return trunk(nc, I, O, scratch, events)


def kernel(**inputs):
    import concourse.bacc as _bacc
    from concourse.bass_utils import run_bass_kernel_spmd as _run

    arrays = {n: np.ascontiguousarray(inputs[n]) for n in _INS}
    arrays.update(constants())
    events = build(_bacc.Bacc("TRN2", target_bir_lowering=False, num_devices=1), arrays, None)
    nc = _bacc.Bacc("TRN2", target_bir_lowering=False, num_devices=1)
    build(nc, arrays, events)
    r = _run(nc, [{"in_" + n: a for n, a in arrays.items()}], core_ids=[0])
    return tuple(r.results[0]["out_" + n] for n in _OUTS)
```

```python
from contextlib import ExitStack

import numpy as np
import concourse.bass as bass
import concourse.mybir as mybir

F32 = mybir.dt.float32
I32 = mybir.dt.int32
U32 = mybir.dt.uint32
ACT = mybir.ActivationFunctionType
ALU = mybir.AluOpType
AX = mybir.AxisListType

D = 1024
KD = D // 128
NP = 528
NM = 16
NB = 8
NT = 8
NS = NB * NT
H = 8
PAST = 4096
PAGE = 128
NPG = PAST // PAGE
QL, KVL, PE_, HD = 768, 256, 32, 64
FF = 2816
NF = FF // 128
EPS = 1e-6
NEG = -1e30
TAKEN = -3e38
DUMMY = 3e38
MLA_SCALE = 96.0 ** -0.5
DSA_SCALE = 64.0 ** -0.5
TOPK_P = 132
TOPK_S = 256
NTILE = 5
TW = [128, 128, 128, 128, 80]
NCOL = 592
LAST = 576
C_CQ, C_CKV, C_KPE, C_QB, C_KB, C_VB, C_QI, C_KI, C_WI, C_GA, C_GB = (
    0, 768, 1024, 1056, 1568, 2080, 2592, 3104, 3168, 3176, 4200)


SHARED = {name: sem for sem, names in {
    "turned": "h_turned sturned pturned mix_turned h2_turned conv_w_turned state_turned conv_turned dots_turned "
              "v_turned "
              "sel_turned rows_turned",
    "product": "keysT_used piece_used index_dots latent_dots scored_p gate_dots branch_dots out_dots up_done y_dots new_dots",
    "turn_out": "turned_act sturn_out pturn_out mix_turn_out sel_out state_out conv_turned_out conv_w_out "
                "row_no_ready o_s_out v_sums_out",
    "squared": "x_squared c_squared x2_squared y_squared",
    "root": "x_root c_root x2_root y_root",
    "exped": "exped_p sel_exped",
    "mean": "x_mean c_mean x2_mean y_mean",
    "h_ready": "h2_ready",
    "chain_dve": "picks_done",
    "o_b_out": "o_b_ready",
    "x_scaled": "x_normed",
}.items() for name in names.split()}


class Signals:

    def __init__(self, nc, ctx, values):
        self.nc, self.ctx, self.values = nc, ctx, values
        self.sems, self.count, self.now = {}, {}, {}
        self.last = Last()

    def sem(self, signal):
        name = SHARED.get(signal, signal)
        if name not in self.sems:
            self.sems[name] = self.ctx.enter_context(self.nc.semaphore(name))
        return self.sems[name]

    def tick(self, signal, *key, by=1):
        name = SHARED.get(signal, signal)
        self.count[name] = self.count.get(name, 0) + by
        assert (signal, *key) not in self.now or not key, (signal, key)
        self.now[(signal, *key)] = self.count[name]
        self.last.sem, self.last.value = self.sem(signal), self.count[name]
        return by

    def upto(self, signal, *key):
        return 1 if self.values is None else self.values[(signal, *key)]

    def same(self, key, event):
        assert SHARED.get(key[0], key[0]) == SHARED.get(event[0], event[0])
        self.now[key] = self.now[event]


class Last:
    pass


class Region:

    def __init__(self, mem, start, end):
        self.mem, self.at, self.end = mem, start, end

    def take(self, *shape, dtype=F32):
        n = int(np.prod(shape))
        assert self.at + n <= self.end, ("SBUF", shape, self.at + n - self.end)
        v = self.mem[:, self.at:self.at + n]
        self.at += n
        if dtype is not F32:
            v = v.bitcast(dtype)
        if len(shape) == 2:
            v = v.rearrange("p (a b) -> p a b", a=shape[0])
        elif len(shape) == 3:
            v = v.rearrange("p (a b c) -> p a b c", a=shape[0], b=shape[1])
        elif len(shape) == 4:
            v = v.rearrange("p (a b c d) -> p a b c d", a=shape[0], b=shape[1], c=shape[2])
        return v


def token_cols(m):
    return slice(128 * m, 128 * m + TW[m])


def trunk(nc, I, O, scratch, events):
    ctx = ExitStack()
    with ctx:
        S = Signals(nc, ctx, events)
        sem, tick, upto, same, last = S.sem, S.tick, S.upto, S.same, S.last
        mem = ctx.enter_context(nc.sbuf_tensor("mem", [128, 53200], F32))
        PS = ctx.enter_context(nc.psum_tensor("PS", [128, 8, 512], F32))

        K = Region(mem, 0, 31000)
        ident = K.take(128)
        cc64, ss64 = K.take(5, 64), K.take(5, 64)
        cc32, ss32 = K.take(5, 32), K.take(5, 32)
        same_t = K.take(8)
        quarter = K.take(1)
        g1c = K.take(KD)
        gqc = K.take(6)
        g2c = K.take(KD)
        w_i = K.take(5, 8)
        wcol = K.take(NB)
        ptx = K.take(NB, dtype=I32)
        idx_row = K.take(NB, dtype=U32)
        idx_ckv = K.take(NB, 4, dtype=U32)
        small = K.take(64)
        wuv = K.take(2, 512)
        heads_at = K.at
        qT, kT, vm = K.take(H, NCOL), K.take(H, NP), K.take(5, 512)
        lent_end = K.at
        qiT, kiT = K.take(4, NCOL), K.take(NCOL)
        qb_at = K.at
        qbT, kbT, vb = K.take(4, NCOL), K.take(4, NCOL), K.take(5, 512)
        ql_s, qpe_s, qi_s = K.take(2, 512), K.take(512), K.take(512)
        ckv_new = K.take(2, NS)
        kpe_new = K.take(NS)
        oT_s = K.take(4, NS)
        picked = K.take(TOPK_S, dtype=U32)
        picked_at = K.take(TOPK_S)
        picked_up = K.take(TOPK_S, dtype=U32)
        picked_at_up = K.take(TOPK_S)
        causal8 = K.take(8)
        pages_q = K.take(NPG, dtype=I32)
        same_b = K.take(8)
        A = Region(mem, K.at, 53200)
        hT = A.take(KD, NCOL)
        ckvT = A.take(2, NCOL)
        w_ring = A.take(2, 4608)
        cq = A.take(2, QL)
        lat = A.take(5, 288)
        q_tok = A.take(2, QL)
        kid = A.take(5, 128)
        tok = A.take(3, 512)
        ta, tb = A.take(512), A.take(512)
        gkv = A.take(KVL)
        wuk = A.take(2, 512)
        T = Region(mem, 53200 - TOPK_S - 64, 53200)
        slot_bias = T.take(TOPK_S)
        new_bias = T.take(8, 8)
        C = Region(mem, K.at, 53200 - TOPK_S - 64)
        C2 = Region(mem, heads_at, lent_end)
        raw = C.take(5, 2048)
        raw_more = C2.take(3, 2048)
        kpe_raw = C.take(1024)
        row_scores = [C.take(PAST + NT), C2.take(PAST + NT)]
        picks_at = C.at
        pick_scores = C.take((PAST + NT) // 2)
        R = Region(mem, picks_at, C.at)
        low, up, keep, page_f, off_f = (R.take(TOPK_S) for _ in range(5))
        offset = R.take(TOPK_S, dtype=U32)
        pages_f = R.take(NPG)
        new_hit = R.take(8)
        keysT = C.take(4, 512)
        kpeT = [C.take(8, 128), C2.take(8, 128)]
        probsT = C.take(33, 64)
        lat_new = C.take(2, KVL)
        qpe_z = C.take(2, 4, 64)
        o_lat = C.take(2, 512)
        chunk_max = C.take(2, 9)
        col = C.take(2, 4)
        o_rows = C.take(KVL)
        relu_i = flat(probsT)[:, 0:1024].rearrange("p (a b) -> p a b", a=2)
        qi_2 = flat(probsT)[:, 1024:2048].rearrange("p (b n) -> p b n", b=NB)
        wb = flat(lat_new)[:, 0:NB * 40].rearrange("p (b n) -> p b n", b=NB)

        P = Region(mem, K.at, 53200 - TOPK_S - 64)
        oT_a, oT_b = P.take(4, NCOL), P.take(4, NCOL)
        wide_tri = P.take(640)
        score_acc = P.take(4 + NP)
        mask_s = P.take(NP)
        probs = P.take(3, NP)
        probs_T = P.take(2, 640)
        relu_p = P.take(2, NP)
        o_tok = P.take(2, 512)
        vb_last = P.take(512)
        wi_last = P.take(8)
        stat = P.take(6, 4)
        top8_p = P.take(8)
        rows_at = P.at
        rows = P.take(5, 1024)
        q_wide = P.take(2, 512)
        prod = P.take(1024)
        v_sums = prod[:, 512:1024]
        dots_k = P.take(16, 64)
        s_sel = P.take(H, TOPK_S + NS)
        p_sel = P.take(2, 64, 8)
        p_new = P.take(8, 64)
        page, phys, hit = picked_up, picked_at, picked_at_up
        row_no = P.take(2, 64, dtype=U32)
        head_max, head_sum = P.take(8), P.take(8)

        F1 = Region(mem, heads_at, K.at)
        F2 = Region(mem, K.at + 2 * 4 * NCOL, 53200)
        w_slots = F1.take(6, 2048)
        hT_f = mem[:, heads_at + 8192:heads_at + 8192 + KD * NCOL].rearrange("p (a b) -> p a b", a=KD)
        F1.take(8192 + KD * NCOL - 6 * 2048)
        o_mix = F1.take(5, D)
        h2T = flat(o_mix)[:, 0:KD * NCOL].rearrange("p (a b) -> p a b", a=KD)
        x2 = F1.take(5, D)
        hT_at = F2.at
        F2.take(KD, NCOL)
        up_at = F2.at
        upT = F2.take(NF, NCOL)
        branch_w = [[mem[:, hT_at + 2048 * i:hT_at + 2048 * i + 2048] for i in range(2)],
                    [mem[:, up_at:up_at + 2048], F1.take(2048)]]
        conv_state = F2.take(FF)
        o_mixT = mem[:, rows_at:rows_at + KD * NCOL].rearrange("p (a b) -> p a b", a=KD)
        gates = flat(s_sel)[:, 0:2048].rearrange("p (a b) -> p a b", a=4)
        gates_last = [v.rearrange("p (b c) -> p b c", b=2) for v in (flat(q_wide), flat(dots_k))]
        F4 = Region(mem, hT_at, hT_at + KD * NCOL)
        conv_in, conv_sum, conv_sig = F4.take(2, 610), F4.take(2, NCOL), F4.take(2, NCOL)
        g_row = F4.take(D)
        x_norm = mem[:, hT_at:hT_at + 2048].rearrange("p (a b) -> p a b", a=2)
        conv_out = mem[:, K.at:K.at + FF]
        conv_w = mem[:, K.at + FF:K.at + FF + 88]
        conv_rows = mem[:, K.at + FF + 96:K.at + FF + 96 + 128]
        last_two = mem[:, K.at + FF + 256:K.at + FF + 256 + 36].rearrange("p (a b) -> p a b", a=2)

        x_ring = flat(qT)[:, 0:2048].rearrange("p (a b) -> p a b", a=2)
        cqT = mem[:, qb_at:qb_at + 6 * NCOL].rearrange("p (a b) -> p a b", a=6)
        junk = flat(vm)[:, 0:1024]
        dup = flat(vm)[:, 1024:2048].rearrange("p (a b) -> p a b", a=8)
        wukT = flat(vb)[:, 0:2048].rearrange("p (a b) -> p a b", a=8)

        units = [(k, m) for k in ("qi", "sm", "cq", "uq") for m in range(NTILE)]
        units += [("wt", 0)] + [("kn", h) for h in range(H)] + [("kl", 0), ("ql", 0), ("ql", 1)]
        units += [(k, m) for k in ("vm", "qb", "kb", "vb") for m in range(NTILE)]
        chunk_at = {"qi": (C_QI, 512), "qb": (C_QB, 512), "kb": (C_KB, 512), "vb": (C_VB, 512)}
        slot_of = {"qi": 0, "sm": 1, "c0": 0, "c1": 1, "uq": 0, "qb": 1, "kb": 0, "vb": 1}
        banks, before = {}, {}
        user, n = [None] * 4, 0
        for u in units:
            banks[u], before[u] = [], []
            for _ in range({"cq": 2, "uq": 2, "wt": 0}.get(u[0], 1)):
                banks[u].append(n % 4)
                before[u].append(user[n % 4])
                user[n % 4] = u
                n += 1

        def turns_of(u):
            kind, m = u
            if kind not in ("qi", "cq", "uq", "wt", "qb", "kb"):
                return []
            r = slice(0, TW[m])
            if kind in ("qi", "qb", "kb"):
                t = tok[:, units_tok[u]]
                out = [((kind, m, 0), [(t[r, 128 * i:128 * i + 128]) for i in range(4)])]
                if u == ("qi", 4):
                    out += [((kind, m, 1 + j), [dup[0:NS, 4 * j + i, :] for i in range(4)]) for j in range(2)]
                return out
            if kind == "cq":
                c = cq[:, m % 2]
                l4 = [lat[r, m, 0:128], lat[r, m, 128:256], lat[r, m, 192:288], kid[r, m, :]]
                out = [((kind, m, 0), [c[r, 128 * i:128 * i + 128] for i in range(4)]),
                       ((kind, m, 1), [c[r, 128 * i:128 * i + 128] for i in range(4, 6)]),
                       ((kind, m, 2), l4)]
                if m == 4:
                    out.append(((kind, m, 3), [lat[0:NS, m, 256:288]]))
                return out
            if kind == "uq":
                q = q_tok[:, m % 2].rearrange("p (h n) -> p h n", h=H)
                out = [((kind, m, j), [q[r, 4 * j + i, :] for i in range(4)]) for j in range(2)]
                if m == 4:
                    out += [((kind, m, 2 + j), [dup[0:NS, 4 * j + i, :] for i in range(4)]) for j in range(2)]
                return out
            return [((kind, m, j), [wuk[:, c, 64 * h:64 * h + 64] for h in (2 * j, 2 * j + 1) for c in range(2)])
                    for j in range(4)]

        units_tok = {u: i % 3 for i, u in enumerate([u for u in units if u[0] in ("qi", "qb", "kb")])}
        tok_before = {}
        for i, u in enumerate([u for u in units if u[0] in ("qi", "qb", "kb")]):
            tok_before[u] = [v for v in units_tok if units_tok[v] == i % 3][i // 3 - 1] if i >= 3 else None
        turns = [(("h", m, j), None) for m in range(NTILE) for j in range(2)]
        for u in units:
            turns += turns_of(u)
        turn_bank = {key: 4 + i % 4 for i, (key, _) in enumerate(turns)}
        turn_before = {key: turns[i - 4][0] if i >= 4 else None for i, (key, _) in enumerate(turns)}

        def load_x(sp, m):
            dst = x_ring[:, m % 2, :]
            if m == 0:
                sp.dma_start(dst[0:NM], I["meta_tokens"]).then_inc(sem(f"x_in{m}"), tick(f"x_in{m}", by=16))
                sp.dma_start(dst[NM:128], I["x_prompt"][0, 0:128 - NM, :]).then_inc(
                    sem(f"x_in{m}"), tick(f"x_in{m}", m, by=16))
            elif m < 4:
                sp.dma_start(dst, I["x_prompt"][0, 128 * m - NM:128 * m + 128 - NM, :]).then_inc(
                    sem(f"x_in{m}"), tick(f"x_in{m}", m, by=16))
            else:
                sp.dma_start(dst[0:NS], I["x_sample"].rearrange("b t d -> (b t) d")).then_inc(
                    sem(f"x_in{m}"), tick(f"x_in{m}", by=16))
                sp.dma_start(dst[NS:NS + 16], I["x_prompt"][0, 512 - NM:528 - NM, :]).then_inc(
                    sem(f"x_in{m}"), tick(f"x_in{m}", m, by=16))

        def w_view(name):
            flat_slot = w_ring[:, slot_of[name], :]
            if name == "uq":
                return flat_slot.rearrange("p (k n) -> p k n", k=6)
            if name == "sm":
                return flat_slot[:, 0:KD * 104].rearrange("p (k n) -> p k n", k=KD)
            return flat_slot[:, 0:KD * 512].rearrange("p (k n) -> p k n", k=KD)

        def load_w(sp, name):
            w = I["w_in"][0].rearrange("(k p) n -> p k n", p=128)
            dst = w_view(name)
            if name == "uq":
                sp.dma_start(dst, I["w_uq"][0].rearrange("(k p) h n -> p k (h n)", p=128)).then_inc(
                    sem("w_uq_in"), tick("w_uq_in", name, by=16))
            elif name == "sm":
                sp.dma_start(dst[:, :, 0:32], w[:, :, C_KPE:C_KPE + 32]).then_inc(
                    sem("w_sm_in"), tick("w_sm_in", by=16))
                sp.dma_start(dst[:, :, 32:104], w[:, :, C_KI:C_KI + 72]).then_inc(
                    sem("w_sm_in"), tick("w_sm_in", name, by=16))
            else:
                at = {"c0": 0, "c1": 512}.get(name)
                at = chunk_at[name][0] if at is None else at
                sp.dma_start(dst, w[:, :, at:at + 512]).then_inc(sem(f"w_{name}_in"), tick(f"w_{name}_in", name, by=16))

        def store_rows(gp, src, to_p, to_s, m, name):
            tp = rows2(to_p[0, 0])
            if m < 4:
                gp.dma_start(tp[128 * m:128 * m + 128, :], src).then_inc(
                    sem(f"stored_{name}_p" + (str(m) if name == "kb" else "")),
                    tick(f"stored_{name}_p" + (str(m) if name == "kb" else ""), m, by=16))
            else:
                gp.dma_start(tp[512:528, :], src[NS:NS + 16]).then_inc(
                    sem(f"stored_{name}_p" + (str(m) if name == "kb" else "")),
                    tick(f"stored_{name}_p" + (str(m) if name == "kb" else ""), m, by=16))
                gp.dma_start(rows3(to_s[0]), src[0:NS]).then_inc(sem(f"stored_{name}_s"), tick(f"stored_{name}_s", m, by=16))

        def act_unit(act, u):
            kind, m = u
            if kind in ("qi", "uq", "qb", "kb", "wt"):
                return
            b = banks[u]
            act.wait_ge(sem("product"), upto("product", *u))
            if kind == "sm":
                r = slice(0, TW[m])
                ins = act.activation(w_i[r, m, :], PS[r, b[0], 96:104], ACT.Copy, scale=8.0 ** -0.5)
                ins.then_inc(sem("wi_scaled"), tick("wi_scaled", m))
            elif kind == "cq":
                r = slice(0, TW[m])
                act.activation(junk[r, 0:512], PS[r, b[0], :], ACT.Square, accum_out=small[r, 16 + m:17 + m])
                act.activation(junk[r, 512:768], PS[r, b[1], 0:256], ACT.Square, accum_out=small[r, 24 + m:25 + m])
                act.activation(junk[r, 768:1024], PS[r, b[1], 256:512], ACT.Square,
                                      accum_out=small[r, 32 + 2 * m:33 + 2 * m]).then_inc(
                    sem("c_squared"), tick("c_squared", m))
                act.wait_ge(sem("c_mean"), upto("c_mean", m))
                act.activation(small[r, 32 + 2 * m:34 + 2 * m], small[r, 32 + 2 * m:34 + 2 * m], ACT.Sqrt).then_inc(
                    sem("c_root"), tick("c_root", m))
            elif kind == "kn":
                act.copy(kT[0:64, m, 0:512], PS[0:64, b[0], :]).then_inc(sem("unit_act"), tick("unit_act", *u))
            elif kind == "kl":
                act.copy(kT[0:64, :, 512:528], PS[0:64, b[0], 0:128].rearrange("p (h n) -> p h n", h=H)).then_inc(
                    sem("unit_act"), tick("unit_act", *u))
            elif kind == "ql":
                act.copy(ql_s[:, m, :].rearrange("p (b h t) -> p h b t", b=NB, h=H),
                                PS[:, b[0], :].rearrange("p (h b t) -> p h b t", h=H, b=NB)).then_inc(
                    sem("unit_act"), tick("unit_act", *u))
            elif kind == "vm":
                r = slice(0, 128 if m < 4 else 16)
                act.copy(vm[r, m, :], PS[r, b[0], :]).then_inc(sem("unit_act"), tick("unit_act", *u))
            elif kind == "vb":
                r = slice(0, TW[m])
                act.copy(vb[r, m, :], PS[r, b[0], :]).then_inc(sem("unit_act"), tick("unit_act", *u))

        def act_turn(act, key):
            kind, m, j = key
            n = TW[m]
            src = PS[:, turn_bank[key], :].rearrange("p (a n) -> p a n", a=4)
            cols = token_cols(m)
            bht = lambda v: v.rearrange("p (b h t) -> p h b t", b=NB, h=H)[:, 4 * jj:4 * jj + 4]
            from_hbt = lambda v: v.rearrange("p a (b t) -> p a b t", b=NB)
            act.wait_ge(sem("turned"), upto("turned", *key))
            if kind in ("qi", "qb", "kb") and j == 0:
                dst = {"qi": qiT, "qb": qbT, "kb": kbT}[kind]
                ins = act.copy(dst[:, :, cols], src[:, :, 0:n])
            elif kind == "qi":
                jj = j - 1
                ins = act.copy(bht(qi_s), from_hbt(src[:, :, 0:NS]))
            elif kind == "cq" and j < 2:
                for i in range(4 if j == 0 else 2):
                    k = 4 * j + i
                    ins = act.activation(cqT[:, k, cols], src[:, i, 0:n], ACT.Copy, scale=gqc[:, k:k + 1])
            elif kind == "cq" and j == 2:
                act.copy(ckvT[:, :, cols], src[:, 0:2, 0:n])
                act.copy(kiT[:, cols], src[:, 3, 0:n])
                if m == 4:
                    act.copy(ckv_new, src[:, 0:2, 0:NS])
                a, b, c = (0, 128, 128 * m) if m < 4 else (NS, NS + 16, 512)
                ins = act.copy(kT[64:96, :, c:c + b - a], src[64:96, 2, a:b].unsqueeze(1).to_broadcast([32, H, b - a]))
            elif kind == "cq":
                ins = act.copy(kpe_new[0:32, :], src[0:32, 0, 0:NS])
            elif kind == "uq" and j < 2:
                ins = act.copy(qT[0:96, 4 * j:4 * j + 4, cols], src[0:96, :, 0:n])
            elif kind == "uq":
                jj = j - 2
                ins = act.copy(bht(qpe_s), from_hbt(src[:, :, 0:NS]))
            elif kind == "wt":
                ins = act.copy(wukT[0:64, 2 * j:2 * j + 2, :].rearrange("p h (c n) -> p (h c) n", c=2), src[0:64, :, :])
            ins.then_inc(sem("turned_act"), tick("turned_act", *key))

        def rope(dve, link, dst, src, cos, sin, half):
            n, h, w = src.shape
            a = ta[0:n, 0:h * w].rearrange("p (h w) -> p h w", h=h)
            b = tb[0:n, 0:h * w].rearrange("p (h w) -> p h w", h=h)
            wide = lambda t: t.unsqueeze(1).to_broadcast([n, h, t.shape[1]])
            dve.wait_ge(last.sem, last.value)
            dve.tensor_tensor(a, src, wide(cos[0:n]), ALU.mult)
            dve.tensor_tensor(b[:, :, 0:half], src[:, :, half:w], wide(sin[0:n, 0:half]), ALU.mult)
            link(dve.tensor_tensor(b[:, :, half:w], src[:, :, 0:half], wide(sin[0:n, half:w]), ALU.mult))
            return dve.tensor_tensor(dst, a, b, ALU.add)

        def dve_unit(dve, link, u):
            kind, m = u
            if kind in ("kn", "kl", "ql", "vm", "vb", "wt"):
                return
            r, n = slice(0, TW[m]), TW[m]
            b = banks[u]
            heads = lambda v: v.rearrange("p (h n) -> p h n", h=H)
            dve.wait_ge(sem("product"), upto("product", *u))
            if kind in ("qi", "qb", "kb"):
                t = tok[:, units_tok[u]]
                if tok_before[u]:
                    dve.wait_ge(sem("turned"), upto("turned", *tok_before[u], 0))
                    if tok_before[u] == ("qb", 4):
                        dve.wait_ge(sem("q_b_stored"), upto("q_b_stored", 0))
                    if tok_before[u][0] == "kb":
                        dve.wait_ge(sem(f"stored_kb_p{tok_before[u][1]}"), upto(f"stored_kb_p{tok_before[u][1]}", tok_before[u][1]))
                rope(dve, link, heads(t[r]), heads(PS[r, b[0], :]), cc64[:, m], ss64[:, m], 32).then_inc(
                    sem("b_roped"), tick("b_roped", *u))
                if u == ("qi", 4):
                    dve.wait_ge(sem("b_roped"), upto("b_roped", *u))
                    q = heads(t[0:NS]).unsqueeze(2).to_broadcast([NS, H, 2, 64])
                    dve.tensor_copy(dup[0:NS].rearrange("p h (a n) -> p h a n", a=2), q).then_inc(
                        sem("dup_ready"), tick("dup_ready", "qi"))
            elif kind == "sm":
                one = lambda v: v.unsqueeze(1)
                dve.wait_ge(sem("wi_scaled"), upto("wi_scaled", m))
                link(rope(dve, link, one(kid[r, m, 0:64]), one(PS[r, b[0], 32:96]), cc64[:, m], ss64[:, m], 32))
                dve.tensor_copy(kid[r, m, 64:128], kid[r, m, 0:64]).then_inc(
                    sem("ki_roped"), tick("ki_roped", m))
                rope(dve, link, one(lat[r, m, 256:288]), one(PS[r, b[0], 0:32]), cc32[:, m], ss32[:, m], 16).then_inc(
                    sem("unit_dve"), tick("unit_dve", *u))
            elif kind == "cq":
                dve.wait_ge(sem("c_squared"), upto("c_squared", m))
                link(dve.tensor_tensor(small[r, 16 + m:17 + m], small[r, 16 + m:17 + m], small[r, 24 + m:25 + m],
                                       ALU.add))
                dve.tensor_scalar(small[r, 33 + 2 * m:34 + 2 * m], small[r, 16 + m:17 + m], 1.0 / QL, EPS,
                                  ALU.mult, ALU.add)
                dve.tensor_scalar(small[r, 32 + 2 * m:33 + 2 * m], small[r, 32 + 2 * m:33 + 2 * m], 1.0 / KVL,
                                         EPS, ALU.mult, ALU.add).then_inc(
                    sem("c_mean"), tick("c_mean", m))
                dve.wait_ge(sem("c_root"), upto("c_root", m))
                link(dve.reciprocal(small[r, 32 + 2 * m:34 + 2 * m], small[r, 32 + 2 * m:34 + 2 * m]))
                if m >= 2:
                    dve.wait_ge(sem("turned"), upto("turned", "cq", m - 2, 1))
                rq, rk = small[r, 33 + 2 * m:34 + 2 * m], small[r, 32 + 2 * m:33 + 2 * m]
                dve.tensor_scalar(cq[r, m % 2, 0:512], PS[r, b[0], :], rq, None, ALU.mult)
                dve.tensor_scalar(cq[r, m % 2, 512:768], PS[r, b[1], 0:256], rq, None, ALU.mult)
                dve.scalar_tensor_tensor(out=lat[r, m, 0:256], in0=PS[r, b[1], 256:512], scalar=rk,
                                                in1=gkv[r, :], op0=ALU.mult, op1=ALU.mult).then_inc(
                    sem("latent_normed"), tick("latent_normed", m))
            elif kind == "uq":
                if m >= 2:
                    dve.wait_ge(sem("turned"), upto("turned", "uq", m - 2, 1))
                q = heads(q_tok[:, m % 2])
                for j in range(2):
                    src = PS[r, b[j], 0:384].rearrange("p (h n) -> p h n", h=4)
                    dve.tensor_copy(q[r, 4 * j:4 * j + 4, 0:64], src[:, :, 0:64])
                    ins = rope(dve, link, q[r, 4 * j:4 * j + 4, 64:96], src[:, :, 64:96], cc32[:, m], ss32[:, m], 16)
                    ins.then_inc(sem("q_roped"), tick("q_roped", m, j))
                if m == 4:
                    dve.wait_ge(sem("q_roped"), upto("q_roped", m, 1))
                    dve.wait_ge(sem("turned"), upto("turned", "qi", 4, 2))
                    dve.tensor_copy(dup[0:NS].rearrange("p h (a n) -> p h a n", a=4),
                                           q[0:NS, :, 64:96].unsqueeze(2).to_broadcast([NS, H, 4, 32])).then_inc(
                        sem("dup_ready"), tick("dup_ready", "uq"))

        def wait_unit_read(pe, u):
            kind, m = u
            if kind in ("qi", "qb", "kb"):
                pe.wait_ge(sem("b_roped"), upto("b_roped", *u))
            elif kind == "sm":
                pe.wait_ge(sem("unit_dve"), upto("unit_dve", *u))
                pe.wait_ge(sem("wi_scaled"), upto("wi_scaled", m))
            elif kind == "cq":
                pe.wait_ge(sem("latent_normed"), upto("latent_normed", m))
            elif kind == "uq":
                pe.wait_ge(sem("q_roped"), upto("q_roped", m, 1))
            else:
                pe.wait_ge(sem("unit_act"), upto("unit_act", *u))

        def pe_unit(pe, u):
            kind, m = u
            for v in before[u]:
                if v:
                    wait_unit_read(pe, v)
            b = banks[u]
            cols = token_cols(m) if kind not in ("kn", "kl", "ql", "wt") else None
            n = TW[m] if cols else 0

            def groups(bank, w, k_range, left, width, at=0, out_at=0):
                for k in range(k_range):
                    ins = pe.matmul(PS[0:n, b[bank], out_at:out_at + width], left[:, k, cols], w[:, k, at:at + width],
                                    start=k == 0, stop=k == k_range - 1)
                return ins

            if kind in ("qi", "qb", "kb", "vb"):
                pe.wait_ge(sem(f"w_{kind}_in"), upto(f"w_{kind}_in", kind))
                pe.wait_ge(sem("h_ready"), upto("h_ready", ("h", m, 1)))
                ins = groups(0, w_view(kind), KD, hT, 512)
            elif kind == "sm":
                pe.wait_ge(sem("w_sm_in"), upto("w_sm_in", "sm"))
                ins = groups(0, w_view(kind), KD, hT, 104)
            elif kind == "cq":
                pe.wait_ge(sem("w_c0_in"), upto("w_c0_in", "c0"))
                groups(0, w_view("c0"), KD, hT, 512)
                pe.wait_ge(sem("w_c1_in"), upto("w_c1_in", "c1"))
                ins = groups(1, w_view("c1"), KD, hT, 512)
            elif kind == "uq":
                pe.wait_ge(sem("w_uq_in"), upto("w_uq_in", "uq"))
                pe.wait_ge(sem("turned_act"), upto("turned_act", "cq", m, 1))
                groups(0, w_view("uq"), 6, cqT, 384)
                ins = groups(1, w_view("uq"), 6, cqT, 384, at=384)
            elif kind == "wt":
                return
            elif kind == "kn":
                pe.wait_ge(sem("turned_act"), upto("turned_act", "cq", 4, 2))
                for c in range(2):
                    ins = pe.matmul(PS[0:64, b[0], :], wuk[:, c, 64 * m:64 * m + 64], ckvT[:, c, 0:512],
                                    start=c == 0, stop=c == 1)
            elif kind == "kl":
                for h in range(H):
                    for c in range(2):
                        ins = pe.matmul(PS[0:64, b[0], 16 * h:16 * h + 16], wuk[:, c, 64 * h:64 * h + 64],
                                        ckvT[:, c, LAST:LAST + 16], start=c == 0, stop=c == 1)
            elif kind == "ql":
                pe.wait_ge(sem("turned_act"), upto("turned_act", "wt", 0, 3))
                pe.wait_ge(sem("turned_act"), upto("turned_act", "uq", 4, 1))
                for h in range(H):
                    ins = pe.matmul(PS[:, b[0], 64 * h:64 * h + 64], wukT[0:64, h, 128 * m:128 * m + 128],
                                    qT[0:64, h, 512:512 + NS], start=True, stop=True)
            elif kind == "vm":
                pe.wait_ge(sem("wuv_in"), upto("wuv_in", 0))
                cols = token_cols(m) if m < 4 else slice(LAST, LAST + 16)
                n = 128 if m < 4 else 16
                ins = groups(0, wuv, 2, ckvT, 512)
            ins.then_inc(sem("product"), tick("product", *u))

        sturns = [("i", b, i) for b in range(NB) for i in range(4)]
        AHEAD = 7
        for b in range(NB + 1):
            if b < NB:
                sturns += [("p", b, 0), ("p", b, 1)]
            for c in range(8):
                if b < NB:
                    sturns += [("c", b, c, 0), ("c", b, c, 1)]
                if b and c == (AHEAD if b < NB else 0):
                    sturns += [("t", b - 1, i) for i in range(5)] + [("o", b - 1)]
        sturn_no = {key: i for i, key in enumerate(sturns)}
        keysT_users = [k for k in sturns if k[0] in "ic"]
        keysT_no = {key: i for i, key in enumerate(keysT_users)}

        def sturn_bank(key):
            return 4 + sturn_no[key] % 4

        def wait_stored(eng, name):
            if name == "kb":
                for m in range(NTILE):
                    eng.wait_ge(sem(f"stored_kb_p{m}"), upto(f"stored_kb_p{m}", m))
            else:
                eng.wait_ge(sem(f"stored_{name}_p"), upto(f"stored_{name}_p", 4))

        def phase_a_done(eng):
            eng.wait_ge(sem("product"), upto("product", "vb", 4))
            eng.wait_ge(sem("unit_act"), upto("unit_act", "vb", 4))
            eng.wait_ge(sem("b_roped"), upto("b_roped", "kb", 4))
            eng.wait_ge(sem("turned_act"), upto("turned_act", "kb", 4, 0))
            eng.wait_ge(sem("h_stored"), upto("h_stored", 0))
            for name in ("ki", "ckv", "kpe", "kb"):
                wait_stored(eng, name)
                eng.wait_ge(sem(f"stored_{name}_s"), upto(f"stored_{name}_s", 4))

        def pe_sturn(pe, key, srcs, width, right=None):
            i = sturn_no[key]
            if i >= 4:
                pe.wait_ge(sem("sturn_out"), upto("sturn_out", sturns[i - 4]))
            bank = PS[:, sturn_bank(key), :].rearrange("p (a n) -> p a n", n=width)
            for n, src in enumerate(srcs):
                k, w = src.shape
                if right is None:
                    ins = pe.transpose(bank[0:w, n, 0:k], src, ident[0:k, 0:k])
                else:
                    ins = pe.matmul(bank[0:w, n, :], src, right, start=True, stop=True)
            ins.then_inc(sem("sturned"), tick("sturned", key))

        def act_sturn(act, key, dst, src):
            act.wait_ge(sem("sturned"), upto("sturned", key))
            if key in keysT_no and keysT_no[key] >= 4:
                act.wait_ge(sem("keysT_used"), upto("keysT_used", keysT_users[keysT_no[key] - 4]))
            act.copy(dst, src).then_inc(sem("sturn_out"), tick("sturn_out", key))

        def raw_slot(n):
            return raw[:, n % 8, :] if n % 8 < 5 else raw_more[:, n % 8 - 5, :]

        def pe_index(pe):
            phase_a_done(pe)
            def turn(b, i):
                if i == 0:
                    pe.wait_ge(sem(f"ik_in{b % 3}"), upto(f"ik_in{b % 3}", b))
                ik = raw[:, b % 3, :]
                pe_sturn(pe, ("i", b, i), [ik[:, 128 * (4 * i + q):128 * (4 * i + q) + 128] for q in range(4)], 128)

            def weigh(n):
                b, i = n
                g = index_groups.index(n)
                pe.wait_ge(sem("relued"), upto("relued", n))
                if g >= 2:
                    pe.wait_ge(sem("weighed_out"), upto("weighed_out", index_groups[g - 2]))
                if i < 4:
                    ins = pe.matmul(PS[0:40, 2 + g % 2, :], wb[:, b, :], relu_i[:, g % 2, :], start=True, stop=True)
                else:
                    ins = pe.matmul(PS[0:8, 2 + g % 2, 0:NT], wb[0:64, b, 0:8], relu_i[0:64, g % 2, 0:NT], start=True,
                                    stop=True)
                ins.then_inc(sem("weighed"), tick("weighed", n))

            turn(0, 0)
            pe.wait_ge(sem("wb_ready"), upto("wb_ready"))
            pe.wait_ge(sem("qi_2_ready"), upto("qi_2_ready"))
            nxt = [(b, i) for b in range(NB) for i in range(4)][1:] + [None]
            for n, (b, i) in enumerate(index_groups):
                if i < 4:
                    t = nxt[4 * b + i]
                    if t:
                        turn(*t)
                    pe.wait_ge(sem("sturn_out"), upto("sturn_out", ("i", b, i)))
                if n >= 2:
                    pe.wait_ge(sem("relued"), upto("relued", index_groups[n - 2]))
                if i < 4:
                    key = ("i", b, i)
                    ins = pe.matmul(PS[:, n % 2, :], qi_2[:, b, :], keysT[:, keysT_no[key] % 4, :], start=True,
                                    stop=True)
                    ins.then_inc(sem("index_dots"), tick("index_dots", (b, i)))
                    same(("keysT_used", key), ("index_dots", (b, i)))
                else:
                    pe.matmul(PS[0:64, n % 2, 0:NT], qi_2[0:64, b, 0:64],
                                     kiT[0:64, 512 + NT * b:512 + NT * b + NT], start=True, stop=True).then_inc(
                        sem("index_dots"), tick("index_dots", (b, i)))
                if n >= 1:
                    weigh(index_groups[n - 1])
            weigh(index_groups[-1])

        index_groups = [(b, i) for b in range(NB) for i in range(5)]

        def act_index(act):
            phase_a_done(act)
            act.wait_ge(sem("zeroed"), upto("zeroed"))
            for b in range(NB):
                for u in range(2):
                    r = slice(64 * u, 64 * u + 64)
                    ins = act.copy(qi_2[r, b, 64 * u:64 * u + 64], qi_s[r, 64 * b:64 * b + 64])
            ins.then_inc(sem("qi_2_ready"), tick("qi_2_ready"))
            turn_list = [("i", b, i) for b in range(NB) for i in range(4)]

            def turn(n):
                if n < len(turn_list):
                    key = turn_list[n]
                    act_sturn(act, key, keysT[:, keysT_no[key] % 4, :], PS[:, sturn_bank(key), :])

            turn(0)
            for g, (b, i) in enumerate(index_groups):
                if i < 4:
                    turn(4 * b + i + 1)
                act.wait_ge(sem("index_dots"), upto("index_dots", (b, i)))
                if g >= 2:
                    act.wait_ge(sem("weighed"), upto("weighed", index_groups[g - 2]))
                r, w = (slice(0, 128), 512) if i < 4 else (slice(0, 64), NT)
                act.activation(relu_i[r, g % 2, 0:w], PS[r, g % 2, 0:w], ACT.Relu, scale=0.125).then_inc(
                    sem("relued"), tick("relued", (b, i)))

        def dve_index(dve, link):
            phase_a_done(dve)
            dve.memset(flat(qi_2), 0.0)
            link(dve.memset(flat(wb), 0.0))
            dve.memset(flat3(qpe_z), 0.0).then_inc(sem("zeroed"), tick("zeroed"))
            dve.wait_ge(sem("wcol_in"), upto("wcol_in", H - 1))
            for b in range(NB):
                for u in range(2):
                    r = slice(64 * u, 64 * u + 64)
                    ins = dve.tensor_scalar(wb[r, b, 32 * u:32 * u + 8], same_t[r], wcol[r, b:b + 1], None, ALU.mult)
            ins.then_inc(sem("wb_ready"), tick("wb_ready"))
            by_key = row_scores[0][0:8, 0:PAST].rearrange("t (p j) -> t j p", j=32)
            for g, (b, i) in enumerate(index_groups):
                dve.wait_ge(sem("weighed"), upto("weighed", (b, i)))
                if b and i == 0:
                    dve.wait_ge(sem(f"rows_moved{(b - 1) % 2}"), upto(f"rows_moved{(b - 1) % 2}", b - 1))
                if i < 4:
                    for par in range(2):
                        ins = dve.tensor_copy(by_key[:, 8 * i + par:8 * i + par + 7:2, :],
                                              PS[32 * par:32 * par + 8, 2 + g % 2, :]
                                              .rearrange("t (q p) -> t q p", q=4))
                else:
                    ins = dve.tensor_tensor(row_scores[0][0:8, PAST:PAST + NT], PS[0:8, 2 + g % 2, 0:NT],
                                            causal8[0:8], ALU.add)
                ins.then_inc(sem("weighed_out"), tick("weighed_out", (b, i)))

        def gp_sample_loads(gp):
            phase_a_done(gp)
            gp.wait_ge(sem("index_ready"), upto("index_ready"))
            ik_rows = I["cache_idx_k"].rearrange("l n (q r) d -> (l n q) (r d)", q=4)
            for b in range(NB):
                if b >= 3:
                    gp.wait_ge(sem("sturned"), upto("sturned", ("i", b - 3, 3)))
                gp.indirect_dma_start(raw[:, b % 3, :], None, ik_rows,
                                             bass.IndirectOffsetOnAxis(ap=idx_row[:, b:b + 1], axis=0)).then_inc(
                    sem(f"ik_in{b % 3}"), tick(f"ik_in{b % 3}", b, by=16))
            kpe_rows = I["cache_mla_kpe"].rearrange("l n (q r) d -> (l n q) (r d)", q=4)
            ckv_rows = I["cache_mla_ckv"].rearrange("l n (q r) c -> (l n q) (r c)", q=16)
            for b in range(NB):
                if b:
                    gp.wait_ge(sem("sturned"), upto("sturned", ("p", b - 1, 1)))
                gp.indirect_dma_start(kpe_raw, None, kpe_rows,
                                             bass.IndirectOffsetOnAxis(ap=idx_row[:, b:b + 1], axis=0)).then_inc(
                    sem("kpe_in"), tick("kpe_in", b, by=16))
                for j in range(4):
                    n = 4 * b + j
                    if n < 8:
                        gp.wait_ge(sem("sturned"), upto("sturned", ("i", NB - 1, 3)))
                        gp.wait_ge(sem("heads_stored"), upto("heads_stored"))
                    else:
                        gp.wait_ge(sem("latents_used"), upto("latents_used", n - 8))
                    gp.indirect_dma_start(raw_slot(n), None, ckv_rows,
                                                 bass.IndirectOffsetOnAxis(ap=idx_ckv[:, b, j:j + 1], axis=0)).then_inc(
                        sem(f"ckv_in{n % 8}"), tick(f"ckv_in{n % 8}", n, by=16))

        def sp_sample(sp):
            sp.dma_start(same_b[0:NS], I["c_same_b"]).then_inc(sem("tables_in"), tick("tables_in", by=16))
            for b in range(NB):
                sp.dma_start(pages_q[8 * b:8 * b + 8, :], I["page_table"][b].partition_broadcast(8)).then_inc(
                    sem("tables_in"), tick("tables_in", by=16))
            sp.wait_ge(sem("turned_act"), upto("turned_act", "uq", 4, 1))
            sp.dma_start(scratch["qT"], flat(qT)[0:96]).then_inc(sem("heads_stored"), tick("heads_stored", by=16))
            sp.wait_ge(sem("unit_act"), upto("unit_act", "kl", 0))
            sp.dma_start(scratch["kT"], flat(kT)[0:96]).then_inc(sem("heads_stored"), tick("heads_stored", by=16))
            sp.wait_ge(sem("unit_act"), upto("unit_act", "vm", 4))
            sp.dma_start(scratch["vm"][:, 0:2048], flat(vm)[:, 0:2048]).then_inc(
                sem("heads_stored"), tick("heads_stored", by=16))
            sp.dma_start(scratch["vm"][0:16, 2048:2560], flat(vm)[0:16, 2048:2560]).then_inc(
                sem("heads_stored"), tick("heads_stored", by=16))
            half = (PAST + NT) // 2
            for b in range(NB):
                sp.wait_ge(sem("weighed_out"), upto("weighed_out", (b, 4)))
                for u in range(2):
                    sp.dma_start(pick_scores[64 * u + 8 * b:64 * u + 8 * b + 8, :],
                                        row_scores[0][0:8, half * u:half * u + half]).then_inc(
                        sem(f"rows_moved{b % 2}"), tick(f"rows_moved{b % 2}", *((b,) if u else ()), by=16))
            sp.wait_ge(sem("stored_ckv_s"), upto("stored_ckv_s", 4))
            sp.wait_ge(sem("weighed"), upto("weighed", index_groups[-1]))
            for b in range(NB):
                if b >= 2:
                    sp.wait_ge(sem("o_lat_done"), upto("o_lat_done", b - 2))
                sp.dma_start(lat_new[0:NT, b % 2, :], O["new_ckv_s"][0, b]).then_inc(
                    sem(f"lat_new_in{b % 2}"), tick(f"lat_new_in{b % 2}", b, by=16))
            sp.wait_ge(sem("picks_done"), upto("picks_done"))
            sp.dma_start(picked_up[0:NS], picked[NS:128]).then_inc(sem("upper_in"), tick("upper_in", by=16))
            sp.dma_start(picked_at_up[0:NS], picked_at[NS:128]).then_inc(
                sem("upper_in"), tick("upper_in", by=16))
            sp.wait_ge(sem("o_lat_done"), upto("o_lat_done", NB - 1))
            sp.dma_start(wide_tri, I["c_wide_tri"]).then_inc(sem("mask_in"), tick("mask_in", by=16))

        def pe_latent(pe):
            def turn(b, c, f):
                n = 4 * b + c // 2
                if c % 2 == 0 and f == 0:
                    pe.wait_ge(sem(f"ckv_in{n % 8}"), upto(f"ckv_in{n % 8}", n))
                slot = raw_slot(n).rearrange("p (j c) -> p j c", j=8)
                pe_sturn(pe, ("c", b, c, f), [slot[:, 4 * (c % 2) + q, 128 * f:128 * f + 128] for q in range(4)], 128)

            def dots(b):
                pe.wait_ge(sem("kpe_in"), upto("kpe_in", b))
                for i in range(2):
                    pe_sturn(pe, ("p", b, i), [kpe_raw[:, 128 * (4 * i + q):128 * (4 * i + q) + 128]
                                               for q in range(4)], 128)
                turn(b, 0, 0)
                turn(b, 0, 1)
                pe.wait_ge(sem("sturn_out"), upto("sturn_out", ("p", b, 1)))
                pe.wait_ge(sem("qpe_spread"), upto("qpe_spread", b))
                if b == 0:
                    pe.wait_ge(sem("relued"), upto("relued", index_groups[-1]))
                q2 = [ql_s[:, f, 64 * b:64 * b + 64] for f in range(2)]
                for c in range(8):
                    if c < 7:
                        turn(b, c + 1, 0)
                        turn(b, c + 1, 1)
                    out = PS[0:64, c % 2, :]
                    if c >= 2:
                        pe.wait_ge(sem("scored"), upto("scored", b, c - 2))
                    elif b:
                        pe.wait_ge(sem("new_scored"), upto("new_scored", b - 1)) if c == 0 else pe.wait_ge(sem("scored"), upto("scored", b - 1, 7))
                    for f in range(2):
                        key = ("c", b, c, f)
                        pe.wait_ge(sem("sturn_out"), upto("sturn_out", key))
                        ins = pe.matmul(out, q2[f], keysT[:, keysT_no[key] % 4, :], start=f == 0, stop=False,
                                        skip_group_check=True)
                        ins.then_inc(sem("keysT_used"), tick("keysT_used", key))
                    for q in range(4):
                        ins = pe.matmul(out[:, 128 * q:128 * q + 128], qpe_z[:, b % 2, q, :], kpeT[b % 2][:, c, :],
                                        start=False, stop=q == 3, skip_group_check=True)
                    ins.then_inc(sem("latent_dots"), tick("latent_dots", b, c))
                    if c == AHEAD - 1 and b:
                        outputs(b - 1)
                pe.wait_ge(sem("scored"), upto("scored", b, 6))
                new = slice(NT * b, NT * b + NT)
                for f in range(2):
                    pe.matmul(PS[0:64, 0, 0:NT], q2[f], ckv_new[:, f, new], start=f == 0, stop=False)
                pe.matmul(PS[0:64, 0, 0:NT], qpe_s[0:32, 64 * b:64 * b + 64],
                                 kpe_new[0:32, NT * b:NT * b + NT], start=False, stop=True).then_inc(
                    sem("latent_dots"), tick("latent_dots", b, 8))

            def outputs(b):
                pe.wait_ge(sem("exped"), upto("exped", b))
                row = row_scores[b % 2]
                for i in range(4):
                    pe_sturn(pe, ("t", b, i), [row[0:64, 128 * j:128 * j + 128] for j in range(8 * i, 8 * i + 8)], 64)
                pe_sturn(pe, ("t", b, 4), [row[0:64, PAST:PAST + NT]], 64)
                if b:
                    pe.wait_ge(sem("o_rows_out"), upto("o_rows_out", b - 1))
                else:
                    pe.wait_ge(sem("weighed_out"), upto("weighed_out", index_groups[-1]))
                out = PS[0:64, 2, 0:KVL]
                for j in range(32):
                    if j % 8 == 0:
                        pe.wait_ge(sem("sturn_out"), upto("sturn_out", ("t", b, j // 8)))
                    slot = raw_slot(4 * b + j // 8).rearrange("p (j c) -> p j c", j=8)
                    ins = pe.matmul(out, probsT[:, j, :], slot[:, j % 8, :], start=j == 0, stop=False)
                    if j % 8 == 7:
                        ins.then_inc(sem("latents_used"), tick("latents_used", 4 * b + j // 8))
                pe.wait_ge(sem("sturn_out"), upto("sturn_out", ("t", b, 4)))
                pe.wait_ge(sem(f"lat_new_in{b % 2}"), upto(f"lat_new_in{b % 2}", b))
                pe.matmul(out, probsT[0:NT, 32, :], lat_new[0:NT, b % 2, :], start=False, stop=True).then_inc(
                    sem("o_lat_done"), tick("o_lat_done", b))
                pe.wait_ge(sem("o_rows_out"), upto("o_rows_out", b))
                pe_sturn(pe, ("o", b), [o_rows[0:64, 128 * f:128 * f + 128] for f in range(2)], 64)

            for b in range(NB + 1):
                if b < NB:
                    dots(b)
                else:
                    outputs(b - 1)
            pe.wait_ge(sem("sturn_out"), upto("sturn_out", ("o", NB - 1)))
            for h in range(H):
                for f in range(2):
                    ins = pe.matmul(PS[64 * (h % 2):64 * (h % 2) + 64, 0, 64 * (h // 2):64 * (h // 2) + 64],
                                    wuv[:, f, 64 * h:64 * h + 64],
                                    o_lat[:, f, :].rearrange("p (b h t) -> p b h t", b=NB, h=H)[:, :, h, :],
                                    start=f == 0, stop=f == 1)
            ins.then_inc(sem("o_s_done"), tick("o_s_done", 0))

        def act_latent(act):
            def exp(b):
                row = row_scores[b % 2][0:64]
                act.wait_ge(sem("neg_max"), upto("neg_max", b))
                act.activation(row, row, ACT.Exp, bias=col[0:64, b % 2, 0:1], accum_out=col[0:64, b % 2, 1:2]).then_inc(
                    sem("exped"), tick("exped", b))

            def dots(b):
                for i in range(2):
                    act_sturn(act, ("p", b, i), kpeT[b % 2][:, 4 * i:4 * i + 4, :],
                              PS[:, sturn_bank(("p", b, i)), :].rearrange("p (a n) -> p a n", a=4))
                for f in range(2):
                    turn_out(act, b, 0, f)
                if b < 2:
                    act.wait_ge(sem("zeroed"), upto("zeroed"))
                    act.wait_ge(sem("heads_stored"), upto("heads_stored"))
                for q in range(4):
                    ins = act.copy(qpe_z[32 * q:32 * q + 32, b % 2, q, :], qpe_s[32 * q:32 * q + 32, 64 * b:64 * b + 64])
                ins.then_inc(sem("qpe_spread"), tick("qpe_spread", b))
                if b == 0:
                    act.wait_ge(sem("rows_moved1"), upto("rows_moved1", NB - 1))
                    act.wait_ge(sem("rows_moved0"), upto("rows_moved0", NB - 2))
                for c in range(8):
                    if c < 7:
                        for f in range(2):
                            turn_out(act, b, c + 1, f)
                    act.wait_ge(sem("latent_dots"), upto("latent_dots", b, c))
                    act.mul(row_scores[b % 2][0:64, 512 * c:512 * c + 512], PS[0:64, c % 2, :], MLA_SCALE).then_inc(
                        sem("scored"), tick("scored", b, c))
                    if c == 1 and b:
                        exp(b - 1)
                    if c == AHEAD - 1 and b:
                        outputs(b - 1)

            def outputs(b):
                for i in range(4):
                    key = ("t", b, i)
                    act_sturn(act, key, probsT[:, 8 * i:8 * i + 8, :],
                              PS[:, sturn_bank(key), :].rearrange("p (a n) -> p a n", a=8))
                act_sturn(act, ("t", b, 4), probsT[0:NT, 32, :], PS[0:NT, sturn_bank(("t", b, 4)), 0:64])
                act.wait_ge(sem("o_lat_done"), upto("o_lat_done", b))
                act.wait_ge(sem("sum_inverse"), upto("sum_inverse", b))
                act.activation(o_rows[0:64], PS[0:64, 2, 0:KVL], ACT.Copy, scale=col[0:64, b % 2, 3:4]).then_inc(
                    sem("o_rows_out"), tick("o_rows_out", b))
                act_sturn(act, ("o", b), o_lat[:, :, 64 * b:64 * b + 64],
                          PS[:, sturn_bank(("o", b)), 0:128].rearrange("p (a n) -> p a n", a=2))

            for b in range(NB):
                dots(b)
            exp(NB - 1)
            outputs(NB - 1)
            act.wait_ge(sem("o_s_done"), upto("o_s_done", 0))
            act.copy(oT_s, PS[:, 0, 0:256].rearrange("p (a n) -> p a n", a=4)).then_inc(
                sem("o_s_out"), tick("o_s_out", 0))

        def turn_out(act, b, c, f):
            key = ("c", b, c, f)
            act_sturn(act, key, keysT[:, keysT_no[key] % 4, :], PS[:, sturn_bank(key), :])

        def dve_latent(dve, link):
            dve.wait_ge(sem("rows_moved0"), upto("rows_moved0", NB - 2))
            dve.wait_ge(sem("rows_moved1"), upto("rows_moved1", NB - 1))

            def pick(step):
                r, k = divmod(step, 3)
                top = picked_at[:, 8 * r:8 * r + 8]
                if k == 0:
                    link(dve.max(top, pick_scores))
                elif k == 1:
                    dve.max_index(picked[:, 8 * r:8 * r + 8], top, pick_scores)
                else:
                    link(dve.match_replace(pick_scores, top, pick_scores, TAKEN))
                    same(("picks_done",), ("chain_dve",))

            q = slice(0, NS)

            def find_rows(i):
                if i == 0:
                    dve.wait_ge(sem("tables_in"), upto("tables_in"))
                    link(dve.tensor_copy(pages_f[q], pages_q[q]))
                    dve.wait_ge(sem("upper_in"), upto("upper_in"))
                    link(dve.tensor_copy(low[q], picked[q]))
                    link(dve.tensor_copy(up[q], picked_up[q]))
                    link(dve.tensor_scalar(up[q], up[q], float((PAST + NT) // 2), None, ALU.add))
                    link(dve.tensor_tensor(keep[q], picked_at[q], picked_at_up[q, ::-1], ALU.is_ge))
                    link(dve.tensor_tensor(low[q], low[q], up[q, ::-1], ALU.subtract))
                    link(dve.tensor_tensor(low[q], low[q], keep[q], ALU.mult))
                    link(dve.tensor_tensor(picked[q], low[q], up[q, ::-1], ALU.add))
                elif i == 1:
                    link(dve.tensor_scalar(page[q], picked[q], 7, None, ALU.logical_shift_right))
                    link(dve.tensor_scalar(offset[q], picked[q], 127, None, ALU.bitwise_and))
                    link(dve.tensor_copy(page_f[q], page[q]))
                    link(dve.tensor_copy(off_f[q], offset[q]))
                    link(dve.tensor_scalar(phys[q], page_f[q], 0.0, pages_f[q, 0:1], ALU.is_equal, ALU.mult))
                elif i <= NPG:
                    p = i - 1
                    link(dve.tensor_scalar(hit[q], page_f[q], float(p), pages_f[q, p:p + 1], ALU.is_equal, ALU.mult))
                    link(dve.tensor_tensor(phys[q], phys[q], hit[q], ALU.add))
                elif i == NPG + 1:
                    dve.scalar_tensor_tensor(out=phys[q], in0=phys[q], scalar=float(PAGE), in1=off_f[q],
                                                    op0=ALU.mult, op1=ALU.add).then_inc(
                        sem("row_found"), tick("row_found"))
                    link(dve.tensor_scalar(slot_bias[q], page_f[q], float(NPG), NEG, ALU.is_ge, ALU.mult))
                    link(dve.tensor_scalar(hit[q], page_f[q], float(NPG), -float(PAGE), ALU.not_equal, ALU.mult))
                    link(dve.tensor_tensor(off_f[q], off_f[q], hit[q], ALU.add))
                elif i < NPG + 2 + NT:
                    j = i - NPG - 2
                    link(dve.tensor_scalar(hit[q], off_f[q], float(j), None, ALU.is_equal))
                    link(dve.tensor_reduce(new_hit[q, j:j + 1], hit[q], AX.X, ALU.max))
                else:
                    link(dve.tensor_tensor(new_bias[q], same_b[q].unsqueeze(2).to_broadcast([NS, 8, 8]),
                                           new_hit[q].unsqueeze(1).to_broadcast([NS, 8, 8]), ALU.mult))
                    link(dve.tensor_scalar(new_bias[q], new_bias[q], 1.0, -NEG, ALU.subtract, ALU.mult))

            def divide(b):
                dve.wait_ge(sem("exped"), upto("exped", b))
                dve.reciprocal(col[0:64, b % 2, 3:4], col[0:64, b % 2, 1:2]).then_inc(
                    sem("sum_inverse"), tick("sum_inverse", b))

            picks, finds, chunks, late = 3 * TOPK_S // 8, NPG + 3 + NT, 9 * NB, 12
            picked_so_far = found_so_far = 0
            for b in range(NB):
                row, cm, cl = row_scores[b % 2], chunk_max[0:64, b % 2, :], col[0:64, b % 2, :]
                for c in range(9):
                    at = 9 * b + c + 1
                    while picked_so_far < min(picks, picks * at // (chunks - late - 1)):
                        pick(picked_so_far)
                        picked_so_far += 1
                    while found_so_far < finds * (at - chunks + late) // late:
                        find_rows(found_so_far)
                        found_so_far += 1
                    if c == 3 and b:
                        divide(b - 1)
                    if c < 8:
                        dve.wait_ge(sem("scored"), upto("scored", b, c))
                        dve.tensor_reduce(cm[:, c:c + 1], row[0:64, 512 * c:512 * c + 512], AX.X, ALU.max).then_inc(
                            sem("chunk_maxed"), tick("chunk_maxed", b, c))
                dve.wait_ge(sem("latent_dots"), upto("latent_dots", b, 8))
                dve.scalar_tensor_tensor(out=row[0:64, PAST:PAST + NT], in0=PS[0:64, 0, 0:NT],
                                                scalar=MLA_SCALE, in1=causal8[0:64], op0=ALU.mult, op1=ALU.add).then_inc(
                    sem("new_scored"), tick("new_scored", b))
                dve.wait_ge(last.sem, last.value)
                link(dve.tensor_reduce(cm[:, 8:9], row[0:64, PAST:PAST + NT], AX.X, ALU.max))
                link(dve.tensor_reduce(cl[:, 2:3], cm, AX.X, ALU.max))
                dve.tensor_scalar(cl[:, 0:1], cl[:, 2:3], -1.0, None, ALU.mult).then_inc(
                    sem("neg_max"), tick("neg_max", b))
            divide(NB - 1)

        KEYS = [128, 256, 384, 512, NP]
        QW = [128, 128, 128, 128, 16]
        groups_p = []
        for m in range(NTILE):
            groups_p += [("i", m, h) for h in range(H)] if m else []
            groups_p += [(kind, m, h) for kind in ("ab" if m else "ba") for h in range(H)]
        group_no = {g: i for i, g in enumerate(groups_p)}
        steps_p = [g for g in groups_p if g[0] != "i"]
        step_no = {g: i for i, g in enumerate(steps_p)}
        pe_order = []
        for n, g in enumerate(steps_p + [None] * 4):
            if g:
                if g[0] == "a" and g[2] == 0 and g[1]:
                    pe_order += [("score", ("i", g[1], h)) for h in range(H)]
                pe_order.append(("score", g))
            if 2 <= n < len(steps_p) + 2:
                pe_order.append(("turn", steps_p[n - 2]))
            if 3 <= n < len(steps_p) + 3:
                pe_order.append(("weigh", steps_p[n - 3]))
            if n >= 4 and steps_p[n - 4][2] == H - 1:
                pe_order.append(("close", steps_p[n - 4]))
        pturns = [({"turn": "P", "close": "O"}[kind], g) for kind, g in pe_order if kind in ("turn", "close")]
        pturn_no = {t: i + 1 for i, t in enumerate(pturns)}

        def q_cols(m):
            return slice(128 * m, 128 * m + 128) if m < 4 else slice(LAST, LAST + 16)

        def scores_at(g):
            n = 2 * (group_no[g] % 2)
            return PS[:, n:n + 2, :].rearrange("p a b -> p (a b)")

        def group_read(eng, g):
            eng.wait_ge(sem("relu_p_done" if g[0] == "i" else "masked"), upto("relu_p_done" if g[0] == "i" else "masked", g))

        def phase_c_done(eng):
            eng.wait_ge(sem("o_s_done"), upto("o_s_done", 0))
            eng.wait_ge(sem("o_s_out"), upto("o_s_out", 0))
            eng.wait_ge(sem("picks_done"), upto("picks_done"))

        def pe_prompt(pe):
            phase_c_done(pe)
            pe.wait_ge(sem("row_found"), upto("row_found"))
            for f in range(2):
                ins = pe.transpose(PS[:, 4, 64 * f:64 * f + 64], phys[0:64, 128 * f:128 * f + 128], ident[0:64, 0:64])
            ins.then_inc(sem("rows_turned"), tick("rows_turned"))
            pe.wait_ge(sem("o_s_out"), upto("o_s_out", 0))

            def score(g):
                kind, m, h = g
                n = group_no[g]
                if n >= 2:
                    group_read(pe, groups_p[n - 2])
                out = scores_at(g)[0:QW[m]]
                par = slice(64 * (h % 2), 64 * (h % 2) + 64)
                if kind == "i":
                    q, keys, last_col = qiT[par, h // 2, q_cols(m)], kiT[par], LAST
                elif kind == "b":
                    q, keys, last_col = qbT[par, h // 2, q_cols(m)], kbT[par, h // 2], LAST
                else:
                    pe.wait_ge(sem("heads_back"), upto("heads_back"))
                    q, keys, last_col = qT[0:96, h, q_cols(m)], kT[0:96, h], 512
                ins = pe.matmul(out[:, 0:min(KEYS[m], 512)], q, keys[:, 0:min(KEYS[m], 512)], start=True, stop=True)
                if m == 4:
                    ins = pe.matmul(out[:, 512:NP], q, keys[:, last_col:last_col + 16], start=True, stop=True)
                ins.then_inc(sem("scored_p"), tick("scored_p", g))

            def turn(t, srcs):
                n = pturn_no[t]
                if n >= 2:
                    pe.wait_ge(sem("pturn_out"), upto("pturn_out", pturns[n - 3] if n >= 3 else ("N",)))
                bank = PS[:, 4 + n % 2, :]
                at = 0
                for src in srcs:
                    k, w = src.shape
                    ins = pe.transpose(bank[0:w, at:at + k], src, ident[0:k, 0:k])
                    at += k
                ins.then_inc(sem("pturned"), tick("pturned", t))

            def tiles_of(m):
                return [(128 * k, 128) for k in range(min(m + 1, 4))] + ([(512, 16)] if m == 4 else [])

            def turn_probs(g):
                kind, m, h = g
                w, n = QW[m], step_no[g]
                pe.wait_ge(sem("exped_p"), upto("exped_p", g))
                turn(("P", g), [probs[0:w, n % 3, a:a + k] for a, k in tiles_of(m)])

            def weigh(g):
                kind, m, h = g
                w, n = QW[m], step_no[g]
                tiles = tiles_of(m)
                pe.wait_ge(sem("pturn_out"), upto("pturn_out", ("P", g)))
                if n >= 2:
                    pe.wait_ge(sem("o_out"), upto("o_out", steps_p[n - 2]))
                v = vm if kind == "a" else vb
                if kind == "b" and m == 4:
                    pe.wait_ge(sem("vb_last_in"), upto("vb_last_in"))
                for k, (a, rows_k) in enumerate(tiles):
                    vk = v[0:rows_k, k, :] if kind == "a" or k < 4 else vb_last[0:16]
                    ins = pe.matmul(PS[0:w, 6 + n % 2, 0:64], probs_T[0:rows_k, n % 2, k * w:k * w + w],
                                    vk[:, 64 * h:64 * h + 64], start=k == 0, stop=k == len(tiles) - 1)
                ins.then_inc(sem("o_done"), tick("o_done", g))

            def close(g):
                pe.wait_ge(sem("o_out"), upto("o_out", g))
                w = QW[g[1]]
                o = o_tok[0:w, 0 if g[0] == "a" else 1, :]
                turn(("O", g), [o[:, 128 * i:128 * i + 128] for i in range(4)])

            for kind, g in pe_order:
                {"score": score, "turn": turn_probs, "weigh": weigh, "close": close}[kind](g)

        def act_prompt(act):
            act.wait_ge(sem("o_lat_done"), upto("o_lat_done", NB - 1))
            act.wait_ge(sem("heads_stored"), upto("heads_stored"))
            act.wait_ge(sem("q_wide_in1"), upto("q_wide_in1", 1))
            act.dma_start(flat(qT)[0:96], scratch["qT"]).then_inc(sem("heads_back"), tick("heads_back", by=16))
            act.dma_start(flat(kT)[0:96], scratch["kT"]).then_inc(sem("heads_back"), tick("heads_back", by=16))
            act.dma_start(flat(vm)[:, 0:2048], scratch["vm"][:, 0:2048]).then_inc(
                sem("heads_back"), tick("heads_back", by=16))
            act.dma_start(flat(vm)[0:16, 2048:2560], scratch["vm"][0:16, 2048:2560]).then_inc(
                sem("heads_back"), tick("heads_back", by=16))
            phase_c_done(act)
            act.wait_ge(sem("rows_turned"), upto("rows_turned"))
            act.copy(row_no, PS[:, 4, 0:128].rearrange("p (a n) -> p a n", a=2)).then_inc(
                sem("row_no_ready"), tick("row_no_ready"))
            same(("pturn_out", ("N",)), ("row_no_ready",))
            act.copy(oT_a[:, :, 512:512 + NS], oT_s)

            def out(g):
                kind, m, h = g
                w, n = QW[m], step_no[g]
                t = ("P", g)
                act.wait_ge(sem("pturned"), upto("pturned", t))
                if n >= 2:
                    act.wait_ge(sem("o_done"), upto("o_done", steps_p[n - 2]))
                bank = PS[:, 4 + pturn_no[t] % 2, :]
                full = min(m + 1, 4) * w
                ins = act.copy(probs_T[:, n % 2, 0:full], bank[:, 0:full])
                if m == 4:
                    ins = act.copy(probs_T[0:16, n % 2, full:full + w], bank[0:16, full:full + w])
                ins.then_inc(sem("pturn_out"), tick("pturn_out", t))

            def outputs_out(g):
                kind, m, h = g
                w, t = QW[m], ("O", g)
                act.wait_ge(sem("pturned"), upto("pturned", t))
                dst = oT_a if kind == "a" else oT_b
                act.copy(dst[:, :, q_cols(m)], PS[:, 4 + pturn_no[t] % 2, 0:4 * w]
                                .rearrange("p (a n) -> p a n", a=4)).then_inc(
                    sem("pturn_out"), tick("pturn_out", t))

            for what, g in pe_order:
                kind, m, h = g
                w = QW[m]
                if what == "turn":
                    out(g)
                    continue
                if what == "close":
                    outputs_out(g)
                    continue
                if what == "weigh":
                    n = step_no[g]
                    act.wait_ge(sem("inverted_p"), upto("inverted_p", g))
                    act.wait_ge(sem("o_done"), upto("o_done", g))
                    if h == 0 and m:
                        act.wait_ge(sem("pturned"), upto("pturned", ("O", (kind, m - 1, H - 1))))
                    act.activation(o_tok[0:w, 0 if kind == "a" else 1, 64 * h:64 * h + 64],
                                          PS[0:w, 6 + n % 2, 0:64], ACT.Copy, scale=stat[0:w, n % 6, 3:4]).then_inc(
                        sem("o_out"), tick("o_out", g))
                    continue
                if kind == "i":
                    act.wait_ge(sem("scored_p"), upto("scored_p", g))
                    if group_no[g] >= 2 and (h >= 2 or m > 1):
                        act.wait_ge(sem("acc_done"), upto("acc_done", ("i", m, h - 2) if h >= 2 else ("i", m - 1, 6 + h)))
                    act.activation(relu_p[0:w, h % 2, 0:KEYS[m]], scores_at(g)[0:w, 0:KEYS[m]], ACT.Relu,
                                          scale=0.125).then_inc(
                        sem("relu_p_done"), tick("relu_p_done", g))
                    continue
                n = step_no[g]
                act.wait_ge(sem("masked"), upto("masked", g))
                st = stat[0:w, n % 6, :]
                act.activation(probs[0:w, n % 3, 0:KEYS[m]], probs[0:w, n % 3, 0:KEYS[m]], ACT.Exp,
                                      bias=st[:, 0:1], scale=-1.0, accum_out=st[:, 2:3]).then_inc(
                    sem("exped_p"), tick("exped_p", g))

        def dve_prompt(dve, link):
            phase_c_done(dve)
            def invert(g):
                w, n = QW[g[1]], step_no[g]
                st = stat[0:w, n % 6, :]
                dve.wait_ge(sem("exped_p"), upto("exped_p", g))
                dve.reciprocal(st[:, 3:4], st[:, 2:3]).then_inc(sem("inverted_p"), tick("inverted_p", g))

            dve.wait_ge(sem("mask_in"), upto("mask_in"))
            dve.memset(score_acc[:, 0:4], DUMMY)
            for g in groups_p:
                kind, m, h = g
                w, keys = QW[m], KEYS[m]
                if kind == "i":
                    if m == 4:
                        dve.wait_ge(sem("wi_last_in"), upto("wi_last_in"))
                    weight = w_i[0:w, m, h:h + 1] if m < 4 else wi_last[0:16, h:h + 1]
                    acc = score_acc[0:w, 4:4 + keys]
                    dve.wait_ge(sem("relu_p_done"), upto("relu_p_done", g))
                    dve.wait_ge(last.sem, last.value)
                    r = relu_p[0:w, h % 2, 0:keys]
                    if h == 0:
                        ins = dve.tensor_scalar(acc, r, weight, None, ALU.mult)
                    else:
                        ins = dve.scalar_tensor_tensor(out=acc, in0=r, scalar=weight, in1=acc, op0=ALU.mult,
                                                       op1=ALU.add)
                    ins.then_inc(sem("acc_done"), tick("acc_done", g))
                    if h == H - 1:
                        dve.wait_ge(last.sem, last.value)
                        d = min(128 * m, 512)
                        link(dve.memset(score_acc[0:w, 0:4], DUMMY))
                        link(dve.tensor_tensor(acc[:, d:keys], acc[:, d:keys], wide_tri[0:w, 512:512 + keys - d],
                                               ALU.add))
                    continue
                n = step_no[g]
                p = probs[0:w, n % 3, 0:keys]
                st = stat[0:w, n % 6, :]
                if kind == "a" or m == 0:
                    d = 512 - min(128 * m, 512)
                    mask = wide_tri[0:w, d:d + keys]
                else:
                    mask = mask_s[0:w, 0:keys]
                scale = -MLA_SCALE if kind == "a" else -DSA_SCALE
                dve.wait_ge(sem("scored_p"), upto("scored_p", g))
                if n >= 6:
                    dve.wait_ge(sem("o_out"), upto("o_out", steps_p[n - 6]))
                if n >= 3:
                    dve.wait_ge(sem("pturned"), upto("pturned", ("P", steps_p[n - 3])))
                dve.tensor_tensor_reduce(p, scores_at(g)[0:w, 0:keys], mask, scale, -NEG, ALU.add, ALU.min,
                                                st[:, 0:1]).then_inc(
                    sem("masked"), tick("masked", g))
                if kind == "a" and m:
                    rounds = TOPK_P // 8 + 1
                    all_s = score_acc[0:w, 0:4 + keys]
                    for _ in range(rounds * h // H, rounds * (h + 1) // H):
                        link(dve.max(top8_p[0:w], all_s))
                        link(dve.match_replace(all_s, top8_p[0:w], all_s, TAKEN))
                    if h == H - 1:
                        link(dve.tensor_scalar(mask_s[0:w, 0:keys], score_acc[0:w, 4:4 + keys], -2e38, NEG,
                                               ALU.is_gt, ALU.mult))
                        d = min(128 * m, 512)
                        link(dve.tensor_tensor(mask_s[0:w, d:keys], mask_s[0:w, d:keys],
                                               wide_tri[0:w, 512:512 + keys - d], ALU.add))
                if LAG <= n < NS + LAG:
                    score_rows(dve, n - LAG)
                if n >= 2:
                    invert(steps_p[n - 2])
            for g in steps_p[-2:]:
                invert(g)

        LAG = 5

        def score_rows(dve, q):
            dve.wait_ge(sem(f"rows_in{q % 5}"), upto(f"rows_in{q % 5}", "k", q))
            dve.wait_ge(sem(f"q_wide_in{q % 2}"), upto(f"q_wide_in{q % 2}", q))
            dve.wait_ge(last.sem, last.value)
            k = rows[:, q % 5, :].rearrange("p (f n) -> p f n", f=2)
            dve.tensor_tensor(prod.rearrange("p (f n) -> p f n", f=2), k,
                                     q_wide[:, q % 2, :].unsqueeze(1).to_broadcast([128, 2, 512]), ALU.mult).then_inc(
                sem("k_used"), tick("k_used", q))
            dve.wait_ge(last.sem, last.value)
            dve.tensor_reduce(dots_k[:, :, q], prod.rearrange("p (a d) -> p a d", d=64), AX.X, ALU.add).then_inc(
                sem("k_scored"), tick("k_scored", q))

        def sp_prompt(sp):
            phase_c_done(sp)
            wait_stored(sp, "vb")
            sp.dma_start(vb_last[0:16], O["new_v_p"][0, 0, 512:528].rearrange("l h d -> l (h d)")).then_inc(
                sem("vb_last_in"), tick("vb_last_in", by=16))
            sp.dma_start(wi_last[0:16], w_i[NS:NS + 16, 4, :]).then_inc(
                sem("wi_last_in"), tick("wi_last_in", by=16))
            sp.wait_ge(sem("q_b_stored"), upto("q_b_stored", 0))
            for q in range(NS):
                if q >= 2:
                    sp.wait_ge(sem("k_used"), upto("k_used", q - 2))
                sp.dma_start(q_wide[:, q % 2, :], scratch["q_b"][q].partition_broadcast(128)).then_inc(
                    sem(f"q_wide_in{q % 2}"), tick(f"q_wide_in{q % 2}", q, by=16))

        def gp_gather(gp):
            phase_c_done(gp)
            gp.wait_ge(sem("row_no_ready"), upto("row_no_ready"))
            for name, pool in (("k", I["cache_dsa_k"]), ("v", I["cache_dsa_v"])):
                pool_rows = pool.rearrange("l n p h d -> (l n p) (h d)")
                for q in range(NS):
                    if q >= 5 or name == "v":
                        if q >= 5:
                            gp.wait_ge(sem(f"{name}_used"), upto(f"{name}_used", q - 5))
                        else:
                            gp.wait_ge(sem("k_used"), upto("k_used", max(x for x in range(NS) if x % 5 == q)))
                    for f in range(2):
                        gp.indirect_dma_start(rows[:, q % 5, 512 * f:512 * f + 512], None, pool_rows,
                                                     bass.IndirectOffsetOnAxis(ap=row_no[:, f, q:q + 1], axis=0)).then_inc(
                            sem(f"rows_in{q % 5}"), tick(f"rows_in{q % 5}", *((name, q) if f else ()), by=16))

        def pe_sparse(pe):
            for g in groups_p[-2:]:
                group_read(pe, g)
            for g in steps_p[-2:]:
                pe.wait_ge(sem("o_out"), upto("o_out", g))
            for t in pturns[-2:]:
                pe.wait_ge(sem("pturn_out"), upto("pturn_out", t))
            for h in range(H):
                par = slice(64 * (h % 2), 64 * (h % 2) + 64)
                ins = pe.matmul(PS[0:NS, 4 + h % 2, 64 * (h // 2):64 * (h // 2) + 64], qbT[par, h // 2, 512:512 + NS],
                                kbT[par, h // 2, 512:512 + NS], start=True, stop=True)
            ins.then_inc(sem("new_dots"), tick("new_dots"))
            pe.wait_ge(sem("k_scored"), upto("k_scored", NS - 1))
            for i in range(4):
                for n in range(4):
                    ins = pe.transpose(PS[0:NS, i, 128 * n:128 * n + 128], dots_k[:, 4 * i + n, :], ident)
                ins.then_inc(sem("dots_turned"), tick("dots_turned", i))
            pe.wait_ge(sem("sel_probs"), upto("sel_probs"))
            for f in range(2):
                for h in range(H):
                    ins = pe.transpose(PS[:, f, 64 * h:64 * h + 64], s_sel[0:NS, h, 128 * f:128 * f + 128],
                                       ident[0:NS, 0:NS])
                ins.then_inc(sem("sel_turned"), tick("sel_turned", f))
            for h in range(H):
                ins = pe.transpose(PS[0:NS, 2, 64 * h:64 * h + 64], s_sel[0:NS, h, TOPK_S:TOPK_S + NS],
                                   ident[0:NS, 0:NS])
            ins.then_inc(sem("sel_turned"), tick("sel_turned", 2))
            for f in range(3):
                pe.wait_ge(sem("sel_out"), upto("sel_out", f))
            for h in range(H):
                p = h // 2
                ins = pe.matmul(PS[:, 7, 64 * h:64 * h + 64], vb[0:NS, 4, 128 * p:128 * p + 128], p_new[0:NS, h, :],
                                start=True, stop=True)
            ins.then_inc(sem("o_new_done"), tick("o_new_done"))
            pe.wait_ge(sem("o_new_out"), upto("o_new_out"))
            pe.wait_ge(sem("h_back"), upto("h_back", 0))
            done = 0

            def turn_v(g):
                if g:
                    pe.wait_ge(sem("o_b_out"), upto("o_b_out", g - 1))
                for p in range(4):
                    ins = pe.transpose(PS[:, 6, 128 * p:128 * p + 128], v_sums[:, 128 * p:128 * p + 128], ident)
                ins.then_inc(sem("v_turned"), tick("v_turned", g))

            for q in range(NS):
                g, i = q // 4, q % 4
                if i == 0 and g:
                    pe.wait_ge(sem("v_sums_out"), upto("v_sums_out", g - 1))
                pe.wait_ge(sem(f"rows_in{q % 5}"), upto(f"rows_in{q % 5}", "v", q))
                v = rows[:, q % 5, :].rearrange("p (f n) -> p f n", f=2)
                for f in range(2):
                    ins = pe.matmul(PS[32 * i:32 * i + 32, 7, :], flat(p_sel[:, f, 4 * g:4 * g + 4, :]), v[:, f, :],
                                    start=f == 0, stop=f == 1)
                ins.then_inc(sem("v_used"), tick("v_used", q))
                if i == 0 and g:
                    turn_v(g - 1)
                while done < len(mix_steps) * (q + 1) // NS:
                    mix_product(pe, *mix_steps[done])
                    done += 1
            pe.wait_ge(sem("v_sums_out"), upto("v_sums_out", NS // 4 - 1))
            turn_v(NS // 4 - 1)

        def act_sparse(act):
            act.wait_ge(sem("sel_shifted"), upto("sel_shifted"))
            act.activation(s_sel[0:NS], s_sel[0:NS], ACT.Exp).then_inc(sem("sel_exped"), tick("sel_exped"))
            for f in range(2):
                act.wait_ge(sem("sel_turned"), upto("sel_turned", f))
                act.copy(p_sel[:, f].rearrange("p q h -> p h q"),
                                PS[:, f, :].rearrange("p (h q) -> p h q", h=H)).then_inc(
                    sem("sel_out"), tick("sel_out", f))
            act.wait_ge(sem("sel_turned"), upto("sel_turned", 2))
            act.copy(p_new[0:NS], PS[0:NS, 2, :].rearrange("p (h q) -> p h q", h=H)).then_inc(
                sem("sel_out"), tick("sel_out", 2))
            act.wait_ge(sem("o_new_done"), upto("o_new_done"))
            act.wait_ge(sem("k_scored"), upto("k_scored", NS - 1))
            act.copy(prod[:, 0:512], PS[:, 7, :]).then_inc(sem("o_new_out"), tick("o_new_out"))
            gate_parts = [x for x in mix_parts if x[0] == "g"]
            done = 0
            for g in range(NS // 4):
                while done < len(gate_parts) and mix_end[gate_parts[done]] <= 4 * g + 2:
                    gate(act, *gate_parts[done][1:])
                    done += 1
                act.wait_ge(sem("v_used"), upto("v_used", 4 * g + 3))
                if g:
                    act.wait_ge(sem("v_turned"), upto("v_turned", g - 1))
                act.copy(v_sums, PS[:, 7, :]).then_inc(sem("v_sums_out"), tick("v_sums_out", g))
            for x in gate_parts[done:]:
                gate(act, *x[1:])

        def gate(act, n, j, m):
            act.wait_ge(sem("gate_dots"), upto("gate_dots", n, j, m))
            u = mix_units.index((n, j, m)) if m < 4 else 0
            if u >= 4:
                act.wait_ge(sem("mixed"), upto("mixed", *mix_units[u - 4]))
            act.activation(gates_of(n, j, m)[0:TW[m]], PS[0:TW[m], mix_bank(("g", n, j, m)), :], ACT.Sigmoid).then_inc(
                sem("gates_ready"), tick("gates_ready", n, j, m))

        def dve_sparse(dve, link):
            q = slice(0, NS)
            dve.wait_ge(sem("new_dots"), upto("new_dots"))
            bias = new_bias[q].rearrange("p a b -> p (a b)").unsqueeze(1).to_broadcast([NS, 4, NS])
            for par in range(2):
                dve.scalar_tensor_tensor(out=s_sel[q, par:H:2, TOPK_S:TOPK_S + NS],
                                         in0=PS[q, 4 + par, 0:256].rearrange("p (h k) -> p h k", h=4),
                                         scalar=DSA_SCALE, in1=bias, op0=ALU.mult, op1=ALU.add)
            for i in range(4):
                f, h0 = i // 2, 4 * (i % 2)
                dve.wait_ge(sem("dots_turned"), upto("dots_turned", i))
                link(dve.scalar_tensor_tensor(out=s_sel[q, h0:h0 + 4, 128 * f:128 * f + 128],
                                              in0=PS[q, i, :].rearrange("p (h k) -> p h k", h=4), scalar=DSA_SCALE,
                                              in1=slot_bias[q, 128 * f:128 * f + 128].unsqueeze(1)
                                              .to_broadcast([NS, 4, 128]), op0=ALU.mult, op1=ALU.add))
            wide = lambda v: v[q].unsqueeze(2).to_broadcast([NS, H, TOPK_S + NS])
            link(dve.tensor_reduce(head_max[q], s_sel[q], AX.X, ALU.max))
            dve.tensor_tensor(s_sel[q], s_sel[q], wide(head_max), ALU.subtract).then_inc(
                sem("sel_shifted"), tick("sel_shifted"))
            dve.wait_ge(sem("sel_exped"), upto("sel_exped"))
            link(dve.tensor_reduce(head_sum[q], s_sel[q], AX.X, ALU.add))
            link(dve.reciprocal(head_sum[q], head_sum[q]))
            dve.tensor_tensor(s_sel[q], s_sel[q], wide(head_sum), ALU.mult).then_inc(
                sem("sel_probs"), tick("sel_probs"))
            done = 0
            for g in range(NS // 4):
                while done < len(mix_units) and mix_end[("b", *mix_units[done])] <= 4 * g + 3:
                    mix(dve, link, *mix_units[done])
                    done += 1
                dve.wait_ge(sem("v_turned"), upto("v_turned", g))
                dve.wait_ge(sem("o_new_out"), upto("o_new_out"))
                c = slice(4 * g, 4 * g + 4)
                for par in range(2):
                    r = slice(64 * par, 64 * par + 64)
                    ins = dve.tensor_tensor(oT_b[r, :, 512 + 4 * g:516 + 4 * g],
                                            flat(PS[r, 6:8, :])[:, 0:520].rearrange("p (a n) -> p a n", a=4)
                                            [:, :, par:par + 121:40],
                                            prod[r, 0:512].rearrange("p (a b q) -> p b a q", a=4, b=2)[:, par, :, c],
                                            ALU.add)
                ins.then_inc(sem("o_b_out"), tick("o_b_out", g))
            same(("o_b_ready",), ("o_b_out", NS // 4 - 1))
            for u in mix_units[done:]:
                mix(dve, link, *u)

        mix_parts = []
        for n in range(2):
            for j in range(2):
                for m in range(4):
                    mix_parts += [("g", n, j, m), ("b", n, j, m)]
                mix_parts.append(("g", n, j, 4))
        mix_part_no = {x: i for i, x in enumerate(mix_parts)}
        mix_steps = [(x, k) for x in mix_parts for k in range(KD if x[0] == "g" else 4)]
        mix_units = [(n, j, m) for n in range(2) for j in range(2) for m in range(4)]
        gate_w = [flat(w_slots)[:, 4096 * i:4096 * i + 4096].rearrange("p (k n) -> p k n", k=KD) for i in range(2)]
        branch_w = [[b.rearrange("p (k n) -> p k n", k=4) for b in half] for half in branch_w]

        mix_end = {}
        for i, (x, k) in enumerate(mix_steps):
            mix_end[x] = next(q for q in range(NS) if len(mix_steps) * (q + 1) // NS > i)

        def mix_bank(x):
            if x[0] == "b" and x[3] == 4:
                return 4 + 2 * x[1] + x[2]
            return mix_part_no[x] % 6

        def gates_of(n, j, m):
            return gates_last[n][:, j] if m == 4 else gates[:, mix_units.index((n, j, m)) % 4]

        w_out = flat(w_slots)[:, 0:8192].rearrange("p (n k c) -> p n k c", n=2, k=KD)
        up_pieces = [(kind, p) for p in range(NF // 2) for kind in ("g", "u")]
        down_pieces = [(n, p) for n in range(2) for p in range(6)]
        pieces = [("up", x) for x in up_pieces] + [("down", x) for x in down_pieces]
        piece_no = {x: i for i, x in enumerate(pieces)}

        def piece_slot(x):
            return w_slots[:, piece_no[x] % 6, :]

        def x_rows(m):
            if m == 0:
                return [(slice(0, NM), None), (slice(NM, 128), slice(0, 128 - NM))]
            if m < 4:
                return [(slice(0, 128), slice(128 * m - NM, 128 * m + 128 - NM))]
            return [(slice(NS, NS + 16), slice(512 - NM, 512))]

        def sp_merge(sp):
            w_in = I["w_in"][0].rearrange("(k p) n -> p k n", p=128)
            br = [I[x][0].rearrange("(k p) n -> p k n", p=128) for x in ("w_br_a", "w_br_b")]
            sp.wait_ge(sem("o_done"), upto("o_done", ("a", 4, H - 1)))
            for j, at in enumerate((C_GA, C_GB)):
                sp.dma_start(gate_w[j], w_in[:, :, at:at + 512]).then_inc(sem(f"gate_w_in{j}"), tick(f"gate_w_in{j}", 0, by=16))
            sp.dma_start(flat(hT_f), scratch["hT"]).then_inc(sem("h_back"), tick("h_back", 0, by=16))
            for t in pturns[-2:]:
                sp.wait_ge(sem("pturn_out"), upto("pturn_out", t))
            sp.wait_ge(sem("o_out"), upto("o_out", steps_p[-1]))
            for n in range(2):
                for i in range(2):
                    sp.dma_start(branch_w[n][i], br[i][:, :, 512 * n:512 * n + 512]).then_inc(
                        sem("branch_w_in"), tick("branch_w_in", by=16))
            sp.wait_ge(sem("o_new_done"), upto("o_new_done"))
            for m in range(NTILE):
                for part, src in x_rows(m):
                    rows_in = I["meta_tokens"] if src is None else I["x_prompt"][0, src, :]
                    sp.dma_start(x2[part, m, :], rows_in).then_inc(sem("x_back"), tick("x_back", by=16))
            sp.dma_start(x2[0:NS, 4, :], I["x_sample"].rearrange("b t d -> (b t) d")).then_inc(
                sem("x_back"), tick("x_back", by=16))
            for j, at in enumerate((C_GA, C_GB)):
                sp.wait_ge(sem("gate_dots"), upto("gate_dots", 0, j, 4))
                sp.dma_start(gate_w[j], w_in[:, :, at + 512:at + 1024]).then_inc(
                    sem(f"gate_w_in{j}"), tick(f"gate_w_in{j}", 1, by=16))
            for n in range(2):
                sp.wait_ge(sem("gate_dots"), upto("gate_dots", 1, n, 4))
                sp.dma_start(w_out[:, n], I["w_o"][0].rearrange("(k p) n -> p k n", p=128)
                                    [:, :, 512 * n:512 * n + 512]).then_inc(
                    sem("w_out_in"), tick("w_out_in", by=16))
            sp.wait_ge(sem("branch_dots"), upto("branch_dots", 1, 1, 4))
            sp.dma_start(conv_rows[0:66], I["ffn_conv_w"][0].rearrange("j (f p) -> (j f) p", p=128)).then_inc(
                sem("conv_in"), tick("conv_in", by=16))
            sp.dma_start(conv_rows[66:88], I["ffn_conv_b"].rearrange("a (f p) -> (a f) p", p=128)).then_inc(
                sem("conv_in"), tick("conv_in", by=16))
            sp.wait_ge(sem("mixed"), upto("mixed", 1, 1, 4))
            sp.dma_start(conv_state[0:16], I["state_ffn_conv"][0].rearrange("b j f -> (b j) f")).then_inc(
                sem("conv_in"), tick("conv_in", by=16))
            for i, x in enumerate(pieces):
                if i < 4:
                    sp.wait_ge(sem("out_dots"), upto("out_dots", (1, 4)))
                elif i >= 6:
                    sp.wait_ge(sem("piece_used"), upto("piece_used", pieces[i - 6]))
                if x[0] == "up":
                    kind, p = x[1]
                    src = I["w_ffn_" + kind][0].rearrange("(k p) n -> p k n", p=128)[:, :, 256 * p:256 * p + 256]
                    dst = piece_slot(x).rearrange("p (k n) -> p k n", k=KD)
                else:
                    n, p = x[1]
                    k = min(4, NF - 4 * p)
                    src = I["w_ffn_d"][0].rearrange("(f p) n -> p f n", p=128)[:, 4 * p:4 * p + k,
                                                                                 512 * n:512 * n + 512]
                    dst = piece_slot(x)[:, 0:512 * k].rearrange("p (k n) -> p k n", k=k)
                sp.dma_start(dst, src).then_inc(sem(f"piece_in{i % 6}"), tick(f"piece_in{i % 6}", x, by=16))
                if i == 6:
                    sp.wait_ge(sem("h2_ready"), upto("h2_ready", ("h2", 4, 1)))
                    sp.dma_start(g_row, I["final_g"].partition_broadcast(128)).then_inc(
                        sem("g_row_in"), tick("g_row_in", by=16))
            sp.wait_ge(sem("conv_turned_out"), upto("conv_turned_out", NF - 1))
            sp.dma_start(O["new_conv_s"][0].rearrange("b j f -> (b j) f"), conv_out[0:16]).then_inc(
                sem("final_store"), tick("final_store", by=16))
            sp.dma_start(O["new_conv_p"][0, 0], conv_out[16:18]).then_inc(
                sem("final_store"), tick("final_store", by=16))
            for m in range(NTILE):
                sp.wait_ge(sem("y_ready"), upto("y_ready", m))
                for part, dst in x_rows(m):
                    if dst is not None:
                        sp.dma_start(O["y_prompt"][0, dst, :], x2[part, m, :]).then_inc(
                            sem("final_store"), tick("final_store", by=16))
                if m == 4:
                    sp.dma_start(O["y_sample"].rearrange("b t d -> (b t) d"), x2[0:NS, m, :]).then_inc(
                        sem("final_store"), tick("final_store", by=16))
            sp.wait_ge(sem("final_store"), upto("final_store"))

        def mix_product(pe, x, k):
            kind, n, j, m = x
            if k == 0:
                if kind == "g":
                    pe.wait_ge(sem(f"gate_w_in{j}"), upto(f"gate_w_in{j}", n))
                elif m == 0:
                    pe.wait_ge(sem("branch_w_in"), upto("branch_w_in"))
                if (kind == "g" or m < 4) and mix_part_no[x] >= 6:
                    before = mix_parts[mix_part_no[x] - 6]
                    pe.wait_ge(sem("gates_ready" if before[0] == "g" else "mixed"), upto("gates_ready" if before[0] == "g" else "mixed", *before[1:]))
            src, w = (hT_f, gate_w[j]) if kind == "g" else ((oT_a, oT_b)[j], branch_w[n][j])
            last_k = (KD if kind == "g" else 4) - 1
            ins = pe.matmul(PS[0:TW[m], mix_bank(x), :], src[:, k, token_cols(m)], w[:, k, :], start=k == 0,
                            stop=k == last_k)
            if k == last_k:
                ins.then_inc(
                    sem("gate_dots" if kind == "g" else "branch_dots"),
                    tick("gate_dots" if kind == "g" else "branch_dots", n, j, m))

        def turn_mix(pe, tiles):
            for m in tiles:
                for j in range(2):
                    i = 2 * m + j
                    if i >= 4:
                        pe.wait_ge(sem("mix_turn_out"), upto("mix_turn_out", (i - 4) // 2, i % 2))
                    for k in range(4):
                        ins = pe.transpose(PS[:, i % 4, 128 * k:128 * k + TW[m]],
                                           o_mix[0:TW[m], m, 512 * j + 128 * k:512 * j + 128 * k + 128],
                                           ident[0:TW[m], 0:TW[m]])
                    ins.then_inc(sem("mix_turned"), tick("mix_turned", m, j))

        def pe_merge(pe):
            pe.wait_ge(sem("mixed"), upto("mixed", 1, 1, 3))
            pe.wait_ge(sem("gates_ready"), upto("gates_ready", 1, 1, 4))
            turn_mix(pe, range(4))
            pe.wait_ge(sem("o_b_ready"), upto("o_b_ready"))
            for n in range(2):
                for j in range(2):
                    for k in range(4):
                        mix_product(pe, ("b", n, j, 4), k)
            pe.wait_ge(sem("mixed"), upto("mixed", 1, 1, 4))
            turn_mix(pe, [4])
            pe.wait_ge(sem("w_out_in"), upto("w_out_in"))

            def h2_turn(m):
                pe.wait_ge(sem("x_normed"), upto("x_normed", m))
                for j in range(2):
                    if m >= 2:
                        pe.wait_ge(sem("h2_ready"), upto("h2_ready", ("h2", m - 2, j)))
                    else:
                        pe.wait_ge(sem("mix_turn_out"), upto("mix_turn_out", 4 - m, j))
                    for k in range(4):
                        ins = pe.transpose(PS[:, 2 * (m % 2) + j, 128 * k:128 * k + TW[m]],
                                           x_norm[0:TW[m], m % 2, 512 * j + 128 * k:512 * j + 128 * k + 128],
                                           ident[0:TW[m], 0:TW[m]])
                    ins.then_inc(sem("h2_turned"), tick("h2_turned", m, j))

            for m in range(NTILE):
                pe.wait_ge(sem("mix_turn_out"), upto("mix_turn_out", m, 1))
                for n in range(2):
                    if m >= 2:
                        pe.wait_ge(sem("x2_ready"), upto("x2_ready", m - 2, n))
                    for k in range(KD):
                        ins = pe.matmul(PS[0:TW[m], 4 + 2 * (m % 2) + n, :], o_mixT[:, k, token_cols(m)],
                                        w_out[:, n, k, :], start=k == 0, stop=k == KD - 1)
                    ins.then_inc(sem("out_dots"), tick("out_dots", (n, m)))
                if m:
                    h2_turn(m - 1)
            h2_turn(4)
            pe.wait_ge(sem("conv_in"), upto("conv_in"))
            pe.wait_ge(sem("x2_ready"), upto("x2_ready", 3, 1))
            pe.wait_ge(sem("x2_ready"), upto("x2_ready", 4, 1))
            pe_ffn(pe)

        def pe_ffn(pe):
            pe.transpose(PS[:, 6, 0:88], conv_rows[0:88], ident[0:88, 0:88]).then_inc(
                sem("conv_w_turned"), tick("conv_w_turned"))
            pe.wait_ge(sem("h2_ready"), upto("h2_ready", ("h2", 4, 1)))
            pe.wait_ge(sem("conv_w_out"), upto("conv_w_out"))

            def last_rows(f):
                pe.wait_ge(sem("last_two_ready"), upto("last_two_ready", f))
                if f:
                    pe.wait_ge(sem("conv_turned_out"), upto("conv_turned_out", f - 1))
                pe.transpose(PS[0:18, 7, 0:128], last_two[:, f % 2, :], ident).then_inc(
                    sem("conv_turned"), tick("conv_turned", f))

            for f in range(NF):
                b = 3 * (f % 2)
                if f >= 2:
                    pe.wait_ge(sem("gated"), upto("gated", f - 2))
                if f:
                    pe.wait_ge(sem("state_out"), upto("state_out", f - 1))
                pe.transpose(PS[:, 6, 0:16], conv_state[0:16, 128 * f:128 * f + 128], ident[0:16, 0:16]).then_inc(
                    sem("state_turned"), tick("state_turned", f))
                for j, kind in enumerate("gu"):
                    x = ("up", (kind, f // 2))
                    pe.wait_ge(sem(f"piece_in{piece_no[x] % 6}"), upto(f"piece_in{piece_no[x] % 6}", x))
                    w = piece_slot(x).rearrange("p (k n) -> p k n", k=KD)[:, :, 128 * (f % 2):128 * (f % 2) + 128]
                    for k in range(KD):
                        pe.matmul(PS[:, b + j, :], w[:, k, :], h2T[:, k, 0:512], start=k == 0, stop=k == KD - 1)
                    for k in range(KD):
                        ins = pe.matmul(PS[:, b + 2, 128 * j:128 * j + 80], w[:, k, :], h2T[:, k, 512:NCOL],
                                        start=k == 0, stop=k == KD - 1)
                    if f % 2:
                        ins.then_inc(sem("piece_used"), tick("piece_used", x))
                        same(("up_done", f, j), ("piece_used", x))
                    else:
                        ins.then_inc(sem("up_done"), tick("up_done", f, j))
                if f:
                    last_rows(f - 1)
            last_rows(NF - 1)
            for g in (NF - 2, NF - 1):
                pe.wait_ge(sem("gated"), upto("gated", g))
            pe.wait_ge(sem("state_out"), upto("state_out", NF - 1))
            for n in range(2):
                for p in range(6):
                    x = ("down", (n, p))
                    pe.wait_ge(sem(f"piece_in{piece_no[x] % 6}"), upto(f"piece_in{piece_no[x] % 6}", x))
                    k = min(4, NF - 4 * p)
                    w = piece_slot(x)[:, 0:512 * k].rearrange("p (k n) -> p k n", k=k)
                    for i in range(k):
                        f = 4 * p + i
                        for m in range(NTILE):
                            if f == 0 and n == 0 and m == 0:
                                pe.wait_ge(sem("conv_turned_out"), upto("conv_turned_out", NF - 1))
                            if f == 0 and n == 1 and m >= 3:
                                pe.wait_ge(sem("y_summed"), upto("y_summed", 0, m - 3))
                            ins = pe.matmul(PS[0:TW[m], (5 * n + m) % 8, :], upT[:, f, token_cols(m)], w[:, i, :],
                                            start=f == 0, stop=f == NF - 1)
                            if f == NF - 1:
                                ins.then_inc(sem("y_dots"), tick("y_dots", n, m))
                    if p < 5:
                        ins.then_inc(sem("piece_used"), tick("piece_used", x))
                    else:
                        same(("piece_used", x), ("y_dots", n, 4))

        def root(act, m, name):
            act.wait_ge(sem(name + "_mean"), upto(name + "_mean", m))
            act.activation(small[0:TW[m], 8 + m:9 + m], small[0:TW[m], m:m + 1], ACT.Sqrt).then_inc(
                sem(name + "_root"), tick(name + "_root", m))

        def act_merge(act):
            for m in range(NTILE):
                for j in range(2):
                    act.wait_ge(sem("mix_turned"), upto("mix_turned", m, j))
                    act.copy(o_mixT[:, 4 * j:4 * j + 4, token_cols(m)], PS[:, (2 * m + j) % 4, :]
                                    .rearrange("p (a n) -> p a n", a=4)[:, :, 0:TW[m]]).then_inc(
                        sem("mix_turn_out"), tick("mix_turn_out", m, j))
            for m in range(NTILE):
                act.wait_ge(sem("x2_ready"), upto("x2_ready", m, 1))
                if m >= 2:
                    act.wait_ge(sem("h2_turned"), upto("h2_turned", m - 2, 1))
                act.activation(x_norm[0:TW[m], m % 2, :], x2[0:TW[m], m, :], ACT.Square,
                                      accum_out=small[0:TW[m], m:m + 1]).then_inc(
                    sem("x2_squared"), tick("x2_squared", m))
                root(act, m, "x2")
            act.wait_ge(sem("conv_w_turned"), upto("conv_w_turned"))
            act.copy(conv_w, PS[:, 6, 0:88]).then_inc(sem("conv_w_out"), tick("conv_w_out"))
            for f in range(NF + 1):
                if f < NF:
                    b, s2 = 3 * (f % 2), f % 2
                    cp, cs = conv_prompt(s2), conv_sample(s2)
                    if f >= 2:
                        act.wait_ge(sem("conv_summed"), upto("conv_summed", f - 2))
                        act.wait_ge(sem("last_two_ready"), upto("last_two_ready", f - 2))
                    else:
                        act.wait_ge(sem("h2_turned"), upto("h2_turned", 4, 1))
                        act.wait_ge(sem("h2_ready"), upto("h2_ready", ("h2", 4, 1)))
                        act.wait_ge(sem("pads_zeroed"), upto("pads_zeroed"))
                    act.wait_ge(sem("state_turned"), upto("state_turned", f))
                    act.copy(cs[:, :, 0:2], PS[:, 6, 0:16].rearrange("p (b j) -> p b j", b=NB)).then_inc(
                        sem("state_out"), tick("state_out", f))
                    act.wait_ge(sem("up_done"), upto("up_done", f, 0))
                    act.copy(cp[:, 2:514], PS[:, b, :])
                    act.wait_ge(sem("up_done"), upto("up_done", f, 1))
                    act.copy(cs[:, :, 2:10], PS[:, b + 2, 0:NS].rearrange("p (b t) -> p b t", b=NB))
                    act.copy(cp[:, 514:530], PS[:, b + 2, NS:NS + 16]).then_inc(
                        sem("conv_in_ready"), tick("conv_in_ready", f))
                    act.wait_ge(last.sem, last.value)
                    if f >= 2:
                        act.wait_ge(sem("conv_turned"), upto("conv_turned", f - 2))
                    act.copy(last_two[:, s2, 0:16].rearrange("p (b j) -> p b j", b=NB), cs[:, :, 8:10])
                    act.copy(last_two[:, s2, 16:18], cp[:, 528:530]).then_inc(sem("last_two_ready"), tick("last_two_ready", f))
                    act.wait_ge(sem("conv_summed"), upto("conv_summed", f))
                    if f >= 2:
                        act.wait_ge(sem("gated"), upto("gated", f - 2))
                    act.activation(conv_sig[:, s2, :], conv_sum[:, s2, :], ACT.Sigmoid).then_inc(
                        sem("sig_ready"), tick("sig_ready", f))
                if f:
                    act.wait_ge(sem("conv_turned"), upto("conv_turned", f - 1))
                    act.copy(conv_out[0:18, 128 * (f - 1):128 * f], PS[0:18, 7, 0:128]).then_inc(
                        sem("conv_turned_out"), tick("conv_turned_out", f - 1))
            for m in range(NTILE):
                act.wait_ge(sem("y_summed"), upto("y_summed", 1, m))
                act.activation(flat(conv_sig)[0:TW[m], 0:D], x2[0:TW[m], m, :], ACT.Square,
                                      accum_out=small[0:TW[m], m:m + 1]).then_inc(
                    sem("y_squared"), tick("y_squared", m))
                root(act, m, "y")

        def conv_prompt(s2):
            return conv_in[:, s2, 0:530]

        def conv_sample(s2):
            return conv_in[:, s2, 530:610].rearrange("p (b t) -> p b t", b=NB)

        def mean(dve, m, name):
            dve.wait_ge(sem(name + "_squared"), upto(name + "_squared", m))
            dve.tensor_scalar(small[0:TW[m], m:m + 1], small[0:TW[m], m:m + 1], 1.0 / D, EPS, ALU.mult,
                                     ALU.add).then_inc(
                sem(name + "_mean"), tick(name + "_mean", m))

        def mix(dve, link, n, j, m):
            w, b = TW[m], mix_bank(("b", n, j, m))
            dve.wait_ge(sem("gates_ready"), upto("gates_ready", n, j, m))
            dve.wait_ge(sem("branch_dots"), upto("branch_dots", n, j, m))
            g, o = gates_of(n, j, m)[0:w], o_mix[0:w, m, 512 * n:512 * n + 512]
            if j == 0:
                dve.tensor_tensor(o, g, PS[0:w, b, :], ALU.mult).then_inc(sem("mixed"), tick("mixed", n, j, m))
                return
            link(dve.tensor_tensor(g, g, PS[0:w, b, :], ALU.mult))
            dve.wait_ge(sem("mixed"), upto("mixed", n, 0, m))
            dve.tensor_tensor(o, o, g, ALU.add).then_inc(sem("mixed"), tick("mixed", n, j, m))

        def dve_merge(dve, link):
            for n in range(2):
                for j in range(2):
                    mix(dve, link, n, j, 4)

            def add_x(m):
                for n in range(2):
                    dve.wait_ge(sem("out_dots"), upto("out_dots", (n, m)))
                    x = x2[0:TW[m], m, 512 * n:512 * n + 512]
                    dve.tensor_tensor(x, x, PS[0:TW[m], 4 + 2 * (m % 2) + n, :], ALU.add).then_inc(
                        sem("x2_ready"), tick("x2_ready", m, n))

            def h2_out(m):
                for j in range(2):
                    dve.wait_ge(sem("h2_turned"), upto("h2_turned", m, j))
                    src = PS[:, 2 * (m % 2) + j, :].rearrange("p (a n) -> p a n", a=4)[:, :, 0:TW[m]]
                    g = g2c[:, 4 * j:4 * j + 4].unsqueeze(2).to_broadcast([128, 4, TW[m]])
                    dve.wait_ge(sem("mix_turned"), upto("mix_turned", 4, 1))
                    dve.tensor_tensor(h2T[:, 4 * j:4 * j + 4, token_cols(m)], src, g, ALU.mult).then_inc(
                        sem("h2_ready"), tick("h2_ready", ("h2", m, j)))

            dve.wait_ge(sem("x_back"), upto("x_back"))
            add_x(0)
            for m in range(NTILE):
                mean(dve, m, "x2")
                if m < 4:
                    add_x(m + 1)
                dve.wait_ge(sem("x2_root"), upto("x2_root", m))
                link(dve.reciprocal(small[0:TW[m], 8 + m:9 + m], small[0:TW[m], 8 + m:9 + m]))
                dve.tensor_scalar(x_norm[0:TW[m], m % 2, :], x2[0:TW[m], m, :], small[0:TW[m], 8 + m:9 + m],
                                         None, ALU.mult).then_inc(
                    sem("x_normed"), tick("x_normed", m))
                h2_out(m)
            for s2 in range(2):
                ins = dve.memset(conv_prompt(s2)[:, 0:2], 0.0)
            ins.then_inc(sem("pads_zeroed"), tick("pads_zeroed"))
            dve.wait_ge(sem("conv_w_out"), upto("conv_w_out"))
            for f in range(NF):
                s2, b = f % 2, 3 * (f % 2)
                dve.wait_ge(sem("conv_in_ready"), upto("conv_in_ready", f))
                if f >= 2:
                    dve.wait_ge(sem("sig_ready"), upto("sig_ready", f - 2))
                    dve.wait_ge(last.sem, last.value)
                cp, cs = conv_prompt(s2), conv_sample(s2)
                out_p = conv_sum[:, s2, 0:NP]
                out_s = conv_sum[:, s2, NP:NCOL].rearrange("p (b t) -> p b t", b=NB)
                w = lambda j: conv_w[:, 22 * j + f:22 * j + f + 1]
                dve.tensor_scalar(out_p, cp[:, 0:NP], w(0), w(3), ALU.mult, ALU.add)
                link(dve.tensor_scalar(out_s, cs[:, :, 0:8], w(0), w(3), ALU.mult, ALU.add))
                for j in (1, 2):
                    dve.scalar_tensor_tensor(out=out_p, in0=cp[:, j:j + NP], scalar=w(j), in1=out_p, op0=ALU.mult,
                                             op1=ALU.add)
                    ins = dve.scalar_tensor_tensor(out=out_s, in0=cs[:, :, j:j + 8], scalar=w(j), in1=out_s,
                                                   op0=ALU.mult, op1=ALU.add)
                    ins.then_inc(
                        sem("conv_summed" if j == 2 else "conv_step"),
                        tick("conv_summed" if j == 2 else "conv_step", f))
                    dve.wait_ge(last.sem, last.value)
                dve.wait_ge(sem("sig_ready"), upto("sig_ready", f))
                sg = conv_sig[:, s2, :]
                link(dve.tensor_tensor(sg, sg, conv_sum[:, s2, :], ALU.mult))
                dve.wait_ge(sem("up_done"), upto("up_done", f, 1))
                dve.tensor_tensor(upT[:, f, 0:512], sg[:, 0:512], PS[:, b + 1, :], ALU.mult)
                dve.tensor_tensor(upT[:, f, 512:576], sg[:, NP:NCOL], PS[:, b + 2, 128:192], ALU.mult)
                dve.tensor_tensor(upT[:, f, 576:592], sg[:, 512:NP], PS[:, b + 2, 192:208], ALU.mult).then_inc(
                    sem("gated"), tick("gated", f))
            for n in range(2):
                for m in range(NTILE):
                    dve.wait_ge(sem("y_dots"), upto("y_dots", n, m))
                    x = x2[0:TW[m], m, 512 * n:512 * n + 512]
                    dve.tensor_tensor(x, x, PS[0:TW[m], (5 * n + m) % 8, :], ALU.add).then_inc(
                        sem("y_summed"), tick("y_summed", n, m))
            dve.wait_ge(sem("g_row_in"), upto("g_row_in"))
            for m in range(NTILE):
                mean(dve, m, "y")
                dve.wait_ge(sem("y_root"), upto("y_root", m))
                link(dve.reciprocal(small[0:TW[m], 8 + m:9 + m], small[0:TW[m], 8 + m:9 + m]))
                x = x2[0:TW[m], m, :]
                dve.scalar_tensor_tensor(out=x, in0=x, scalar=small[0:TW[m], 8 + m:9 + m], in1=g_row[0:TW[m]],
                                                op0=ALU.mult, op1=ALU.mult).then_inc(
                    sem("y_ready"), tick("y_ready", m))

        block = ctx.enter_context(nc.Block())

        @block.sync
        def _(sp):
            for n, (dst, src) in enumerate([
                    (ident, I["c_ident"]), (cc64, I["c_cos64"]), (ss64, I["c_sin64"]), (cc32, I["c_cos32"]),
                    (ss32, I["c_sin32"]), (same_t[0:64], I["c_same_t"]), (same_t[64:128], I["c_same_t"]), (causal8[0:64], I["c_causal8"]), (quarter, I["c_quarter"]),
                    (g1c, I["norm1_g"].rearrange("a (k p) -> p (a k)", p=128)),
                    (gqc, I["g_q"].rearrange("a (k p) -> p (a k)", p=128)),
                    (g2c, I["norm2_g"].rearrange("a (k p) -> p (a k)", p=128)),
                    (gkv, I["g_kv"][0].partition_broadcast(128))] + [(ptx[:, b:b + 1], bass.AP(I["page_table"].tensor, NPG * b, [[1, NPG], [0, 4]]))
                         for b in range(NB)]):
                sp.dma_start(dst, src, allow_slow_non_contiguous=True).then_inc(
                    sem("consts_in"), tick("consts_in", by=16))
                if n == 0:
                    load_x(sp, 0)
                    load_x(sp, 1)
            sp.dma_start(wuk, I["w_uk"][0].rearrange("(c p) h n -> p c (h n)", p=128)).then_inc(
                sem("wuk_in"), tick("wuk_in", 0, by=16))
            sp.dma_start(wuv, I["w_uv"][0].rearrange("(c p) h n -> p c (h n)", p=128)).then_inc(
                sem("wuv_in"), tick("wuv_in", 0, by=16))
            load_w(sp, "qi")
            load_w(sp, "sm")
            for m in range(2, NTILE):
                sp.wait_ge(sem("h_turned"), upto("h_turned", ("h", m - 2, 1)))
                load_x(sp, m)
            for name, last in (("c0", "qi"), ("c1", "sm"), ("uq", "cq"), ("qb", "cq"), ("kb", "uq"), ("vb", "qb")):
                sp.wait_ge(sem("product"), upto("product", last, 4))
                load_w(sp, name)
            sp_sample(sp)
            sp_prompt(sp)
            sp_merge(sp)

        @block.gpsimd
        def _(gp):
            p, s = slice(0, 128), slice(0, NS)
            for m in range(NTILE):
                gp.wait_ge(sem("ki_roped"), upto("ki_roped", m))
                store_rows(gp, kid[:, m, 0:64], O["new_ik_p"], O["new_ik_s"], m, "ki")
            gp.wait_ge(sem("wi_scaled"), upto("wi_scaled", 4))
            gp.dma_start(scratch["w_i"], w_i[0:NS, 4, :]).then_inc(sem("wi_stored"), tick("wi_stored", 0, by=16))
            gp.wait_ge(sem("wi_stored"), upto("wi_stored", 0))
            for h in range(H):
                gp.dma_start(wcol[8 * h:8 * h + 8, :], bass.AP(scratch["w_i"].tensor, h, [[8, 8], [64, 8]]),
                                    allow_slow_non_contiguous=True).then_inc(
                    sem("wcol_in"), tick("wcol_in", by=16))
                gp.dma_start(wcol[64 + 8 * h:72 + 8 * h, :], bass.AP(scratch["w_i"].tensor, h, [[8, 8], [64, 8]]),
                                    allow_slow_non_contiguous=True).then_inc(
                    sem("wcol_in"), tick("wcol_in", h, by=16))
            gp.wait_ge(sem("h_ready"), upto("h_ready", ("h", NTILE - 1, 1)))
            gp.dma_start(scratch["hT"], flat(hT)).then_inc(sem("h_stored"), tick("h_stored", 0, by=16))
            for m in range(NTILE):
                gp.wait_ge(sem("latent_normed"), upto("latent_normed", m))
                store_rows(gp, lat[:, m, 0:256], O["new_ckv_p"], O["new_ckv_s"], m, "ckv")
                store_rows(gp, lat[:, m, 256:288], O["new_kpe_p"], O["new_kpe_s"], m, "kpe")
            gp.wait_ge(sem("b_roped"), upto("b_roped", "qb", 4))
            gp.dma_start(scratch["q_b"], tok[0:NS, units_tok[("qb", 4)]]).then_inc(
                sem("q_b_stored"), tick("q_b_stored", 0, by=16))
            for kind in ("kb", "vb"):
                for m in range(NTILE):
                    if kind == "kb":
                        gp.wait_ge(sem("b_roped"), upto("b_roped", kind, m))
                        src, names = tok[:, units_tok[(kind, m)]], ("new_k_p", "new_k_s")
                    else:
                        gp.wait_ge(sem("unit_act"), upto("unit_act", kind, m))
                        src, names = vb[:, m, :], ("new_v_p", "new_v_s")
                    store_rows(gp, src, O[names[0]], O[names[1]], m, kind)
            for name in ("ki", "ckv", "kpe", "kb", "vb"):
                wait_stored(gp, name)
                gp.wait_ge(sem(f"stored_{name}_s"), upto(f"stored_{name}_s", 4))
            gp_sample_loads(gp)
            gp_gather(gp)

        @block.scalar
        def _(act):
            for m in range(NTILE):
                r = slice(0, TW[m])
                act.wait_ge(sem(f"x_in{m}"), upto(f"x_in{m}", m))
                act.activation(junk[r, 0:D], x_ring[r, m % 2, :], ACT.Square, accum_out=small[r, m:m + 1]).then_inc(
                    sem("x_squared"), tick("x_squared", m))
                act.wait_ge(sem("x_mean"), upto("x_mean", m))
                act.activation(small[r, 8 + m:9 + m], small[r, m:m + 1], ACT.Sqrt).then_inc(
                    sem("x_root"), tick("x_root", m))
            for i, u in enumerate(units + [None]):
                if u:
                    act_unit(act, u)
                if i:
                    for key, _ in turns_of(units[i - 1]):
                        act_turn(act, key)
            act_index(act)
            act_latent(act)
            act_prompt(act)
            act_sparse(act)
            act_merge(act)

        @block.vector
        def _(dve):
            dve.wait_ge(sem("consts_in"), upto("consts_in"))
            link = linker(S, dve)
            link(dve.tensor_copy(ta[:, 0:NB], ptx))
            link(dve.tensor_scalar(tb[:, 0:NB], ta[:, 0:NB], 4.0, quarter[:, 0:1], ALU.mult, ALU.add))
            dve.tensor_copy(idx_row, tb[:, 0:NB])
            for j in range(4):
                ins = dve.tensor_scalar(idx_ckv[:, :, j], tb[:, 0:NB], 4.0, float(j), ALU.mult, ALU.add)
            ins.then_inc(sem("index_ready"), tick("index_ready"))
            def h_out(m):
                for j in range(2):
                    n = TW[m]
                    dve.wait_ge(sem("h_turned"), upto("h_turned", ("h", m, j)))
                    src = PS[:, turn_bank[("h", m, j)], :].rearrange("p (a n) -> p a n", a=4)[:, :, 0:n]
                    g = g1c[:, 4 * j:4 * j + 4].unsqueeze(2).to_broadcast([128, 4, n])
                    dve.tensor_tensor(hT[:, 4 * j:4 * j + 4, token_cols(m)], src, g, ALU.mult).then_inc(
                        sem("h_ready"), tick("h_ready", ("h", m, j)))
            for m in range(NTILE):
                r = slice(0, TW[m])
                dve.wait_ge(sem("x_squared"), upto("x_squared", m))
                dve.tensor_scalar(small[r, m:m + 1], small[r, m:m + 1], 1.0 / D, EPS, ALU.mult, ALU.add).then_inc(
                    sem("x_mean"), tick("x_mean", m))
                if m:
                    h_out(m - 1)
                dve.wait_ge(sem("x_root"), upto("x_root", m))
                link(dve.reciprocal(small[r, 8 + m:9 + m], small[r, 8 + m:9 + m]))
                dve.tensor_scalar(x_ring[r, m % 2, :], x_ring[r, m % 2, :], small[r, 8 + m:9 + m], None,
                                         ALU.mult).then_inc(
                    sem("x_scaled"), tick("x_scaled", m))
            h_out(NTILE - 1)
            for u in units:
                dve_unit(dve, link, u)
            dve_index(dve, link)
            dve_latent(dve, link)
            dve_prompt(dve, link)
            dve_sparse(dve, link)
            dve_merge(dve, link)

        @block.tensor
        def _(pe):
            pe.wait_ge(sem("consts_in"), upto("consts_in"))

            def turn(key, srcs, name="turned"):
                if turn_before[key]:
                    p = turn_before[key]
                    pe.wait_ge(sem("h_ready"), upto("h_ready", p)) if p[0] == "h" else pe.wait_ge(sem("turned_act"), upto("turned_act", *p))
                bank = PS[:, turn_bank[key], :].rearrange("p (a n) -> p a n", a=4)
                for i, s in enumerate(srcs):
                    n, w = s.shape
                    ins = pe.transpose(bank[0:w, i, 0:n], s, ident[0:n, 0:n])
                ins.then_inc(sem(name), tick(name, *(key if name == "turned" else (key,))))

            for m in range(NTILE):
                pe.wait_ge(sem("x_scaled"), upto("x_scaled", m))
                for j in range(2):
                    x = x_ring[0:TW[m], m % 2, :]
                    turn(("h", m, j), [x[:, 128 * k:128 * k + 128] for k in range(4 * j, 4 * j + 4)], "h_turned")
            for i, u in enumerate(units + [None]):
                if u:
                    pe_unit(pe, u)
                if i:
                    v = units[i - 1]
                    if turns_of(v):
                        if v[0] in ("qi", "qb", "kb"):
                            pe.wait_ge(sem("b_roped"), upto("b_roped", *v))
                        elif v[0] == "cq":
                            pe.wait_ge(sem("latent_normed"), upto("latent_normed", v[1]))
                            pe.wait_ge(sem("unit_dve"), upto("unit_dve", "sm", v[1]))
                        elif v[0] == "uq":
                            pe.wait_ge(sem("q_roped"), upto("q_roped", v[1], 1))
                        else:
                            pe.wait_ge(sem("wuk_in"), upto("wuk_in", 0))
                    for key, srcs in turns_of(v):
                        if key in (("qi", 4, 1), ("uq", 4, 2)):
                            pe.wait_ge(sem("dup_ready"), upto("dup_ready", v[0]))
                        turn(key, srcs)
            pe_index(pe)
            pe_latent(pe)
            pe_prompt(pe)
            pe_sparse(pe)
            pe_merge(pe)

    return S.now


def linker(S, eng):
    def link(ins):
        ins.then_inc(S.sem("chain_dve"), S.tick("chain_dve"))
        eng.wait_ge(S.last.sem, S.last.value)
    return link


def flat3(v):
    return v.rearrange("p a b c -> p (a b c)")


def flat(v):
    return v.rearrange("p a b -> p (a b)")


def rows2(v):
    return v if len(v.shape) == 2 else v.rearrange("l h d -> l (h d)")


def rows3(v):
    return v.rearrange("b t c -> (b t) c") if len(v.shape) == 3 else v.rearrange("b t h d -> (b t) (h d)")


_OUTS = {
    "y_prompt": (1, 512, D), "y_sample": (NB, NT, D),
    "new_ckv_p": (1, 1, NP, KVL), "new_kpe_p": (1, 1, NP, PE_), "new_k_p": (1, 1, NP, H, HD),
    "new_v_p": (1, 1, NP, H, HD), "new_ik_p": (1, 1, NP, HD), "new_conv_p": (1, 1, 2, FF),
    "new_ckv_s": (1, NB, NT, KVL), "new_kpe_s": (1, NB, NT, PE_), "new_k_s": (1, NB, NT, H, HD),
    "new_v_s": (1, NB, NT, H, HD), "new_ik_s": (1, NB, NT, HD), "new_conv_s": (1, NB, 2, FF)}
_SCRATCH = {"w_i": (NS, 8), "q_b": (NS, 512), "hT": (128, KD * NCOL), "qT": (96, H * NCOL), "kT": (96, H * NP),
            "vm": (128, 5 * 512)}


def constants():
    pos = np.zeros((5, 128))
    for m in range(4):
        pos[m] = np.arange(128) + 128 * m
    pos[4, 0:NS] = PAST + np.arange(NS) % NT
    pos[4, NS:NS + 16] = 512 + np.arange(16)
    out = {"c_ident": np.eye(128, dtype=np.float32),
           "c_same_t": np.tile(np.eye(8), (8, 1)).astype(np.float32),
           "c_causal8": np.tile(np.where(np.tri(8) > 0, 0.0, NEG), (8, 1)).astype(np.float32),
           "c_wide_tri": np.concatenate([np.zeros((128, 512)), np.where(np.tri(128) > 0, 0.0, NEG)],
                                        1).astype(np.float32),
           "c_same_b": np.repeat(np.eye(8), 8, 0).astype(np.float32),
           "c_quarter": (np.arange(128) % 4).astype(np.float32)[:, None]}
    for w in (64, 32):
        half = w // 2
        freq = np.float32(1.0) / np.power(10000.0, np.arange(half) / half).astype(np.float32)
        ang = (pos.astype(np.float32)[:, :, None] * freq).astype(np.float32)
        cos, sin = np.cos(ang), np.sin(ang)
        out[f"c_cos{w}"] = np.concatenate([cos, cos], -1).transpose(1, 0, 2).astype(np.float32).copy()
        out[f"c_sin{w}"] = np.concatenate([-sin, sin], -1).transpose(1, 0, 2).astype(np.float32).copy()
    return out


_INS = ["x_prompt", "x_sample", "cache_mla_ckv", "cache_mla_kpe", "cache_dsa_k", "cache_dsa_v", "cache_idx_k",
        "state_ffn_conv", "page_table", "meta_tokens", "norm1_g", "w_in", "g_q", "g_kv", "w_uq", "w_uk", "w_uv",
        "w_br_a", "w_br_b", "w_o", "norm2_g", "w_ffn_g", "w_ffn_u", "ffn_conv_w", "ffn_conv_b", "w_ffn_d", "final_g"]


def build(nc, arrays, events):
    I = {n: nc.dram_tensor("in_" + n, a.shape, mybir.dt.from_np(a.dtype), kind="ExternalInput").ap()
         for n, a in arrays.items()}
    O = {n: nc.dram_tensor("out_" + n, s, F32, kind="ExternalOutput").ap() for n, s in _OUTS.items()}
    scratch = {n: nc.dram_tensor("tmp_" + n, s, F32).ap() for n, s in _SCRATCH.items()}
    return trunk(nc, I, O, scratch, events)


def kernel(**inputs):
    import concourse.bacc as _bacc
    from concourse.bass_utils import run_bass_kernel_spmd as _run

    arrays = {n: np.ascontiguousarray(inputs[n]) for n in _INS}
    arrays.update(constants())
    events = build(_bacc.Bacc("TRN2", target_bir_lowering=False, num_devices=1), arrays, None)
    nc = _bacc.Bacc("TRN2", target_bir_lowering=False, num_devices=1)
    build(nc, arrays, events)
    r = _run(nc, [{"in_" + n: a for n, a in arrays.items()}], core_ids=[0])
    return tuple(r.results[0]["out_" + n] for n in _OUTS)
```
